# Optimizing a Trainium2 kernel written in Bass

```python
import jax, jax.numpy as jnp
from jax import lax
import numpy as np

D_MODEL = 1024
BATCH = 1
SEQ = 256
DEPTH = 1

RWKV_HEADS = 8
RWKV_HEAD_DIM = 64
RWKV_WIDTH = RWKV_HEADS * RWKV_HEAD_DIM
DECAY_LORA = 64
ICLR_LORA = 64
GATE_LORA = 128
ATTN_HEADS = 8
ATTN_HEAD_DIM = 64
ATTN_WIDTH = ATTN_HEADS * ATTN_HEAD_DIM
MOBA_BLOCK = 256
MOBA_TOP_K = 3
Q_CHUNK = 128
POOL_WINDOWS = (2, 4, 8, 16)
POOL_GROUPS = 4
POOL_GROUP_DIM = 128
POOL_WIDTH = POOL_GROUPS * POOL_GROUP_DIM
N_BRANCH = 3
D_FF = 4 * D_MODEL
RMS_EPS = 1e-6
GN_EPS = 64e-5
NEG_INF = -1e30

RWKV_IN = 3 * RWKV_WIDTH + DECAY_LORA + ICLR_LORA + GATE_LORA
ATTN_IN = 3 * ATTN_WIDTH
GATE_IN = N_BRANCH * D_MODEL
N_IN = RWKV_IN + ATTN_IN + POOL_WIDTH + GATE_IN

kernel_name = 'hybrid_rwkv7_moba_pool_gated_block'

def rms_norm(x, g):
    x = x.astype(jnp.float32)
    return x * lax.rsqrt(jnp.mean(x * x, axis=-1, keepdims=True) + RMS_EPS) * g.astype(jnp.float32)

def token_shift(p):
    return jnp.pad(p, ((0, 0), (1, 0), (0, 0)))[:, :-1]

def rwkv7_time_mix(p, mu, w0, w_up, a0, a_up, g_up, k_k, k_a, r_k, lnx_g, lnx_b):
    B, T, _ = p.shape
    H, N, W = RWKV_HEADS, RWKV_HEAD_DIM, RWKV_WIDTH
    p = p + (token_shift(p) - p) * mu
    o3 = 3 * W
    o4 = o3 + DECAY_LORA
    o5 = o4 + ICLR_LORA
    r, k, v = p[..., :W], p[..., W:2 * W], p[..., 2 * W:o3]
    xw, xa, xg = p[..., o3:o4], p[..., o4:o5], p[..., o5:]
    w_log = -jax.nn.softplus(-(w0 + jnp.tanh(xw) @ w_up)) - 0.5
    decay = jnp.exp(-jnp.exp(w_log))
    a = jax.nn.sigmoid(a0 + xa @ a_up)
    g = jax.nn.sigmoid(xg) @ g_up
    heads = lambda t: t.reshape(B, T, H, N)
    kk = heads(k * k_k)
    kk = kk / jnp.maximum(jnp.linalg.norm(kk, axis=-1, keepdims=True), 1e-12)
    k = k * (1.0 + (a - 1.0) * k_a)
    r, decay, k, v, a = heads(r), heads(decay), heads(k), heads(v), heads(a)

    def step(S, inp):
        r_t, w_t, k_t, v_t, a_t, b_t = inp
        sa = jnp.einsum('bhvk,bhk->bhv', S, a_t)
        S = S * w_t[:, :, None, :] + sa[..., None] * b_t[:, :, None, :] + v_t[..., None] * k_t[:, :, None, :]
        return S, jnp.einsum('bhvk,bhk->bhv', S, r_t)

    xs = tuple(jnp.swapaxes(t, 0, 1) for t in (r, decay, k, v, -kk, kk * a))
    S0 = jnp.zeros((B, H, N, N), jnp.float32)
    _, o = lax.scan(step, S0, xs)
    o = jnp.swapaxes(o, 0, 1)
    mean = jnp.mean(o, axis=-1, keepdims=True)
    var = jnp.mean(jnp.square(o - mean), axis=-1, keepdims=True)
    o = ((o - mean) * lax.rsqrt(var + GN_EPS)).reshape(B, T, W) * lnx_g + lnx_b
    bonus = jnp.sum(r * k * r_k, axis=-1, keepdims=True) * v
    return (o + bonus.reshape(B, T, W)) * g

def moba_attention(q, k, v):
    B, T, H, Dh = q.shape
    NB = -(-T // MOBA_BLOCK)
    Tp = NB * MOBA_BLOCK
    NC = Tp // Q_CHUNK
    ks = min(MOBA_TOP_K, NB)
    pad = ((0, 0), (0, Tp - T), (0, 0), (0, 0))
    q, k, v = (jnp.pad(t, pad).transpose(0, 2, 1, 3) for t in (q, k, v))
    kb = k.reshape(B, H, NB, MOBA_BLOCK, Dh)
    vb = v.reshape(B, H, NB, MOBA_BLOCK, Dh)
    k_mean = jnp.mean(kb, axis=3)
    gate = jnp.einsum('bhtd,bhnd->bhtn', q, k_mean)
    q_blk = jnp.arange(Tp) // MOBA_BLOCK
    past = jnp.arange(NB)[None, :] < q_blk[:, None]
    gate = jnp.where(past, gate, NEG_INF)
    _, sel = lax.top_k(gate, ks)
    valid = sel < q_blk[:, None]
    slopes = jnp.asarray(2.0 ** (-8.0 * np.arange(1, H + 1) / H), jnp.float32)
    scale = Dh ** -0.5
    offs = jnp.arange(MOBA_BLOCK)
    head_idx = jnp.arange(H)[:, None, None]

    def per_batch(args):
        qb, kbb, vbb, selb, validb = args

        def to_chunks(t):
            return jnp.swapaxes(t.reshape(H, NC, Q_CHUNK, *t.shape[2:]), 0, 1)

        def chunk(cargs):
            c, qc, sc, vc = cargs
            t_pos = c * Q_CHUNK + jnp.arange(Q_CHUNK)
            own = (c * Q_CHUNK) // MOBA_BLOCK
            k_own = lax.dynamic_index_in_dim(kbb, own, axis=1, keepdims=False)
            v_own = lax.dynamic_index_in_dim(vbb, own, axis=1, keepdims=False)
            k_sel = kbb[head_idx, sc]
            v_sel = vbb[head_idx, sc]
            dist_own = (t_pos[:, None] - (own * MOBA_BLOCK + offs)[None, :]).astype(jnp.float32)
            dist_sel = (t_pos[None, :, None, None] - (sc[..., None] * MOBA_BLOCK + offs)).astype(jnp.float32)
            l_own = jnp.einsum('hcd,hsd->hcs', qc, k_own) * scale - slopes[:, None, None] * dist_own
            l_own = jnp.where(dist_own >= 0, l_own, NEG_INF)
            l_sel = jnp.einsum('hcd,hcjsd->hcjs', qc, k_sel) * scale - slopes[:, None, None, None] * dist_sel
            l_sel = jnp.where(vc[..., None], l_sel, NEG_INF)
            logits = jnp.concatenate([l_sel.reshape(H, Q_CHUNK, ks * MOBA_BLOCK), l_own], axis=-1)
            prob = jax.nn.softmax(logits, axis=-1)
            p_sel = prob[..., :ks * MOBA_BLOCK].reshape(H, Q_CHUNK, ks, MOBA_BLOCK)
            p_own = prob[..., ks * MOBA_BLOCK:]
            return jnp.einsum('hcs,hsd->hcd', p_own, v_own) + jnp.einsum('hcjs,hcjsd->hcd', p_sel, v_sel)

        out = lax.map(chunk, (jnp.arange(NC), to_chunks(qb), to_chunks(selb), to_chunks(validb)))
        return jnp.swapaxes(out, 0, 1).reshape(H, Tp, Dh)

    out = lax.map(per_batch, (q, kb, vb, sel, valid))
    return out.transpose(0, 2, 1, 3)[:, :T].reshape(B, T, H * Dh)

def pool_mix(u, pool_w, pool_scale):
    B, T, _ = u.shape
    ug = u.reshape(B, T, POOL_GROUPS, POOL_GROUP_DIM)
    cs = jnp.cumsum(ug, axis=1)
    outs = []
    for gi, w in enumerate(POOL_WINDOWS):
        c = cs[:, :, gi]
        lo = jnp.pad(c[:, :T - w], ((0, 0), (w, 0), (0, 0)))
        count = jnp.minimum(jnp.arange(T) + 1, w).astype(jnp.float32)[None, :, None]
        outs.append((c - lo) / count - ug[:, :, gi])
    d = jnp.stack(outs, axis=2)
    y = jnp.einsum('btgc,gcd->btgd', d, pool_w).reshape(B, T, POOL_WIDTH)
    return y * pool_scale

def setup_inputs(seed: int = 0) -> dict:
    key = jax.random.key(seed)
    ks = jax.random.split(key, 24)
    L, D, W = DEPTH, D_MODEL, RWKV_WIDTH
    nrm = lambda k, s: jax.random.normal(k, s, jnp.float32)
    return {
        'x': nrm(ks[0], (BATCH, SEQ, D)),
        'norm1_g': 1.0 + 0.05 * nrm(ks[1], (L, D)),
        'w_in': nrm(ks[2], (L, D, N_IN)) * D ** -0.5,
        'shift_mu': jax.random.uniform(ks[3], (L, RWKV_IN), jnp.float32),
        'w0': jax.random.uniform(ks[4], (L, W), jnp.float32, minval=-6.0, maxval=-1.0),
        'w_up': nrm(ks[5], (L, DECAY_LORA, W)) * 0.5 * DECAY_LORA ** -0.5,
        'a0': 0.5 * nrm(ks[6], (L, W)),
        'a_up': nrm(ks[7], (L, ICLR_LORA, W)) * 0.5 * ICLR_LORA ** -0.5,
        'g_up': nrm(ks[8], (L, GATE_LORA, W)) * GATE_LORA ** -0.5,
        'k_k': 0.85 + 0.05 * nrm(ks[9], (L, W)),
        'k_a': 1.0 + 0.05 * nrm(ks[10], (L, W)),
        'r_k': 0.1 * nrm(ks[11], (L, RWKV_HEADS, RWKV_HEAD_DIM)),
        'lnx_g': 1.0 + 0.05 * nrm(ks[12], (L, W)),
        'lnx_b': 0.01 * nrm(ks[13], (L, W)),
        'qn_g': 1.0 + 0.05 * nrm(ks[14], (L, ATTN_HEAD_DIM)),
        'kn_g': 1.0 + 0.05 * nrm(ks[15], (L, ATTN_HEAD_DIM)),
        'pool_w': nrm(ks[16], (L, POOL_GROUPS, POOL_GROUP_DIM, POOL_GROUP_DIM)) * POOL_GROUP_DIM ** -0.5,
        'pool_scale': 1.0 + 0.1 * nrm(ks[17], (L, POOL_WIDTH)),
        'w_branch': nrm(ks[18], (L, N_BRANCH, W, D)) * W ** -0.5,
        'w_out': nrm(ks[19], (L, D, D)) * D ** -0.5,
        'norm2_g': 1.0 + 0.05 * nrm(ks[20], (L, D)),
        'w_ff1': nrm(ks[21], (L, D, D_FF)) * D ** -0.5,
        'w_ff2': nrm(ks[22], (L, D_FF, D)) * D_FF ** -0.5,
    }

def reference(x, norm1_g, w_in, shift_mu, w0, w_up, a0, a_up, g_up, k_k, k_a, r_k, lnx_g, lnx_b,
              qn_g, kn_g, pool_w, pool_scale, w_branch, w_out, norm2_g, w_ff1, w_ff2):
    B, T, _ = x.shape
    out_dtype = x.dtype
    x = x.astype(jnp.float32)
    o1 = RWKV_IN
    o2 = o1 + ATTN_IN
    o3 = o2 + POOL_WIDTH
    for l in range(DEPTH):
        h = rms_norm(x, norm1_g[l])
        proj = h @ w_in[l]
        p_rwkv, p_attn, p_pool, p_gate = proj[..., :o1], proj[..., o1:o2], proj[..., o2:o3], proj[..., o3:]
        y_rwkv = rwkv7_time_mix(p_rwkv, shift_mu[l], w0[l], w_up[l], a0[l], a_up[l], g_up[l],
                                k_k[l], k_a[l], r_k[l], lnx_g[l], lnx_b[l])
        q = p_attn[..., :ATTN_WIDTH].reshape(B, T, ATTN_HEADS, ATTN_HEAD_DIM)
        k = p_attn[..., ATTN_WIDTH:2 * ATTN_WIDTH].reshape(B, T, ATTN_HEADS, ATTN_HEAD_DIM)
        v = p_attn[..., 2 * ATTN_WIDTH:].reshape(B, T, ATTN_HEADS, ATTN_HEAD_DIM)
        y_attn = moba_attention(rms_norm(q, qn_g[l]), rms_norm(k, kn_g[l]), v)
        y_pool = pool_mix(p_pool, pool_w[l], pool_scale[l])
        ys = jnp.stack([y_rwkv, y_attn, y_pool], axis=2)
        branch = jnp.einsum('btnc,ncd->btnd', ys, w_branch[l])
        gates = jax.nn.sigmoid(p_gate.reshape(B, T, N_BRANCH, D_MODEL))
        x = x + jnp.sum(gates * branch, axis=2) @ w_out[l]
        h2 = rms_norm(x, norm2_g[l])
        x = x + jnp.square(jax.nn.relu(h2 @ w_ff1[l])) @ w_ff2[l]
    return x.astype(out_dtype)


_drawn_inputs = setup_inputs


def setup_inputs(seed=0):
    import zlib

    import numpy as np

    out = dict(_drawn_inputs(seed))
    spreads = {}
    factors = {'w_up': 8.0,
     'k_k': 17.884,
     'k_a': 3.54,
     'lnx_g': 4.091,
     'lnx_b': 30.041,
     'qn_g': 8.0,
     'kn_g': 8.0}
    for name, (base, spread) in spreads.items():
        noise = np.random.default_rng([zlib.crc32(name.encode()), seed]).standard_normal(out[name].shape)
        drawn = base * np.exp(spread * noise) if base else spread * noise
        out[name] = __import__('jax').numpy.asarray(drawn.astype(out[name].dtype))
    for name, factor in factors.items():
        out[name] = (out[name] * factor).astype(out[name].dtype)
    return out
```

```python
from contextlib import ExitStack

import numpy as np

import concourse.bass as bass
from concourse import mybir

F32 = mybir.dt.float32
F32R = mybir.dt.float32r
ALU = mybir.AluOpType
ACT = mybir.ActivationFunctionType
AX_X = mybir.AxisListType.X

P = 128
T, D = 256, 1024
TT = T // P
KD = D // P
HEADS, HD = 8, 64
W = HEADS * HD
PAIRS = HEADS // 2
N_RWKV, N_ATTN, N_POOL = 3 * W + 256, 3 * W, W
D_FF = 4 * D
RMS_EPS, GN_EPS = 1e-6, 64e-5
WINDOWS = (2, 4, 8, 16)
PAD = 16
LEVELS = 6
SLOPES = [2.0 ** (-8.0 * (h + 1) / HEADS) for h in range(HEADS)]

C_ID, C_BLK, C_CUM, C_BIAS, C_SI = 0, 128, 256, 386, 770
C_LEV = C_SI + 256
C_M1 = C_LEV + LEVELS * 128
C_M1T = C_M1 + 128
C_INV = C_M1T + 128
C_ALL = C_INV + 4 * 16
V_MU, V_A0, V_KK, V_KA, V_RK, V_LG, V_LB, V_PS, V_G1, V_G2, V_QN, V_KN = 0, 14, 18, 22, 26, 30, 34, 38, 42, 50, 58, 59
V_ALL = 60

UNITS = [("feat", c) for c in (3 * W, W, W + 256, 0, 256, 2 * W, 2 * W + 256)]
UNITS += [("feat", N_RWKV + c) for c in (0, 256, W, W + 256)]
UNITS += [("tok", N_RWKV + 2 * W, kh) for kh in range(2)]
UNITS += [("feat", N_RWKV + N_ATTN + c) for c in (0, 256)]
UNITS += [("tok", N_RWKV + N_ATTN + N_POOL + 512 * p, kh) for p in range(6) for kh in range(2)]
UNITS += [("branch", n, ch) for n in (1, 2, 0) for ch in range(2)]
UNITS += [("out", kh, ch) for kh in range(2) for ch in range(2)]
UNITS += [("ff1", 0)]
for i in range(1, D_FF // 256):
    UNITS += [("ff1", i), ("ff2", i - 1)]
UNITS += [("ff2", D_FF // 256 - 1)]
SLOTS = len(UNITS)
PIECES = 2 * SLOTS
RING = 4
AHEAD = 3
S_QK, S_VA, S_POOL, S_GATE, S_BR, S_OUT = 7, 11, 13, 15, 27, 33
S_FF = 37
S_PROD, S_LEV, S_APPLY, S_GN = (8, 17), (10, 19), (16, 25), (18, 27)
S_HEAD = 13
S_PY = 22


def level_places(t):
    for c in range(TT):
        if S_LEV[c] <= t < S_LEV[c] + LEVELS:
            return c, t - S_LEV[c]
    return None


def product_place(t, p):
    for c in range(TT):
        n = 4 * (t - S_PROD[c]) + p
        if 0 <= n < 6:
            return c, n // 3, n % 3
    return None


def plan_turns():
    turn, count, signalled, ring = {}, [0] * 8, [0] * 8, [0]

    def use(name, bank=None, dense=False):
        if bank is None:
            bank = 4 + ring[0] % 4
            ring[0] += 1
        turn[name] = (bank, count[bank], signalled[bank])
        count[bank] += 1
        signalled[bank] += not dense

    for i in range(4):
        use(("x", i))
    for t, u in enumerate(UNITS):
        for p in range(4):
            if p == 0:
                if u[0] == "feat":
                    use(("unit", t), t % 2, dense=True)
                elif u[0] == "tok" and u[2] == 0:
                    use(("tok", u[1], 0), 0, dense=True)
                    use(("tok", u[1], 1), 1, dense=True)
                elif u[0] == "branch":
                    b = 2 * ((t - S_BR) % 2)
                    use(("unit", t, 0), b, dense=True)
                    use(("unit", t, 1), b + 1, dense=True)
                elif u[0] == "out" and u[1] == 0:
                    for tt in range(TT):
                        use(("out", u[2], tt), 2 * u[2] + tt, dense=True)
                elif u[0] == "ff1":
                    use(("ff", u[1]), dense=True)
                elif u == ("ff2", 0):
                    for b in range(4):
                        use(("mlp", b // 2, b % 2), b)
            for n in pe_uses(t, p):
                use(*n)
    return turn


def pe_uses(t, p):
    if (t, p) == (1, 3):
        return [(("z", 0),), (("z", 1),), (("a", 0),), (("a", 1),)]
    if (t, p) == (2, 3):
        return [(("cum", 0, 0),), (("cum", 0, 1),)]
    if (t, p) == (3, 1):
        return [(("cum", 1, 0),), (("cum", 1, 1),)]
    if (t, p) == (3, 3):
        return [(("kk", 0),), (("kk", 1),)]
    if (t, p) == (4, 3):
        return [(("g", 0),), (("g", 1),)]
    if (t, p) == (7, 1):
        return [(("vt", 0),), (("vt", 1),)]
    if (t, p) == (7, 3):
        return [(("bonus", 0),), (("bonus", 1),)]
    out = []
    if S_QK < t <= S_QK + 4 and p == 3:
        out.append((("ss", t - 1 - S_QK), 2 + (t - 1 - S_QK) % 2))
    if product_place(t, p):
        out += [(("prod", *product_place(t, p), e),) for e in range(2)]
    if (t, p) == (9, 2):
        out += [(("bt",),), (("kt",),)]
    if level_places(t):
        c, l = level_places(t)
        if p == 0:
            out += [(("Y", c, l, g),) for g in range(2)]
        if p == 2:
            for g in range(2):
                if l < LEVELS - 1:
                    out.append((("X", c, l, g),))
                out.append((("XT", c, l, g),))
    if t in S_APPLY:
        c = S_APPLY.index(t)
        if p == 0:
            out += [(("rhs", c, e),) for e in range(2)]
        if p == 1:
            out += [(("sa", c),)]
        if p == 2:
            out += [(("o", c, e),) for e in range(2)]
        if p == 3 and c == 0:
            out += [(("state",),)]
    if (t, p) in ((S_GN[0], 3), (S_GN[1], 0)):
        out += [(("ot", S_GN.index(t)),)]
    if S_HEAD <= t <= S_HEAD + HEADS:
        h = t - S_HEAD
        if p == 0 and h >= 1:
            out += [(("pt", h - 1), 3)]
        if p == 1 and h < HEADS:
            out += [(("score", h), 2)]
        if p == 3 and h >= 1:
            out += [(("pv", h - 1), 3)]
    if t == S_PY and p in (0, 2):
        out += [(("pool", p // 2), 2 + p // 2)]
    if (t, p) == (S_OUT - 1, 3):
        out += [(("m", 0),), (("m", 1),)]
    if (t, p) == (S_OUT, 3):
        out += [(("m", 2),), (("m", 3),)]
    if (t, p) == (S_FF - 1, 3):
        out += [(("h2", i),) for i in range(4)]
    return out


def dense_ends():
    ends = {}
    for t, u in enumerate(UNITS):
        if u[0] == "feat":
            ends[("unit", t)] = 2 * t + 2
        for tt in range(TT):
            if u[0] == "tok" and u[2] == 1:
                ends[("tok", u[1], tt)] = 2 * t + 2
            if u[0] == "branch":
                ends[("unit", t, tt)] = 2 * t + 2
            if u[0] == "out" and u[1] == 1:
                ends[("out", u[2], tt)] = 2 * t + 2
        if u[0] == "ff1":
            ends[("ff", u[1])] = 2 * t + 2
    return ends


DENSE_END = dense_ends()


def build_layer(nc: bass.Bass, x, w_in, w_up, w0, a_up, g_up, pool_w, w_branch, w_out, w_ff1, w_ff2, vecs, consts, out):
    turn = plan_turns()
    ctx = ExitStack()
    with ctx:
        def sb(name, shape, dt=F32):
            return ctx.enter_context(nc.sbuf_tensor(name, shape, dt))

        def sem(name):
            return ctx.enter_context(nc.semaphore(name))

        stage = sb("stage", [P, RING, 1024])
        w_hi = sb("w_hi", [P, RING, 1024], F32R)
        w_lo = sb("w_lo", [P, RING, 1024], F32R)
        h_hi = sb("h_hi", [P, KD, T], F32R)
        h_lo = sb("h_lo", [P, KD, T], F32R)
        y_hi = sb("y_hi", [P, KD, T], F32R)
        y_lo = sb("y_lo", [P, KD, T], F32R)
        r_hi = sb("r_hi", [P, 4, T], F32R)
        r_lo = sb("r_lo", [P, 4, T], F32R)
        xs = sb("xs", [P, TT, D])
        cst = sb("cst", [P, C_ALL])
        vec = sb("vec", [P, V_ALL])
        big = sb("big", [P, 6, 1024])
        mat = sb("mat", [P, 7, HEADS, P])
        lora = sb("lora", [P, 3, 512])
        pool_sb = sb("pool_sb", [P, 4, P])
        vmix = sb("vmix", [P, PAIRS, T])
        lmix = sb("lmix", [P, 2, T])
        th = sb("th", [P, T])
        sgx = sb("sgx", [P, T])
        gg = sb("gg", [P, PAIRS, T])
        bonus = sb("bonus", [P, PAIRS, T])
        ops = sb("ops", [P, 4096])
        vtok = sb("vtok", [P, TT, W])
        s_in = sb("s_in", [P, PAIRS, HD])
        att = sb("att", [P, 1024])
        small = sb("small", [P, 96])

        ident = cst[:, C_ID:C_ID + P]
        blk = cst[:, C_BLK:C_BLK + P]
        gates = [big[:, p].rearrange("p (t n) -> p t n", t=TT) for p in range(6)]
        q4 = lambda v: v.rearrange("p (j t) -> p j t", j=PAIRS)
        rmix, kmix = q4(big[:, 0]), q4(big[:, 1])
        btok, ktok = big[:, 2, 0:512], big[:, 2, 512:1024]
        qraw, kraw = q4(big[:, 3]), q4(big[:, 4])
        vatt = big[:, 5].rearrange("p (t n) -> p t n", t=TT)
        sg = big[:, 2].rearrange("p (t n) -> p t n", t=TT)
        xn = big[:, 4:6]
        flat = mat[:].rearrange("p a h s -> p (a h s)")
        a_s, kkn, k2, ksq = (q4(flat[:, 1024 * i:1024 * i + 1024]) for i in range(4))
        e_up, e_dn = (flat[:, 4096 + 1040 * i:4096 + 1040 * i + 1032].rearrange("p (c j t) -> p c j t", c=TT, j=PAIRS)
                      for i in range(2))
        gm = flat[:, 0:4096].rearrange("p (h a s) -> p h a s", h=HEADS, a=4)
        mx, mxt, my = (mat[:, i] for i in (4, 5, 6))
        opv = ops[:].rearrange("p (c z) -> p c z", c=TT)
        bk = [opv[:, c, 0:1024].rearrange("p (a j t) -> p a j t", a=2, j=PAIRS) for c in range(TT)]
        ar = [opv[:, c, 1024:2048].rearrange("p (j a t) -> p j a t", j=PAIRS, a=2) for c in range(TT)]
        pu = ops[:, 0:4 * (PAD + T)].rearrange("p (g t) -> p g t", g=4)
        pt1, pt2 = (ops[:, 1088 + 272 * i:1088 + 272 * i + 272] for i in range(2))
        pd = ops[:, 1632:1632 + 256]
        rhs_sb, sa_sb = (lora[:, i].rearrange("p (h v) -> p h v", h=HEADS) for i in range(2))
        o_sb = lora[:, 2].rearrange("p (h v) -> p h v", h=HEADS)
        vflat = vmix[:].rearrange("p j t -> p (j t)")
        oc, osq = (vflat[:, 512 * i:512 * i + 512] for i in range(2))
        ytmp = lmix[:].rearrange("p a t -> p (a t)").rearrange("p (j t) -> p j t", j=PAIRS)
        sq_att = [att[:, 512 * i:512 * i + 512] for i in range(2)]
        prob, prob_t = att[:, 0:384], att[:, 512:896]
        ffs, fsq = ([flat[:, 512 * i + o:512 * i + o + 512] for i in range(2)] for o in (0, 1024))
        omu, oka, gq8 = small[:, 0:14], small[:, 14:18], small[:, 18:19]
        ss1, rs1, ss2, r2, nmax, psm = (small[:, 20 + 2 * i:22 + 2 * i] for i in range(6))
        gsum, gvar = small[:, 32:40], small[:, 40:48]
        e_end, e_mid = small[:, 48:52], small[:, 52:56]

        def col(i):
            return vec[:, i:i + 1]

        def wide(ap, n):
            return ap.unsqueeze(1).to_broadcast([P, n, ap.shape[1]])

        banks = [ctx.enter_context(nc.psum_tensor(f"bank{i}", [P, 512], F32)) for i in range(8)]
        full = [sem(f"full{i}") for i in range(8)]
        drained = [sem(f"drained{i}") for i in range(8)]

        def ps(name):
            return banks[turn[name][0]]

        def full_of(name):
            return full[turn[name][0]]

        def drained_of(name):
            return drained[turn[name][0]]

        def room(eng, name):
            b, before, _ = turn[name]
            if before:
                eng.wait_ge(drained[b], before)
            return banks[b]

        def take(eng, name):
            b, _, before = turn[name]
            if name in DENSE_END:
                eng.wait_ge(used, DENSE_END[name])
            else:
                eng.wait_ge(full[b], before + 1)
            return banks[b]

        def copied(eng, name):
            b, before, _ = turn[name]
            eng.wait_ge(drained[b], before + 1)

        x_in, cst_in, small_in = sem("x_in"), sem("cst_in"), sem("small_in")
        loaded = [sem(f"loaded{i}") for i in range(RING)]
        hi_done, lo_done = sem("hi_done"), sem("lo_done")
        used = sem("used")
        consts_ready = sem("consts_ready")
        ones_ready = sem("ones_ready")
        ss_ready, ms_ready, root_ready, rs_ready, xn_ready = (
            sem(n) for n in ("ss_ready", "ms_ready", "root_ready", "rs_ready", "xn_ready"))
        h_hi_done = sem("h_hi_done")
        keep_part = sem("keep_part")
        lora_ready = sem("lora_ready")
        kkraw_ready, ksq_ready, kkroot_ready = sem("kkraw_ready"), sem("ksq_ready"), sem("kkroot_ready")
        own = sem("own")
        rk_ready, ops_ready = sem("rk_ready"), sem("ops_ready")
        nt_ready, x1_ready, xt1_ready = sem("nt_ready"), sem("x1_ready"), sem("xt1_ready")
        oc_ready, osq_ready, gvar_ready, groot_ready, on_ready, yr_pre, yr_hi_done, yr_ready = (
            sem(n) for n in ("oc_ready", "osq_ready", "gvar_ready", "groot_ready", "on_ready", "yr_pre", "yr_hi_done",
                             "yr_ready"))
        qroot_ready, qk_ready = sem("qroot_ready"), sem("qk_ready")
        neg_ready, exps_ready, p_ready = sem("neg_ready"), sem("exps_ready"), sem("p_ready")
        ya_hi = sem("ya_hi")
        pad_ready, pool_step, pd_ready, yp_hi = (sem(n) for n in ("pad_ready", "pool_step", "pd_ready", "yp_hi"))
        sum_ready, m_pre, m_hi = sem("sum_ready"), sem("m_pre"), sem("m_hi")
        ss2_ready, h2_hi = sem("ss2_ready"), sem("h2_hi")
        f_hi, f_ready = sem("f_hi"), sem("f_ready")
        fin_ready, stored = sem("fin_ready"), sem("stored")

        block = ctx.enter_context(nc.Block())

        def piece_view(buf, v):
            kind = UNITS[v // 2][0]
            k = {"feat": KD, "ff1": KD, "ff2": 1}.get(kind, 2)
            return buf[:, v % RING].rearrange("p (k n) -> p k n", k=k)

        def piece_dram(v):
            u, half = UNITS[v // 2], v % 2
            if u[0] == "feat":
                return w_in[0, :, u[1] + P * half:u[1] + P * half + P].rearrange("(k p) n -> p k n", p=P)
            if u[0] == "ff1":
                c = 256 * u[1] + P * half
                return w_ff1[0, :, c:c + P].rearrange("(k p) n -> p k n", p=P)
            if u[0] == "ff2":
                r = 256 * u[1] + P * half
                return w_ff2[0, r:r + P, :].rearrange("(k p) n -> p k n", p=P)
            if u[0] == "tok":
                r, m, c = 512 * u[2] + 256 * half, w_in[0], u[1]
            elif u[0] == "branch":
                r, m, c = 256 * half, w_branch[0, u[1]], 512 * u[2]
            else:
                r, m, c = 512 * u[1] + 256 * half, w_out[0], 512 * u[2]
            return m[r:r + 256, c:c + 512].rearrange("(k p) n -> p k n", p=P)

        def mix_tile(t, j):
            return UNITS[t][1] // P + j

        def mix_dst(t, j):
            m = mix_tile(t, j)
            return (rmix, kmix, vmix, lmix)[m // 4][:, m % 4]

        @block.sync
        def _(sp):
            for tt in range(TT):
                sp.dma_start(xs[:, tt], x[0, P * tt:P * tt + P, :]).then_inc(x_in, 16)
            sp.dma_start(vec[:], vecs).then_inc(cst_in, 16)
            sp.dma_start(cst[:], consts).then_inc(cst_in, 16)
            for v in range(PIECES):
                if v >= RING:
                    sp.wait_ge(lo_done, v - RING + 1)
                sp.dma_start(piece_view(stage, v), piece_dram(v)).then_inc(loaded[v % RING], 16)
                if v == 1:
                    sp.dma_start(lora[0:64, 0], w_up[0]).then_inc(small_in, 16)
                    sp.dma_start(lora[64:65, 0], w0).then_inc(small_in, 16)
                    sp.dma_start(lora[64:128, 1], a_up[0]).then_inc(small_in, 16)
                    sp.dma_start(lora[:, 2], g_up[0]).then_inc(small_in, 16)
                    sp.dma_start(pool_sb[:], pool_w[0].rearrange("g c d -> c g d")).then_inc(small_in, 16)
            for n in range(4):
                sp.wait_ge(fin_ready, n + 1)
                tt, c = n // 2, n % 2
                sp.dma_start(out[0, P * tt:P * tt + P, 512 * c:512 * c + 512],
                             xs[:, tt, 512 * c:512 * c + 512]).then_inc(stored, 16)
            sp.wait_ge(stored, 64)

        @block.tensor
        def _(pe):
            def mm3(o, lh, ll, rh, rl, first, last):
                pe.matmul(o, lh, rh, start=first, stop=False)
                pe.matmul(o, lh, rl, start=False, stop=False)
                return pe.matmul(o, ll, rh, start=False, stop=last)

            def part(t, p):
                u, v = UNITS[t], 2 * t + p // 2
                if p % 2 == 0:
                    pe.wait_ge(lo_done, v + 1)
                wh, wl = piece_view(w_hi, v), piece_view(w_lo, v)
                i = p % 2
                if u[0] in ("feat", "ff1"):
                    name = ("unit", t) if u[0] == "feat" else ("ff", u[1])
                    if p == 0:
                        if u == ("ff1", 0):
                            for i4 in range(4):
                                copied(pe, ("h2", i4))
                        o = room(pe, name)
                    else:
                        o = ps(name)
                    j = p // 2
                    for k in range(4 * i, 4 * i + 4):
                        ins = mm3(o[:, T * j:T * j + T], wh[:, k], wl[:, k], h_hi[:, k], h_lo[:, k], k == 0, k == 7)
                elif u[0] == "ff2":
                    kt, buf = p // 2, 2 * (u[1] % 2)
                    if p == 0:
                        pe.wait_ge(f_ready, u[1] + 1)
                    for c in range(2):
                        name = ("mlp", i, c)
                        if u[1] == 0 and kt == 0:
                            room(pe, name)
                        ins = mm3(ps(name)[:], r_hi[:, buf + kt, P * i:P * i + P], r_lo[:, buf + kt, P * i:P * i + P],
                                  wh[:, 0, 512 * c:512 * c + 512], wl[:, 0, 512 * c:512 * c + 512],
                                  u[1] == 0 and kt == 0, u == UNITS[-1] and kt == 1)
                        if u == UNITS[-1] and kt == 1 and (i, c) != (1, 1):
                            ins.then_inc(full_of(name), 1)
                else:
                    if u[0] == "tok":
                        name, lh, ll, k0 = ("tok", u[1], i), h_hi, h_lo, 4 * u[2]
                        first, last = u[2] == 0, u[2] == 1
                    elif u[0] == "branch":
                        name, first, last = ("unit", t, i), True, True
                        lh, ll, k0 = {1: (y_hi, y_lo, 0), 2: (y_hi, y_lo, 4), 0: (r_hi, r_lo, 0)}[u[1]]
                        if p == 0:
                            if u[1] == 1:
                                copied(pe, ("pv", HEADS - 2))
                                copied(pe, ("pv", HEADS - 1))
                            elif u[1] == 2:
                                copied(pe, ("pool", 0))
                                copied(pe, ("pool", 1))
                            else:
                                pe.wait_ge(yr_ready, TT)
                    else:
                        name, lh, ll, k0 = ("out", u[2], i), y_hi, y_lo, 4 * u[1]
                        first, last = u[1] == 0, u[1] == 1
                        if p == 0:
                            copied(pe, ("m", 2 * u[1]))
                            copied(pe, ("m", 2 * u[1] + 1))
                    o = room(pe, name) if first and p < 2 else ps(name)
                    for kk in range(2):
                        k = 2 * (p // 2) + kk
                        ins = mm3(o[:], lh[:, k0 + k, P * i:P * i + P], ll[:, k0 + k, P * i:P * i + P],
                                  wh[:, kk], wl[:, kk], first and k == 0, last and k == 3)
                if p % 2:
                    ins.then_inc(used, 1)

            pe.wait_ge(cst_in, 32)
            pe.wait_ge(xn_ready, 2)
            for i in range(4):
                o = room(pe, ("x", i))
                for kk in range(2):
                    for tt in range(TT):
                        k = 2 * i + kk
                        ins = pe.transpose(o[:, T * kk + P * tt:T * kk + P * tt + P], xn[:, tt, P * k:P * k + P], ident)
                ins.then_inc(full_of(("x", i)), 1)
            for i in range(4):
                copied(pe, ("x", i))

            def products(c, g, kind):
                if kind == 0 and g == 0:
                    pe.wait_ge(ops_ready, 1)
                for e in range(2):
                    name = ("prod", c, g, kind, e)
                    o = room(pe, name)
                    rows = slice(HD * e, HD * e + HD)
                    for i in range(2):
                        j = 2 * g + i
                        if kind < 2:
                            ins = pe.matmul(o[:, 256 * i:256 * i + 256], bk[c][rows, kind, j], ar[c][rows, j],
                                            start=True, stop=True)
                        else:
                            ins = pe.matmul(o[:, P * i:P * i + P], ar[c][rows, j, 0], bk[c][rows, 0, j],
                                            start=True, stop=True)
                    ins.then_inc(full_of(name), 1)

            def extra(t, p):
                if (t, p) == (1, 3):
                    pe.wait_ge(small_in, 80)
                    pe.wait_ge(ones_ready, 1)
                    pe.wait_ge(lora_ready, 1)
                    for c in range(TT):
                        o = room(pe, ("z", c))
                        pe.matmul(o[:], th[0:65, P * c:P * c + P], lora[0:65, 0], start=True, stop=True)\
                          .then_inc(full_of(("z", c)), 1)
                    for i in range(2):
                        o = room(pe, ("a", i))
                        for jj in range(2):
                            j = 2 * i + jj
                            ins = pe.matmul(o[:, T * jj:T * jj + T], lora[64:128, 1, P * j:P * j + P], lmix[64:128, 0],
                                            start=True, stop=True)
                        ins.then_inc(full_of(("a", i)), 1)
                if (t, p) in ((2, 3), (3, 1)):
                    c = t - 2
                    copied(pe, ("z", c))
                    for i in range(2):
                        o = room(pe, ("cum", c, i))
                        for jj in range(2):
                            j = 2 * i + jj
                            ins = pe.matmul(o[:, 256 * jj:256 * jj + 129], sg[:, c, P * j:P * j + P],
                                            cst[:, C_CUM:C_CUM + 129], start=True, stop=True)
                        ins.then_inc(full_of(("cum", c, i)), 1)
                if (t, p) == (3, 3):
                    pe.wait_ge(ksq_ready, 1)
                    for i in range(2):
                        o = room(pe, ("kk", i))
                        pe.matmul(o[:], blk, ksq[:, 2 * i:2 * i + 2].rearrange("p j t -> p (j t)"),
                                  start=True, stop=True).then_inc(full_of(("kk", i)), 1)
                if (t, p) == (4, 3):
                    pe.wait_ge(lora_ready, 2)
                    for i in range(2):
                        o = room(pe, ("g", i))
                        for jj in range(2):
                            j = 2 * i + jj
                            ins = pe.matmul(o[:, T * jj:T * jj + T], lora[:, 2, P * j:P * j + P], sgx[:],
                                            start=True, stop=True)
                        ins.then_inc(full_of(("g", i)), 1)
                if (t, p) == (7, 1):
                    copied(pe, ("unit", 5))
                    copied(pe, ("unit", 6))
                    for c in range(TT):
                        o = room(pe, ("vt", c))
                        for j in range(PAIRS):
                            ins = pe.transpose(o[:, P * j:P * j + P], vmix[:, j, P * c:P * c + P], ident)
                        ins.then_inc(full_of(("vt", c)), 1)
                if (t, p) == (7, 3):
                    pe.wait_ge(rk_ready, 1)
                    for i in range(2):
                        o = room(pe, ("bonus", i))
                        pe.matmul(o[:], blk, ksq[:, 2 * i:2 * i + 2].rearrange("p j t -> p (j t)"),
                                  start=True, stop=True).then_inc(full_of(("bonus", i)), 1)
                if S_QK < t <= S_QK + 4 and p == 3:
                    n = t - 1 - S_QK
                    copied(pe, ("unit", t - 1))
                    o = room(pe, ("ss", n))
                    pe.matmul(o[:], blk, sq_att[n % 2], start=True, stop=True).then_inc(full_of(("ss", n)), 1)
                if product_place(t, p):
                    products(*product_place(t, p))
                if (t, p) == (9, 2):
                    for a, name in ((0, ("bt",)), (1, ("kt",))):
                        o = room(pe, name)
                        for j in range(PAIRS):
                            ins = pe.transpose(o[:, P * j:P * j + P], bk[0][:, a, j], ident)
                        ins.then_inc(full_of(name), 1)
                if level_places(t) and p == 0:
                    c, l = level_places(t)
                    for g in range(2):
                        if l == 0:
                            pe.wait_ge(nt_ready, 2 * c + g + 1)
                            pe.wait_ge(x1_ready, 2 * c + g + 1)
                        else:
                            copied(pe, ("X", c, l - 1, g))
                        o = room(pe, ("Y", c, l, g))
                        for i in range(4):
                            h = 4 * g + i
                            ins = pe.matmul(o[:, P * i:P * i + P], gm[:, h, 0], mx[:, h], start=True, stop=True)
                        ins.then_inc(full_of(("Y", c, l, g)), 1)
                if level_places(t) and p == 2:
                    c, l = level_places(t)
                    for g in range(2):
                        copied(pe, ("Y", c, l, g))
                        if l == 0:
                            pe.wait_ge(xt1_ready, 2 * c + g + 1)
                        else:
                            copied(pe, ("XT", c, l - 1, g))
                        if l < LEVELS - 1:
                            o = room(pe, ("X", c, l, g))
                            for i in range(4):
                                h = 4 * g + i
                                ins = pe.matmul(o[:, P * i:P * i + P], mxt[:, h], my[:, h], start=True, stop=True)
                            ins.then_inc(full_of(("X", c, l, g)), 1)
                        o = room(pe, ("XT", c, l, g))
                        for i in range(4):
                            h = 4 * g + i
                            ins = pe.matmul(o[:, P * i:P * i + P], my[:, h], mxt[:, h], start=True, stop=True)
                        ins.then_inc(full_of(("XT", c, l, g)), 1)
                if t in S_APPLY:
                    c = S_APPLY.index(t)
                    if p == 0:
                        for g in range(2):
                            for e in range(2):
                                copied(pe, ("prod", c, g, 1, e))
                        copied(pe, ("vt", c))
                        if c == 1:
                            copied(pe, ("state",))
                        for e in range(2):
                            o = room(pe, ("rhs", c, e))
                            rows = slice(HD * e, HD * e + HD)
                            for j in range(PAIRS):
                                h = 2 * j + e
                                ins = pe.matmul(o[:, HD * j:HD * j + HD], gm[:, h, 2], vtok[:, c, HD * h:HD * h + HD],
                                                start=True, stop=c == 0)
                                if c == 1:
                                    ins = pe.matmul(o[:, HD * j:HD * j + HD], ar[c][rows, j, 0], s_in[rows, j],
                                                    start=False, stop=True)
                            ins.then_inc(full_of(("rhs", c, e)), 1)
                    if p == 1:
                        for e in range(2):
                            copied(pe, ("rhs", c, e))
                        for g in range(2):
                            copied(pe, ("XT", c, LEVELS - 1, g))
                        o = room(pe, ("sa", c))
                        for h in range(HEADS):
                            ins = pe.matmul(o[:, HD * h:HD * h + HD], mxt[:, h], rhs_sb[:, h], start=True, stop=True)
                        ins.then_inc(full_of(("sa", c)), 1)
                    if p == 2:
                        copied(pe, ("sa", c))
                        for e in range(2):
                            o = room(pe, ("o", c, e))
                            rows = slice(HD * e, HD * e + HD)
                            for j in range(PAIRS):
                                h = 2 * j + e
                                oo = o[:, HD * j:HD * j + HD]
                                pe.matmul(oo, gm[:, h, 1], sa_sb[:, h], start=True, stop=False)
                                ins = pe.matmul(oo, gm[:, h, 3], vtok[:, c, HD * h:HD * h + HD],
                                                start=False, stop=c == 0)
                                if c == 1:
                                    ins = pe.matmul(oo, ar[c][rows, j, 1], s_in[rows, j], start=False, stop=True)
                            ins.then_inc(full_of(("o", c, e)), 1)
                    if p == 3 and c == 0:
                        copied(pe, ("bt",))
                        copied(pe, ("kt",))
                        o = room(pe, ("state",))
                        for h in range(HEADS):
                            j, e = h // 2, h % 2
                            oo = o[HD * e:HD * e + HD, HD * j:HD * j + HD]
                            pe.matmul(oo, btok[:, HD * h:HD * h + HD], sa_sb[:, h], start=True, stop=False)
                            ins = pe.matmul(oo, ktok[:, HD * h:HD * h + HD], vtok[:, 0, HD * h:HD * h + HD],
                                            start=False, stop=True)
                        ins.then_inc(full_of(("state",)), 1)
                if (t, p) in ((S_GN[0], 3), (S_GN[1], 0)):
                    c = S_GN.index(t)
                    pe.wait_ge(on_ready, c + 1)
                    o = room(pe, ("ot", c))
                    for j in range(PAIRS):
                        ins = pe.transpose(o[:, P * j:P * j + P], oc[:, P * j:P * j + P], ident)
                    ins.then_inc(full_of(("ot", c)), 1)
                if S_HEAD <= t <= S_HEAD + HEADS:
                    h = t - S_HEAD
                    if p == 1 and h < HEADS:
                        pe.wait_ge(qk_ready, 4)
                        j, rows = h // 2, slice(HD * (h % 2), HD * (h % 2) + HD)
                        o = room(pe, ("score", h))
                        pe.matmul(o[:, 0:P], qraw[rows, j, 0:P], kraw[rows, j, 0:P], start=True, stop=True)
                        pe.matmul(o[:, P:P + T], qraw[rows, j, P:T], kraw[rows, j], start=True, stop=True)\
                          .then_inc(full_of(("score", h)), 1)
                    if p == 0 and h >= 1:
                        pe.wait_ge(p_ready, h)
                        o = room(pe, ("pt", h - 1))
                        for i in range(3):
                            ins = pe.transpose(o[:, P * i:P * i + P], prob[:, P * i:P * i + P], ident)
                        ins.then_inc(full_of(("pt", h - 1)), 1)
                    if p == 3 and h >= 1:
                        n = h - 1
                        copied(pe, ("pt", n))
                        for tt in range(TT):
                            copied(pe, ("tok", N_RWKV + 2 * W, tt))
                        o = room(pe, ("pv", n))
                        rows = slice(HD * (n % 2), HD * (n % 2) + HD)
                        pe.matmul(o[rows, 0:T], vatt[:, 0, HD * n:HD * n + HD], prob_t[:, 0:T], start=True, stop=False)
                        pe.matmul(o[rows, P:T], vatt[:, 1, HD * n:HD * n + HD], prob_t[:, T:T + P],
                                  start=False, stop=True).then_inc(full_of(("pv", n)), 1)
                if t == S_PY and p in (0, 2):
                    i = p // 2
                    pe.wait_ge(pd_ready, 2 * i + 2)
                    o = room(pe, ("pool", i))
                    for gi in range(2):
                        g = 2 * i + gi
                        ins = pe.matmul(o[:, T * gi:T * gi + T], pool_sb[:, g], pu[:, g, PAD:PAD + T],
                                        start=True, stop=True)
                    ins.then_inc(full_of(("pool", i)), 1)
                if (t, p) in ((S_OUT - 1, 3), (S_OUT, 3)):
                    ch = t - S_OUT + 1
                    pe.wait_ge(m_pre, ch + 1)
                    for i in range(2):
                        o = room(pe, ("m", 2 * ch + i))
                        for kk in range(2):
                            for tt in range(TT):
                                k = 2 * i + kk
                                ins = pe.transpose(o[:, T * kk + P * tt:T * kk + P * tt + P],
                                                   gates[ch][:, tt, P * k:P * k + P], ident)
                        ins.then_inc(full_of(("m", 2 * ch + i)), 1)
                if (t, p) == (S_FF - 1, 3):
                    for i in range(4):
                        for tt in range(TT):
                            copied(pe, ("out", i // 2, tt))
                        o = room(pe, ("h2", i))
                        for kk in range(2):
                            for tt in range(TT):
                                k = 2 * i + kk
                                ins = pe.transpose(o[:, T * kk + P * tt:T * kk + P * tt + P],
                                                   xs[:, tt, P * k:P * k + P], ident)
                        ins.then_inc(full_of(("h2", i)), 1)

            for t in range(SLOTS):
                for p in range(4):
                    part(t, p)
                    extra(t, p)

        @block.scalar
        def _(act):
            def high(v):
                act.wait_ge(loaded[v % RING], 16 * (v // RING + 1))
                if v >= RING:
                    act.wait_ge(used, v - RING + 1)
                nc.scalar.copy(w_hi[:, v % RING], stage[:, v % RING]).then_inc(hi_done, 1)

            for tt in range(TT):
                act.wait_ge(x_in, 16 * TT)
                nc.scalar.activation(xn[:, tt], xs[:, tt], ACT.Square, accum_out=ss1[:, tt:tt + 1]).then_inc(ss_ready, 1)
            act.wait_ge(ms_ready, 1)
            nc.scalar.activation(rs1, rs1, ACT.Sqrt).then_inc(root_ready, 1)
            act.wait_ge(rs_ready, 1)
            act.wait_ge(ss_ready, 2)
            for tt in range(TT):
                nc.scalar.mul(xn[:, tt], xs[:, tt], rs1[:, tt:tt + 1]).then_inc(xn_ready, 1)
            act.wait_ge(cst_in, 32)
            for i in range(4):
                o = take(act, ("x", i))
                for kk in range(2):
                    k = 2 * i + kk
                    ins = nc.scalar.mul(h_hi[:, k], o[:, T * kk:T * kk + T], col(V_G1 + k))
                ins.then_inc(h_hi_done, 1)
                if i < AHEAD:
                    high(i)

            def extra(t, p):
                if (t, p) == (1, 0):
                    copied(act, ("unit", 0))
                    nc.scalar.activation(th[0:64], lmix[0:64, 0], ACT.Tanh).then_inc(lora_ready, 1)
                    nc.scalar.activation(sgx[:], lmix[:, 1], ACT.Sigmoid).then_inc(lora_ready, 1)
                if (t, p) == (1, 3):
                    for c in range(TT):
                        o = take(act, ("z", c))
                        nc.scalar.activation(sg[:, c], o[:], ACT.Sigmoid).then_inc(drained_of(("z", c)), 1)
                    for i in range(2):
                        o = take(act, ("a", i))
                        for jj in range(2):
                            j = 2 * i + jj
                            ins = nc.scalar.activation(a_s[:, j], o[:, T * jj:T * jj + T], ACT.Sigmoid, bias=col(V_A0 + j))
                        ins.then_inc(drained_of(("a", i)), 1)
                if (t, p) in ((2, 3), (3, 1)):
                    c = t - 2
                    for i in range(2):
                        o = take(act, ("cum", c, i))
                        v = o[:].rearrange("p (j t) -> p j t", j=2)[:, :, 0:129]
                        nc.scalar.activation(e_up[:, c, 2 * i:2 * i + 2], v, ACT.Exp)
                        nc.scalar.activation(e_dn[:, c, 2 * i:2 * i + 2], v, ACT.Exp, scale=-1.0)\
                          .then_inc(drained_of(("cum", c, i)), 1)
                    if t == 3:
                        act.wait_ge(kkraw_ready, 1)
                        nc.scalar.activation(ksq, kkn, ACT.Square).then_inc(ksq_ready, 1)
                if (t, p) == (3, 3):
                    copied(act, ("kk", 0))
                    copied(act, ("kk", 1))
                    nc.scalar.activation(ksq, ksq, ACT.Sqrt).then_inc(kkroot_ready, 1)
                if (t, p) == (4, 3):
                    for i in range(2):
                        o = take(act, ("g", i))
                        nc.scalar.copy(gg[:, 2 * i:2 * i + 2], o[:].rearrange("p (j t) -> p j t", j=2))\
                          .then_inc(drained_of(("g", i)), 1)
                if (t, p) == (7, 1):
                    for c in range(TT):
                        o = take(act, ("vt", c))
                        nc.scalar.copy(vtok[:, c], o[:]).then_inc(drained_of(("vt", c)), 1)
                if S_QK < t <= S_QK + 4 and p == 3:
                    n = t - 1 - S_QK
                    copied(act, ("ss", n))
                    nc.scalar.activation(sq_att[n % 2], sq_att[n % 2], ACT.Sqrt).then_inc(qroot_ready, 1)
                if (t, p) == (9, 2):
                    for dst, name in ((btok, ("bt",)), (ktok, ("kt",))):
                        o = take(act, name)
                        nc.scalar.copy(dst, o[:]).then_inc(drained_of(name), 1)
                if level_places(t) and p == 2:
                    c, l = level_places(t)
                    for g in range(2):
                        hs = slice(4 * g, 4 * g + 4)
                        for kind, dst in (("X", mx), ("XT", mxt)):
                            if kind == "X" and l == LEVELS - 1:
                                continue
                            o = take(act, (kind, c, l, g))
                            nc.scalar.copy(dst[:, hs], o[:].rearrange("p (h s) -> p h s", h=4))\
                              .then_inc(drained_of((kind, c, l, g)), 1)
                if t in S_APPLY:
                    c = S_APPLY.index(t)
                    if p == 1:
                        o = take(act, ("sa", c))
                        nc.scalar.copy(sa_sb, o[:].rearrange("p (h v) -> p h v", h=HEADS)).then_inc(drained_of(("sa", c)), 1)
                    if p == 2:
                        if c:
                            act.wait_ge(on_ready, c)
                        for e in range(2):
                            o = take(act, ("o", c, e))
                            nc.scalar.copy(o_sb.rearrange("p (j e) v -> p e j v", e=2)[:, e],
                                           o[:, 0:256].rearrange("p (j v) -> p j v", j=PAIRS))\
                              .then_inc(drained_of(("o", c, e)), 1)
                if t - 1 in S_APPLY:
                    c = S_APPLY.index(t - 1)
                    if p == 0:
                        act.wait_ge(oc_ready, c + 1)
                        nc.scalar.activation(osq, oc, ACT.Square).then_inc(osq_ready, 1)
                    if p == 1:
                        act.wait_ge(gvar_ready, c + 1)
                        nc.scalar.activation(gvar, gvar, ACT.Sqrt).then_inc(groot_ready, 1)
                if (t, p) in ((S_GN[0], 3), (S_GN[1], 0)):
                    c = S_GN.index(t)
                    act.wait_ge(yr_pre, c + 1)
                    nc.scalar.copy(r_hi[:, :, P * c:P * c + P], ytmp).then_inc(yr_hi_done, 1)
                if S_HEAD <= t <= S_HEAD + HEADS:
                    h = t - S_HEAD
                    if p == 1 and h < HEADS:
                        act.wait_ge(neg_ready, 2 * h + 2)
                        for tt in range(TT):
                            w = prob[:, 0:P] if tt == 0 else prob[:, P:P + T]
                            nc.scalar.activation(w, w, ACT.Exp, bias=nmax[:, tt:tt + 1],
                                                 accum_out=psm[:, tt:tt + 1]).then_inc(exps_ready, 1)
                    if p == 0 and h >= 1:
                        o = take(act, ("pt", h - 1))
                        nc.scalar.copy(prob_t, o[:, 0:384]).then_inc(drained_of(("pt", h - 1)), 1)
                    if p == 3 and h >= 1:
                        n = h - 1
                        o = take(act, ("pv", n))
                        rows = slice(HD * (n % 2), HD * (n % 2) + HD)
                        nc.scalar.copy(y_hi[rows, n // 2], o[rows, 0:T]).then_inc(ya_hi, 1)
                if t == S_PY and p in (0, 2):
                    i = p // 2
                    o = take(act, ("pool", i))
                    for gi in range(2):
                        g = 2 * i + gi
                        ins = nc.scalar.mul(y_hi[:, 4 + g], o[:, T * gi:T * gi + T], col(V_PS + g))
                    ins.then_inc(yp_hi, 1)
                if (t, p) in ((S_OUT - 1, 3), (S_OUT, 3)):
                    ch = t - S_OUT + 1
                    for i in range(2):
                        o = take(act, ("m", 2 * ch + i))
                        k = 4 * ch + 2 * i
                        nc.scalar.copy(y_hi[:, k:k + 2], o[:].rearrange("p (k t) -> p k t", k=2)).then_inc(m_hi, 1)
                if (t, p) == (S_FF - 1, 3):
                    for i in range(4):
                        o = take(act, ("h2", i))
                        for kk in range(2):
                            k = 2 * i + kk
                            ins = nc.scalar.mul(h_hi[:, k], o[:, T * kk:T * kk + T], col(V_G2 + k))
                        ins.then_inc(h2_hi, 1)
                    for ch in range(2):
                        for tt in range(TT):
                            copied(act, ("out", ch, tt))
                    for tt in range(TT):
                        nc.scalar.activation(big[:, 2 + tt], xs[:, tt], ACT.Square, accum_out=ss2[:, tt:tt + 1])\
                          .then_inc(ss2_ready, 1)

            def finish(t):
                u = UNITS[t]
                if t < S_QK:
                    act.wait_ge(consts_ready, 1)
                    o = take(act, ("unit", t))
                    for j in range(2):
                        nc.scalar.mul(mix_dst(t, j), o[:, T * j:T * j + T], omu[:, mix_tile(t, j):mix_tile(t, j) + 1])\
                          .then_inc(keep_part, 1)
                elif t < S_VA:
                    n = t - S_QK
                    o = take(act, ("unit", t))
                    nc.scalar.copy((qraw if n < 2 else kraw)[:, 2 * (n % 2):2 * (n % 2) + 2],
                                   o[:].rearrange("p (j t) -> p j t", j=2))
                    if n >= 2:
                        act.wait_ge(qk_ready, n - 1)
                    nc.scalar.activation(sq_att[n % 2], o[:], ACT.Square).then_inc(drained_of(("unit", t)), 1)
                elif u[0] == "tok" and u[2] == 1:
                    p = (t - S_GATE) // 2
                    for tt in range(TT):
                        name = ("tok", u[1], tt)
                        o = take(act, name)
                        if t < S_GATE:
                            nc.scalar.copy(vatt[:, tt], o[:]).then_inc(drained_of(name), 1)
                        else:
                            nc.scalar.activation(gates[p][:, tt], o[:], ACT.Sigmoid).then_inc(drained_of(name), 1)
                elif t in (S_POOL, S_POOL + 1):
                    i = t - S_POOL
                    act.wait_ge(pad_ready, 1)
                    o = take(act, ("unit", t))
                    nc.scalar.copy(pu[:, 2 * i:2 * i + 2, PAD:PAD + T], o[:].rearrange("p (g t) -> p g t", g=2))\
                      .then_inc(drained_of(("unit", t)), 1)
                elif u[0] == "ff1":
                    i = u[1]
                    if i >= 2:
                        act.wait_ge(f_ready, i - 1)
                    o = take(act, ("ff", i))
                    nc.scalar.activation(ffs[i % 2], o[:], ACT.Relu).then_inc(drained_of(("ff", i)), 1)
                    copied(act, ("ff", i))
                    if i >= 2:
                        act.wait_ge(used, 2 * (UNITS.index(("ff2", i - 2)) + 1))
                    nc.scalar.activation(r_hi[:, 2 * (i % 2):2 * (i % 2) + 2], ffs[i % 2].rearrange("p (k t) -> p k t", k=2),
                                         ACT.Square).then_inc(f_hi, 1)

            for t in range(SLOTS):
                if 2 * t + AHEAD < PIECES:
                    high(2 * t + AHEAD)
                extra(t, 0)
                extra(t, 1)
                if 2 * t + 1 + AHEAD < PIECES:
                    high(2 * t + 1 + AHEAD)
                extra(t, 2)
                finish(t)
                extra(t, 3)

        @block.vector
        def _(dve):
            step = [0]

            def link(ins):
                step[0] += 1
                ins.then_inc(own, 1)
                dve.wait_ge(own, step[0])

            def low(v):
                dve.wait_ge(hi_done, v + 1)
                dve.tensor_tensor(w_lo[:, v % RING], stage[:, v % RING], w_hi[:, v % RING].bitcast(F32), ALU.subtract)\
                   .then_inc(lo_done, 1)

            def rest(dst, src, high_part):
                return dve.tensor_tensor(dst, src, high_part.bitcast(F32), ALU.subtract)

            dve.wait_ge(cst_in, 32)
            dve.tensor_scalar(omu, vec[:, V_MU:V_MU + 14], -1.0, 1.0, ALU.mult, ALU.add)
            dve.tensor_scalar(oka, vec[:, V_KA:V_KA + 4], -1.0, 1.0, ALU.mult, ALU.add)
            link(dve.tensor_scalar(gq8, vec[:, V_QN:V_QN + 1], HD ** -0.5, None, ALU.mult))
            dve.sem_inc(consts_ready, 1)
            dve.wait_ge(ss_ready, 2)
            dve.tensor_scalar(rs1, ss1, 1.0 / D, RMS_EPS, ALU.mult, ALU.add).then_inc(ms_ready, 1)
            dve.wait_ge(root_ready, 1)
            dve.reciprocal(rs1, rs1).then_inc(rs_ready, 1)
            for i in range(4):
                dve.wait_ge(h_hi_done, i + 1)
                o = take(dve, ("x", i))
                for kk in range(2):
                    k = 2 * i + kk
                    ins = dve.scalar_tensor_tensor(out=h_lo[:, k], in0=o[:, T * kk:T * kk + T], scalar=col(V_G1 + k),
                                                   in1=h_hi[:, k].bitcast(F32), op0=ALU.mult, op1=ALU.subtract)
                ins.then_inc(drained_of(("x", i)), 1)
                if i < AHEAD:
                    low(i)

            def extra(t, p):
                if (t, p) == (3, 0):
                    copied(dve, ("unit", 1))
                    copied(dve, ("unit", 2))
                    for j in range(PAIRS):
                        ins = dve.tensor_scalar(kkn[:, j], kmix[:, j], col(V_KK + j), None, ALU.mult)
                    ins.then_inc(kkraw_ready, 1)
                if (t, p) == (3, 3):
                    for i in range(2):
                        o = take(dve, ("kk", i))
                        dve.tensor_scalar(ksq[:, 2 * i:2 * i + 2], o[:].rearrange("p (j t) -> p j t", j=2), 1e-24, None,
                                          ALU.max).then_inc(drained_of(("kk", i)), 1)
                if (t, p) == (4, 0):
                    dve.wait_ge(kkroot_ready, 1)
                    link(dve.reciprocal(ksq, ksq))
                    link(dve.tensor_tensor(kkn, kkn, ksq, ALU.mult))
                    copied(dve, ("a", 0))
                    copied(dve, ("a", 1))
                    for j in range(PAIRS):
                        ins = dve.tensor_scalar(k2[:, j], a_s[:, j], col(V_KA + j), oka[:, j:j + 1], ALU.mult, ALU.add)
                    link(ins)
                    dve.tensor_tensor(k2, k2, kmix, ALU.mult)
                    link(dve.tensor_tensor(a_s, a_s, kkn, ALU.mult))
                if (t, p) in ((4, 3), (5, 0)):
                    c = t - 4
                    for i in range(2):
                        copied(dve, ("cum", c, i))
                    ts = slice(P * c, P * c + P)
                    dve.tensor_tensor(bk[c][:, 0], a_s[:, :, ts], e_dn[:, c, :, 1:129], ALU.mult)
                    dve.tensor_tensor(bk[c][:, 1], k2[:, :, ts], e_dn[:, c, :, 1:129], ALU.mult)
                    dve.scalar_tensor_tensor(out=ar[c][:, :, 0], in0=kkn[:, :, ts], scalar=-1.0, in1=e_up[:, c, :, 0:128],
                                             op0=ALU.mult, op1=ALU.mult)
                if (t, p) == (5, 1):
                    copied(dve, ("unit", 3))
                    copied(dve, ("unit", 4))
                    for c in range(TT):
                        dve.tensor_tensor(ar[c][:, :, 1], rmix[:, :, P * c:P * c + P], e_up[:, c, :, 1:129], ALU.mult)
                    ins = dve.tensor_tensor(e_end, e_up[:, 0, :, 128:129].squeeze(2), e_dn[:, 1, :, 0:1].squeeze(2), ALU.mult)
                    ins.then_inc(ops_ready, 1)
                    for j in range(PAIRS):
                        ins = dve.scalar_tensor_tensor(out=ksq[:, j], in0=rmix[:, j], scalar=col(V_RK + j), in1=k2[:, j],
                                                       op0=ALU.mult, op1=ALU.mult)
                    ins.then_inc(rk_ready, 1)
                if (t, p) == (7, 3):
                    copied(dve, ("unit", 5))
                    copied(dve, ("unit", 6))
                    for i in range(2):
                        o = take(dve, ("bonus", i))
                        dve.tensor_tensor(bonus[:, 2 * i:2 * i + 2], o[:].rearrange("p (j t) -> p j t", j=2),
                                          vmix[:, 2 * i:2 * i + 2], ALU.mult).then_inc(drained_of(("bonus", i)), 1)
                if S_QK < t <= S_QK + 4 and p == 3:
                    n = t - 1 - S_QK
                    o = take(dve, ("ss", n))
                    dve.tensor_scalar(sq_att[n % 2], o[:], 1.0 / HD, RMS_EPS, ALU.mult, ALU.add)\
                       .then_inc(drained_of(("ss", n)), 1)
                if S_QK + 2 <= t < S_QK + 6 and p == 0:
                    n = t - 2 - S_QK
                    dve.wait_ge(qroot_ready, n + 1)
                    link(dve.reciprocal(sq_att[n % 2], sq_att[n % 2]))
                    dst = (qraw if n < 2 else kraw)[:, 2 * (n % 2):2 * (n % 2) + 2]
                    dve.scalar_tensor_tensor(out=dst, in0=dst, scalar=gq8 if n < 2 else col(V_KN),
                                             in1=sq_att[n % 2].rearrange("p (j t) -> p j t", j=2),
                                             op0=ALU.mult, op1=ALU.mult).then_inc(qk_ready, 1)
                if product_place(t, p):
                    c, g, kind = product_place(t, p)
                    for e in range(2):
                        name = ("prod", c, g, kind, e)
                        o = take(dve, name)
                        if kind < 2:
                            dst = gm.rearrange("p (i e) a s -> p e i a s", e=2)[:, e, 2 * g:2 * g + 2, 2 * kind:2 * kind + 2]
                            dve.tensor_tensor(dst.rearrange("p i a s -> p i (a s)"),
                                              o[:].rearrange("p (i n) -> p i n", i=2), wide(cst[:, C_SI:C_SI + 256], 2),
                                              ALU.mult).then_inc(drained_of(name), 1)
                        else:
                            dve.tensor_tensor(mx.rearrange("p (i e) s -> p e i s", e=2)[:, e, 2 * g:2 * g + 2],
                                              o[:, 0:256].rearrange("p (i s) -> p i s", i=2),
                                              wide(cst[:, C_M1:C_M1 + P], 2), ALU.mult).then_inc(drained_of(name), 1)
                    if kind == 2:
                        hs = slice(4 * g, 4 * g + 4)
                        dve.wait_ge(nt_ready, 2 * c + g + 1)
                        dve.tensor_tensor(mxt[:, hs], gm[:, hs, 0], wide(cst[:, C_M1T:C_M1T + P], 4), ALU.mult)\
                           .then_inc(xt1_ready, 1)
                if level_places(t) and p == 0:
                    c, l = level_places(t)
                    for g in range(2):
                        o = take(dve, ("Y", c, l, g))
                        dve.tensor_tensor(my[:, 4 * g:4 * g + 4], o[:].rearrange("p (h s) -> p h s", h=4),
                                          wide(cst[:, C_LEV + P * l:C_LEV + P * l + P], 4), ALU.mult)\
                           .then_inc(drained_of(("Y", c, l, g)), 1)
                if t in S_APPLY:
                    c = S_APPLY.index(t)
                    if p == 0:
                        for e in range(2):
                            o = take(dve, ("rhs", c, e))
                            dve.tensor_copy(rhs_sb.rearrange("p (j e) v -> p e j v", e=2)[:, e],
                                            o[:, 0:256].rearrange("p (j v) -> p j v", j=PAIRS))\
                               .then_inc(drained_of(("rhs", c, e)), 1)
                    if p == 3 and c == 0:
                        o = take(dve, ("state",))
                        for j in range(PAIRS):
                            ins = dve.tensor_scalar(s_in[:, j], o[:, HD * j:HD * j + HD], e_end[:, j:j + 1], None, ALU.mult)
                        ins.then_inc(drained_of(("state",)), 1)
                if t - 1 in S_APPLY:
                    c = S_APPLY.index(t - 1)
                    heads = lambda v: v.rearrange("p (h v) -> p h v", h=HEADS)
                    per_head = lambda v: v.unsqueeze(2).to_broadcast([P, HEADS, HD])
                    if p == 0:
                        copied(dve, ("o", c, 0))
                        copied(dve, ("o", c, 1))
                        link(dve.tensor_reduce(gsum, o_sb, AX_X, ALU.add))
                        link(dve.tensor_scalar(gsum, gsum, -1.0 / HD, None, ALU.mult))
                        dve.tensor_tensor(heads(oc), o_sb, per_head(gsum), ALU.add).then_inc(oc_ready, 1)
                    if p == 1:
                        dve.wait_ge(osq_ready, c + 1)
                        link(dve.tensor_reduce(gvar, heads(osq), AX_X, ALU.add))
                        dve.tensor_scalar(gvar, gvar, 1.0 / HD, GN_EPS, ALU.mult, ALU.add).then_inc(gvar_ready, 1)
                    if p == 2:
                        dve.wait_ge(groot_ready, c + 1)
                        link(dve.reciprocal(gvar, gvar))
                        dve.tensor_tensor(heads(oc), heads(oc), per_head(gvar), ALU.mult).then_inc(on_ready, 1)
                if (t, p) in ((S_GN[0], 3), (S_GN[1], 0)):
                    c = S_GN.index(t)
                    ts = slice(P * c, P * c + P)
                    o = take(dve, ("ot", c))
                    for j in range(PAIRS):
                        ins = dve.tensor_scalar(ytmp[:, j], o[:, P * j:P * j + P], col(V_LG + j), col(V_LB + j),
                                                ALU.mult, ALU.add)
                    ins.then_inc(drained_of(("ot", c)), 1)
                    copied(dve, ("ot", c))
                    link(dve.tensor_tensor(ytmp, ytmp, bonus[:, :, ts], ALU.add))
                    copied(dve, ("g", 0))
                    copied(dve, ("g", 1))
                    dve.tensor_tensor(ytmp, ytmp, gg[:, :, ts], ALU.mult).then_inc(yr_pre, 1)
                    dve.wait_ge(yr_hi_done, c + 1)
                    rest(r_lo[:, :, ts], ytmp, r_hi[:, :, ts]).then_inc(yr_ready, 1)
                if S_HEAD <= t <= S_HEAD + HEADS:
                    h = t - S_HEAD
                    if p == 1 and h < HEADS:
                        o = take(dve, ("score", h))
                        dve.scalar_tensor_tensor(out=prob, in0=cst[:, C_BIAS:C_BIAS + 384], scalar=SLOPES[h],
                                                 in1=o[:, 0:384], op0=ALU.mult, op1=ALU.add)\
                           .then_inc(drained_of(("score", h)), 1)
                        copied(dve, ("score", h))
                        dve.tensor_reduce(nmax[:, 0:1], prob[:, 0:P], AX_X, ALU.max, negate=True).then_inc(neg_ready, 1)
                        dve.tensor_reduce(nmax[:, 1:2], prob[:, P:P + T], AX_X, ALU.max, negate=True).then_inc(neg_ready, 1)
                    if p == 2 and h < HEADS:
                        dve.wait_ge(exps_ready, 2 * h + 2)
                        link(dve.reciprocal(psm, psm))
                        dve.tensor_scalar(prob[:, 0:P], prob[:, 0:P], psm[:, 0:1], None, ALU.mult)
                        dve.tensor_scalar(prob[:, P:P + T], prob[:, P:P + T], psm[:, 1:2], None, ALU.mult)\
                           .then_inc(p_ready, 1)
                    if p == 3 and h >= 1:
                        n = h - 1
                        dve.wait_ge(ya_hi, h)
                        o = take(dve, ("pv", n))
                        rows = slice(HD * (n % 2), HD * (n % 2) + HD)
                        rest(y_lo[rows, n // 2], o[rows, 0:T], y_hi[rows, n // 2]).then_inc(drained_of(("pv", n)), 1)
                if t == S_PY and p in (0, 2):
                    i = p // 2
                    dve.wait_ge(yp_hi, i + 1)
                    o = take(dve, ("pool", i))
                    for gi in range(2):
                        g = 2 * i + gi
                        ins = dve.scalar_tensor_tensor(out=y_lo[:, 4 + g], in0=o[:, T * gi:T * gi + T], scalar=col(V_PS + g),
                                                       in1=y_hi[:, 4 + g].bitcast(F32), op0=ALU.mult, op1=ALU.subtract)
                    ins.then_inc(drained_of(("pool", i)), 1)
                if (t, p) in ((S_OUT - 1, 3), (S_OUT, 3)):
                    ch = t - S_OUT + 1
                    for i in range(2):
                        dve.wait_ge(m_hi, 2 * ch + i + 1)
                        o = take(dve, ("m", 2 * ch + i))
                        k = 4 * ch + 2 * i
                        rest(y_lo[:, k:k + 2], o[:].rearrange("p (k t) -> p k t", k=2), y_hi[:, k:k + 2])\
                            .then_inc(drained_of(("m", 2 * ch + i)), 1)
                if (t, p) == (S_FF - 1, 3):
                    for i in range(4):
                        dve.wait_ge(h2_hi, i + 1)
                        o = take(dve, ("h2", i))
                        for kk in range(2):
                            k = 2 * i + kk
                            ins = dve.scalar_tensor_tensor(out=h_lo[:, k], in0=o[:, T * kk:T * kk + T], scalar=col(V_G2 + k),
                                                           in1=h_hi[:, k].bitcast(F32), op0=ALU.mult, op1=ALU.subtract)
                        ins.then_inc(drained_of(("h2", i)), 1)
                    dve.wait_ge(ss2_ready, 2)
                    link(dve.tensor_scalar(r2, ss2, 1.0 / D, RMS_EPS, ALU.mult, ALU.add))
                    link(dve.reciprocal(r2, r2))

            def finish(t):
                u = UNITS[t]
                if t < S_QK:
                    o = take(dve, ("unit", t))
                    dve.wait_ge(keep_part, 2 * t + 2)
                    for j in range(2):
                        dst, m = mix_dst(t, j), mix_tile(t, j)
                        ins = dve.scalar_tensor_tensor(out=dst[:, 1:T], in0=o[:, T * j:T * j + T - 1], scalar=col(V_MU + m),
                                                       in1=dst[:, 1:T], op0=ALU.mult, op1=ALU.add)
                    ins.then_inc(drained_of(("unit", t)), 1)
                elif u[0] == "branch":
                    n, ch = u[1], u[2]
                    g = 2 * n + ch
                    for tt in range(TT):
                        o = take(dve, ("unit", t, tt))
                        copied(dve, ("tok", N_RWKV + N_ATTN + N_POOL + 512 * g, tt))
                        dve.tensor_tensor(gates[g][:, tt], gates[g][:, tt], o[:], ALU.mult)\
                           .then_inc(drained_of(("unit", t, tt)), 1)
                    if n == 0:
                        for tt in range(TT):
                            copied(dve, ("unit", t, tt))
                        dve.wait_ge(sum_ready, ch + 1)
                        dve.tensor_tensor(gates[ch], gates[ch], gates[2 + ch], ALU.add).then_inc(m_pre, 1)
                elif u[0] == "out" and u[1] == 1:
                    for tt in range(TT):
                        name = ("out", u[2], tt)
                        o = take(dve, name)
                        xc = xs[:, tt, 512 * u[2]:512 * u[2] + 512]
                        dve.tensor_tensor(xc, xc, o[:], ALU.add).then_inc(drained_of(name), 1)
                elif u[0] == "ff1":
                    i = u[1]
                    copied(dve, ("ff", i))
                    link(dve.tensor_tensor(fsq[i % 2], ffs[i % 2], ffs[i % 2], ALU.mult))
                    dve.wait_ge(f_hi, i + 1)
                    b = 2 * (i % 2)
                    rest(r_lo[:, b:b + 2], fsq[i % 2].rearrange("p (k t) -> p k t", k=2), r_hi[:, b:b + 2])\
                        .then_inc(f_ready, 1)

            for t in range(SLOTS):
                if 2 * t + AHEAD < PIECES:
                    low(2 * t + AHEAD)
                extra(t, 0)
                extra(t, 1)
                if 2 * t + 1 + AHEAD < PIECES:
                    low(2 * t + 1 + AHEAD)
                extra(t, 2)
                finish(t)
                extra(t, 3)
            for tt in range(TT):
                for c in range(2):
                    if (tt, c) == (1, 1):
                        dve.wait_ge(used, PIECES)
                        o = ps(("mlp", tt, c))
                    else:
                        o = take(dve, ("mlp", tt, c))
                    xc = xs[:, tt, 512 * c:512 * c + 512]
                    dve.scalar_tensor_tensor(out=xc, in0=o[:], scalar=r2[:, tt:tt + 1], in1=xc, op0=ALU.mult, op1=ALU.add)\
                       .then_inc(fin_ready, 1)

        @block.gpsimd
        def _(pool):
            pool.memset(th[64:65], 1.0).then_inc(ones_ready, 1)

            def add_identity(c):
                for g in range(2):
                    hs = slice(4 * g, 4 * g + 4)
                    for e in range(2):
                        copied(pool, ("prod", c, g, 0, e))
                    pool.tensor_tensor(gm[:, hs, 0], gm[:, hs, 0], wide(ident, 4), ALU.subtract).then_inc(nt_ready, 1)
                    for e in range(2):
                        copied(pool, ("prod", c, g, 2, e))
                    pool.tensor_tensor(mx[:, hs], mx[:, hs], wide(ident, 4), ALU.add).then_inc(x1_ready, 1)

            add_identity(0)
            copied(pool, ("kt",))
            pool.memset(pu[:, :, 0:PAD], 0.0).then_inc(pad_ready, 1)
            pool.memset(pt1[:, 0:PAD], 0.0).then_inc(pad_ready, 1)
            pool.memset(pt2[:, 0:PAD], 0.0).then_inc(pad_ready, 1)
            pool.wait_ge(pad_ready, 3)
            steps = 0
            for g, w in enumerate(WINDOWS):
                copied(pool, ("unit", S_POOL + g // 2))
                src, s = pu[:, g], 1
                while s < w:
                    dst = (pt1, pt2)[s.bit_length() % 2]
                    pool.tensor_tensor(dst[:, PAD:], src[:, PAD:], src[:, PAD - s:PAD + T - s], ALU.add).then_inc(pool_step, 1)
                    steps += 1
                    pool.wait_ge(pool_step, steps)
                    src, s = dst, 2 * s
                pool.tensor_tensor(pd[:, 0:PAD], src[:, PAD:2 * PAD], cst[:, C_INV + PAD * g:C_INV + PAD * g + PAD], ALU.mult)\
                    .then_inc(pool_step, 1)
                pool.tensor_scalar(pd[:, PAD:T], src[:, 2 * PAD:], 1.0 / w, None, ALU.mult).then_inc(pool_step, 1)
                steps += 2
                pool.wait_ge(pool_step, steps)
                pool.tensor_tensor(pu[:, g, PAD:], pd, pu[:, g, PAD:], ALU.subtract).then_inc(pd_ready, 1)
                pool.wait_ge(pd_ready, g + 1)
            add_identity(1)
            for ch in range(2):
                for n in (1, 2):
                    for tt in range(TT):
                        copied(pool, ("unit", S_BR + 2 * (n - 1) + ch, tt))
                pool.tensor_tensor(gates[2 + ch], gates[2 + ch], gates[4 + ch], ALU.add).then_inc(sum_ready, 1)


def shape_constants():
    c = np.zeros((P, C_ALL), np.float32)
    t, s = np.arange(P)[:, None], np.arange(P)[None, :]
    c[:, C_ID:C_ID + P] = t == s
    c[:, C_BLK:C_BLK + P] = t // HD == s // HD
    j = np.arange(129)[None, :]
    c[:, C_CUM:C_CUM + 129] = -np.exp(-0.5) * ((t < j).astype(np.float64) - (t < 64))
    c[:, C_BIAS:C_BIAS + P] = np.where(s <= t, s - t, -1e30)
    s2 = np.arange(T)[None, :]
    c[:, C_BIAS + P:C_BIAS + P + T] = np.where(s2 <= t + P, s2 - t - P, -1e30)
    c[:, C_SI:C_SI + P] = t < s
    c[:, C_SI + P:C_SI + 2 * P] = t <= s
    for l in range(LEVELS):
        b = 2 << l
        c[:, C_LEV + P * l:C_LEV + P * l + P] = ((t // b % 2 == 1) & (s // b == t // b - 1)).astype(np.float32) - (t == s)
    c[:, C_M1:C_M1 + P] = (t % 2 == 1) & (s == t - 1)
    c[:, C_M1T:C_M1T + P] = ((s % 2 == 1) & (t == s - 1)).astype(np.float32) - (t == s)
    for g, w in enumerate(WINDOWS):
        c[:, C_INV + PAD * g:C_INV + PAD * g + PAD] = 1.0 / np.minimum(np.arange(PAD) + 1, w)
    return c


def channel_columns(shift_mu, a0, k_k, k_a, r_k, lnx_g, lnx_b, pool_scale, norm1_g, norm2_g, qn_g, kn_g):
    rows = [a.reshape(-1, P) for a in (shift_mu, a0, k_k, k_a, r_k, lnx_g, lnx_b, pool_scale, norm1_g, norm2_g)]
    rows += [np.concatenate([a, a], axis=1) for a in (qn_g, kn_g)]
    return np.ascontiguousarray(np.concatenate(rows, axis=0).T)


_WEIGHTS = ["x", "w_in", "w_up", "w0", "a_up", "g_up", "pool_w", "w_branch", "w_out", "w_ff1", "w_ff2"]


def kernel(**inputs):
    import concourse.bacc as _bacc
    from concourse.bass_utils import run_bass_kernel_spmd as _run

    a = {k: np.ascontiguousarray(v) for k, v in inputs.items()}
    arrays = {f"in_{k}": a[k] for k in _WEIGHTS}
    arrays["in_vecs"] = channel_columns(*(a[k] for k in (
        "shift_mu", "a0", "k_k", "k_a", "r_k", "lnx_g", "lnx_b", "pool_scale", "norm1_g", "norm2_g", "qn_g", "kn_g")))
    arrays["in_consts"] = shape_constants()
    nc = _bacc.Bacc("TRN2", target_bir_lowering=False, num_devices=1)
    args = [nc.dram_tensor(n, v.shape, mybir.dt.from_np(v.dtype), kind="ExternalInput").ap() for n, v in arrays.items()]
    args.append(nc.dram_tensor("out_0", (1, T, D), F32, kind="ExternalOutput").ap())
    build_layer(nc, *args)
    r = _run(nc, [arrays], core_ids=[0])
    return r.results[0]["out_0"]
```

```python
from contextlib import ExitStack

import numpy as np

import concourse.bass as bass
from concourse import mybir

F32 = mybir.dt.float32
F32R = mybir.dt.float32r
ALU = mybir.AluOpType
ACT = mybir.ActivationFunctionType
AX_X = mybir.AxisListType.X

P = 128
T, D = 256, 1024
TT = T // P
KD = D // P
HEADS, HD = 8, 64
W = HEADS * HD
PAIRS = HEADS // 2
N_RWKV, N_ATTN, N_POOL = 3 * W + 256, 3 * W, W
D_FF = 4 * D
RMS_EPS, GN_EPS = 1e-6, 64e-5
WINDOWS = (2, 4, 8, 16)
PAD = 16
LEVELS = 5
SLOPES = [2.0 ** (-8.0 * (h + 1) / HEADS) for h in range(HEADS)]

C_ID, C_BLK, C_CUM, C_BIAS = 0, 128, 256, 386
C_SDI = C_BIAS + 384
C_SI = C_SDI + 256
C_LEV = C_SI + 256
C_M1 = C_LEV + LEVELS * HD
C_IDC = C_M1 + HD
C_M1T = C_IDC + HD
C_INV = C_M1T + 128
C_ALL = C_INV + 4 * 16
V_MU, V_A0, V_KK, V_KA, V_RK, V_LG, V_LB, V_PS, V_G1, V_G2, V_QN, V_KN = 0, 14, 18, 22, 26, 30, 34, 38, 42, 50, 58, 59
V_ALL = 60

UNITS = [("feat", c) for c in (3 * W, W, W + 256, 0, 256, 2 * W, 2 * W + 256)]
UNITS += [("feat", N_RWKV + c) for c in (0, 256, W, W + 256)]
UNITS += [("tok", N_RWKV + 2 * W, kh) for kh in range(2)]
UNITS += [("feat", N_RWKV + N_ATTN + c) for c in (0, 256)]
UNITS += [("tok", N_RWKV + N_ATTN + N_POOL + 512 * p, kh) for p in range(6) for kh in range(2)]
UNITS += [("branch", n, ch) for n in (1, 2, 0) for ch in range(2)]
UNITS += [("out", kh, ch) for kh in range(2) for ch in range(2)]
UNITS += [("ff1", 0)]
for i in range(1, D_FF // 256):
    UNITS += [("ff1", i), ("ff2", i - 1)]
UNITS += [("ff2", D_FF // 256 - 1)]
SLOTS = len(UNITS)
PIECES = 2 * SLOTS
STAGES = 3
RING = 5
AHEAD = 4
S_QK, S_VA, S_POOL, S_GATE, S_BR, S_OUT = 7, 11, 13, 15, 27, 33
S_FF = 37
S_PROD, S_LEV, S_APPLY, S_GN = (8, 17), (10, 19), (16, 25), (18, 27)
S_HEAD = 13
S_PY = 22


def level_places(t):
    for c in range(TT):
        if S_LEV[c] <= t <= S_LEV[c] + LEVELS:
            return c, t - S_LEV[c]
    return None


def product_place(t, p):
    for c in range(TT):
        n = 4 * (t - S_PROD[c]) + p
        if 0 <= n < 6:
            return c, n // 3, n % 3
    return None


def plan_turns():
    turn, count, signalled, ring = {}, [0] * 8, [0] * 8, [0]

    def use(name, bank=None, dense=False):
        if bank is None:
            bank = 4 + ring[0] % 4
            ring[0] += 1
        turn[name] = (bank, count[bank], signalled[bank])
        count[bank] += 1
        signalled[bank] += not dense

    for i in range(4):
        use(("x", i))
    for t, u in enumerate(UNITS):
        for p in range(4):
            if p == 0:
                if u[0] == "feat":
                    use(("unit", t), t % 2, dense=True)
                elif u[0] == "tok" and u[2] == 0:
                    use(("tok", u[1], 0), 0, dense=True)
                    use(("tok", u[1], 1), 1, dense=True)
                elif u[0] == "branch":
                    b = 2 * ((t - S_BR) % 2)
                    use(("unit", t, 0), b, dense=True)
                    use(("unit", t, 1), b + 1, dense=True)
                elif u[0] == "out" and u[1] == 0:
                    for tt in range(TT):
                        use(("out", u[2], tt), 2 * u[2] + tt, dense=True)
                elif u[0] == "ff1":
                    use(("ff", u[1]), dense=True)
                elif u == ("ff2", 0):
                    for b in range(4):
                        use(("mlp", b // 2, b % 2), b)
            for n in pe_uses(t, p):
                use(*n)
    return turn


def pe_uses(t, p):
    if (t, p) == (1, 3):
        return [(("z", 0),), (("z", 1),), (("a", 0),), (("a", 1),)]
    if (t, p) == (2, 3):
        return [(("cum", 0, 0),), (("cum", 0, 1),)]
    if (t, p) == (3, 1):
        return [(("cum", 1, 0),), (("cum", 1, 1),)]
    if (t, p) == (3, 3):
        return [(("kk",),)]
    if (t, p) == (4, 1):
        return [(("kb", 0),), (("kb", 1),)]
    if (t, p) == (4, 3):
        return [(("g", 0),), (("g", 1),)]
    if (t, p) == (7, 1):
        return [(("vt", 0),), (("vt", 1),)]
    if (t, p) == (7, 3):
        return [(("bonus", 0),), (("bonus", 1),)]
    out = []
    if S_QK < t <= S_QK + 4 and p == 3:
        out.append((("ss", t - 1 - S_QK), 2))
    if S_QK + 1 < t <= S_QK + 5 and p == 1:
        out.append((("qb", t - 2 - S_QK), 3))
    if product_place(t, p):
        out += [(("prod", *product_place(t, p), e),) for e in range(2)]
    if (t, p) == (9, 2):
        out += [(("bt",),), (("kt",),)]
    if level_places(t):
        c, l = level_places(t)
        if p == 0:
            out += [(("Y", c, l),)]
        if p == 2 and l < LEVELS:
            out += [(("X", c, l),)]
        if p == 2:
            out += [(("XT", c, l),)]
    if t in S_APPLY:
        c = S_APPLY.index(t)
        if p == 0:
            out += [(("rhs", c, e),) for e in range(2)]
        if p == 1:
            out += [(("sa", c),)]
        if p == 2:
            out += [(("o", c, e),) for e in range(2)]
        if p == 3 and c == 0:
            out += [(("state",),)]
    if (t, p) in ((S_GN[0], 3), (S_GN[1], 0)):
        out += [(("ot", S_GN.index(t)),)]
    if S_HEAD <= t <= S_HEAD + HEADS:
        h = t - S_HEAD
        if p == 0 and h >= 1:
            out += [(("pt", h - 1), 3)]
        if p == 1 and h < HEADS:
            out += [(("score", h), 2)]
        if p == 3 and h >= 1:
            out += [(("pv", h - 1), 3)]
    if t == S_PY and p in (0, 2):
        out += [(("pool", p // 2), 2 + p // 2)]
    if (t, p) == (S_OUT - 1, 3):
        out += [(("m", 0),), (("m", 1),)]
    if (t, p) == (S_OUT, 3):
        out += [(("m", 2),), (("m", 3),)]
    if t == S_FF - 1 and p in (1, 3):
        out += [(("h2", p - 1 + i),) for i in range(2)]
    return out


def dense_ends():
    ends = {}
    for t, u in enumerate(UNITS):
        if u[0] == "feat":
            ends[("unit", t)] = 2 * t + 2
        for tt in range(TT):
            if u[0] == "tok" and u[2] == 1:
                ends[("tok", u[1], tt)] = 2 * t + 2
            if u[0] == "branch":
                ends[("unit", t, tt)] = 2 * t + 2
            if u[0] == "out" and u[1] == 1:
                ends[("out", u[2], tt)] = 2 * t + 2
        if u[0] == "ff1":
            ends[("ff", u[1])] = 2 * t + 2
    return ends


DENSE_END = dense_ends()


def build_layer(nc: bass.Bass, x, w_in, w_up, w0, a_up, g_up, pool_w, w_branch, w_out, w_ff1, w_ff2, vecs, consts, out):
    turn = plan_turns()
    ctx = ExitStack()
    with ctx:
        def sb(name, shape, dt=F32):
            return ctx.enter_context(nc.sbuf_tensor(name, shape, dt))

        def sem(name):
            return ctx.enter_context(nc.semaphore(name))

        stage = sb("stage", [P, STAGES, 1024])
        w_hi = sb("w_hi", [P, RING, 1024], F32R)
        w_lo = sb("w_lo", [P, RING, 1024], F32R)
        h_hi = sb("h_hi", [P, KD, T], F32R)
        h_lo = sb("h_lo", [P, KD, T], F32R)
        y_hi = sb("y_hi", [P, KD, T], F32R)
        y_lo = sb("y_lo", [P, KD, T], F32R)
        r_hi = sb("r_hi", [P, 4, T], F32R)
        r_lo = sb("r_lo", [P, 4, T], F32R)
        xs = sb("xs", [P, TT, D])
        cst = sb("cst", [P, C_ALL])
        vec = sb("vec", [P, V_ALL])
        big = sb("big", [P, 6, 1024])
        mat = sb("mat", [P, 7680])
        lora = sb("lora", [P, 3, 512])
        pool_sb = sb("pool_sb", [P, 4, P])
        vmix = sb("vmix", [P, PAIRS, T])
        lmix = sb("lmix", [P, 2, T])
        tsg = sb("tsg", [P, 2, T])
        gg = sb("gg", [P, PAIRS, T])
        ops = sb("ops", [P, 4096])
        vtok = sb("vtok", [P, TT, W])
        s_in = sb("s_in", [P, PAIRS, HD])
        att = sb("att", [P, 1024])
        small = sb("small", [P, 96])

        ident = cst[:, C_ID:C_ID + P]
        blk = cst[:, C_BLK:C_BLK + P]
        gates = [big[:, p].rearrange("p (t n) -> p t n", t=TT) for p in range(6)]
        q4 = lambda v: v.rearrange("p (j t) -> p j t", j=PAIRS)
        rmix, kmix = q4(big[:, 0]), q4(big[:, 1])
        btok, ktok = big[:, 2, 0:512], big[:, 2, 512:1024]
        qraw, kraw = q4(big[:, 3]), q4(big[:, 4])
        vatt = big[:, 5].rearrange("p (t n) -> p t n", t=TT)
        sg = big[:, 2].rearrange("p (t n) -> p t n", t=TT)
        xn = big[:, 4:6]
        flat = mat[:]
        a_s, kkn, k2, ksq = (q4(flat[:, 1024 * i:1024 * i + 1024]) for i in range(4))
        e_up, e_dn = (flat[:, 4096 + 1040 * i:4096 + 1040 * i + 1032].rearrange("p (c j t) -> p c j t", c=TT, j=PAIRS)
                      for i in range(2))
        gm = flat[:, 0:4096].rearrange("p (h a s) -> p h a s", h=HEADS, a=4)
        y_e, xt_e = (flat[:, o:o + 1024].rearrange("p (h s) -> p h s", h=HEADS) for o in (4096, 5120))
        x_c, y_c, xt_c = (flat[:, o:o + 512].rearrange("p (h s) -> p h s", h=HEADS) for o in (6144, 6656, 7168))
        opv = ops[:].rearrange("p (c z) -> p c z", c=TT)
        bk = [opv[:, c, 0:1024].rearrange("p (a j t) -> p a j t", a=2, j=PAIRS) for c in range(TT)]
        ar = [opv[:, c, 1024:2048].rearrange("p (j a t) -> p j a t", j=PAIRS, a=2) for c in range(TT)]
        pu = ops[:, 0:4 * (PAD + T)].rearrange("p (g t) -> p g t", g=4)
        pt1, pt2 = (ops[:, 1088 + 272 * i:1088 + 272 * i + 272] for i in range(2))
        pd = ops[:, 1632:1632 + 256]
        corner = lora[0:HD, 0].rearrange("p (h s) -> p h s", h=HEADS)
        th, sgx = tsg[:, 0], tsg[:, 1]
        osq = tsg[:].rearrange("p a t -> p (a t)")
        rhs_sb, sa_sb = (lora[:, i].rearrange("p (h v) -> p h v", h=HEADS) for i in range(2))
        oc = lora[:, 2]
        o_sb = oc.rearrange("p (h v) -> p h v", h=HEADS)
        ytmp = lmix[:].rearrange("p a t -> p (a t)").rearrange("p (j t) -> p j t", j=PAIRS)
        sq_att = [att[:, 512 * i:512 * i + 512] for i in range(2)]
        prob, prob_t = att[:, 0:384], att[:, 512:896]
        ffs, fsq = ([flat[:, 512 * i + o:512 * i + o + 512] for i in range(2)] for o in (0, 1024))
        omu, oka, gq8 = small[:, 0:14], small[:, 14:18], small[:, 18:19]
        ss1, rs1, ss2, r2, nmax, psm = (small[:, 20 + 2 * i:22 + 2 * i] for i in range(6))
        gsum, gvar = small[:, 32:40], small[:, 40:48]
        e_end, minus_half = small[:, 48:52], small[:, 52:53]
        kk_tok = small[:, 56:72].rearrange("p (c h) -> p c h", c=TT)
        qk_tok = [small[:, 72 + 8 * i:80 + 8 * i].rearrange("p (c h) -> p c h", c=TT) for i in range(2)]

        kkb = flat[:, 3072:4096].rearrange("p (c n) -> p c n", c=TT)

        def col(i):
            return vec[:, i:i + 1]

        def by_channel(ap):
            return ap.unsqueeze(3).to_broadcast([P, ap.shape[1], ap.shape[2], HD])

        def wide(ap, n):
            return ap.unsqueeze(1).to_broadcast([ap.shape[0], n, ap.shape[1]])

        banks = [ctx.enter_context(nc.psum_tensor(f"bank{i}", [P, 512], F32)) for i in range(8)]
        full = [sem(f"full{i}") for i in range(8)]
        drained = [sem(f"drained{i}") for i in range(8)]

        def ps(name):
            return banks[turn[name][0]]

        def full_of(name):
            return full[turn[name][0]]

        def drained_of(name):
            return drained[turn[name][0]]

        def room(eng, name):
            b, before, _ = turn[name]
            if before:
                eng.wait_ge(drained[b], before)
            return banks[b]

        def take(eng, name):
            b, _, before = turn[name]
            if name in DENSE_END:
                eng.wait_ge(used, DENSE_END[name])
            else:
                eng.wait_ge(full[b], before + 1)
            return banks[b]

        def copied(eng, name):
            b, before, _ = turn[name]
            eng.wait_ge(drained[b], before + 1)

        x_in, cst_in, small_in = sem("x_in"), sem("cst_in"), sem("small_in")
        loaded = [sem(f"loaded{i}") for i in range(STAGES)]
        hi_done, lo_done = sem("hi_done"), sem("lo_done")
        used = sem("used")
        consts_ready = sem("consts_ready")
        ones_ready = sem("ones_ready")
        ss_ready, ms_ready, rs_ready, xn_ready = (
            sem(n) for n in ("ss_ready", "ms_ready", "rs_ready", "xn_ready"))
        h_hi_done = sem("h_hi_done")
        keep_part = sem("keep_part")
        lora_ready = sem("lora_ready")
        kkraw_ready, ksq_ready, kk_inv, qk_inv, kkb_ready, qkb_ready = (
            sem(n) for n in ("kkraw_ready", "ksq_ready", "kk_inv", "qk_inv", "kkb_ready", "qkb_ready"))
        own = sem("own")
        rk_ready, ops_ready = sem("rk_ready"), sem("ops_ready")
        nt_ready, x1_ready, xte_ready, xt1_ready, y_zero = (
            sem(n) for n in ("nt_ready", "x1_ready", "xte_ready", "xt1_ready", "y_zero"))
        oc_ready, osq_ready, gvar_ready, groot_ready, on_ready, yr_pre, yr_hi_done, yr_ready = (
            sem(n) for n in ("oc_ready", "osq_ready", "gvar_ready", "groot_ready", "on_ready", "yr_pre", "yr_hi_done",
                             "yr_ready"))
        neg_ready, exps_ready, p_ready = sem("neg_ready"), sem("exps_ready"), sem("p_ready")
        ya_hi = sem("ya_hi")
        pad_ready, pool_step, pd_ready, yp_hi = (sem(n) for n in ("pad_ready", "pool_step", "pd_ready", "yp_hi"))
        sum_ready, m_pre, m_hi = sem("sum_ready"), sem("m_pre"), sem("m_hi")
        ss2_ready, h2_hi = sem("ss2_ready"), sem("h2_hi")
        f_hi, f_ready = sem("f_hi"), sem("f_ready")
        fin_ready, stored = sem("fin_ready"), sem("stored")

        block = ctx.enter_context(nc.Block())

        def piece_view(buf, v, slots=RING):
            kind = UNITS[v // 2][0]
            k = {"feat": KD, "ff1": KD, "ff2": 1}.get(kind, 2)
            return buf[:, v % slots].rearrange("p (k n) -> p k n", k=k)

        def piece_dram(v):
            u, half = UNITS[v // 2], v % 2
            if u[0] == "feat":
                return w_in[0, :, u[1] + P * half:u[1] + P * half + P].rearrange("(k p) n -> p k n", p=P)
            if u[0] == "ff1":
                c = 256 * u[1] + P * half
                return w_ff1[0, :, c:c + P].rearrange("(k p) n -> p k n", p=P)
            if u[0] == "ff2":
                r = 256 * u[1] + P * half
                return w_ff2[0, r:r + P, :].rearrange("(k p) n -> p k n", p=P)
            if u[0] == "tok":
                r, m, c = 512 * u[2] + 256 * half, w_in[0], u[1]
            elif u[0] == "branch":
                r, m, c = 256 * half, w_branch[0, u[1]], 512 * u[2]
            else:
                r, m, c = 512 * u[1] + 256 * half, w_out[0], 512 * u[2]
            return m[r:r + 256, c:c + 512].rearrange("(k p) n -> p k n", p=P)

        def mix_tile(t, j):
            return UNITS[t][1] // P + j

        def mix_dst(t, j):
            m = mix_tile(t, j)
            return (rmix, kmix, vmix, lmix)[m // 4][:, m % 4]

        @block.sync
        def _(sp):
            for tt in range(TT):
                sp.dma_start(xs[:, tt], x[0, P * tt:P * tt + P, :]).then_inc(x_in, 16)
            sp.dma_start(vec[:], vecs).then_inc(cst_in, 16)
            sp.dma_start(cst[:], consts).then_inc(cst_in, 16)
            for v in range(PIECES):
                if v >= STAGES:
                    sp.wait_ge(lo_done, v - STAGES + 1)
                sp.dma_start(piece_view(stage, v, STAGES), piece_dram(v)).then_inc(loaded[v % STAGES], 16)
                if v == 1:
                    sp.dma_start(lora[0:64, 0], w_up[0]).then_inc(small_in, 16)
                    sp.dma_start(lora[64:65, 0], w0).then_inc(small_in, 16)
                    sp.dma_start(lora[64:128, 1], a_up[0]).then_inc(small_in, 16)
                    sp.dma_start(lora[:, 2], g_up[0]).then_inc(small_in, 16)
                    sp.dma_start(pool_sb[:], pool_w[0].rearrange("g c d -> c g d")).then_inc(small_in, 16)
            for n in range(4):
                sp.wait_ge(fin_ready, n + 1)
                tt, c = n // 2, n % 2
                sp.dma_start(out[0, P * tt:P * tt + P, 512 * c:512 * c + 512],
                             xs[:, tt, 512 * c:512 * c + 512]).then_inc(stored, 16)
            sp.wait_ge(stored, 64)

        @block.tensor
        def _(pe):
            def mm3(o, lh, ll, rh, rl, first, last):
                pe.matmul(o, lh, rh, start=first, stop=False)
                pe.matmul(o, lh, rl, start=False, stop=False)
                return pe.matmul(o, ll, rh, start=False, stop=last)

            def part(t, p):
                u, v = UNITS[t], 2 * t + p // 2
                if p % 2 == 0:
                    pe.wait_ge(lo_done, v + 1)
                wh, wl = piece_view(w_hi, v), piece_view(w_lo, v)
                i = p % 2
                if u[0] in ("feat", "ff1"):
                    name = ("unit", t) if u[0] == "feat" else ("ff", u[1])
                    if p == 0:
                        o = room(pe, name)
                    else:
                        o = ps(name)
                    j = p // 2
                    for k in range(4 * i, 4 * i + 4):
                        if p < 2 and k % 2 == 0 and (t == 0 or u == ("ff1", 0)):
                            copied(pe, ("h2" if t else "x", k // 2))
                        ins = mm3(o[:, T * j:T * j + T], wh[:, k], wl[:, k], h_hi[:, k], h_lo[:, k], k == 0, k == 7)
                elif u[0] == "ff2":
                    kt, buf = p // 2, 2 * (u[1] % 2)
                    if p == 0:
                        pe.wait_ge(f_ready, u[1] + 1)
                    for c in range(2):
                        name = ("mlp", i, c)
                        if u[1] == 0 and kt == 0:
                            room(pe, name)
                        ins = mm3(ps(name)[:], r_hi[:, buf + kt, P * i:P * i + P], r_lo[:, buf + kt, P * i:P * i + P],
                                  wh[:, 0, 512 * c:512 * c + 512], wl[:, 0, 512 * c:512 * c + 512],
                                  u[1] == 0 and kt == 0, u == UNITS[-1] and kt == 1)
                        if u == UNITS[-1] and kt == 1 and (i, c) != (1, 1):
                            ins.then_inc(full_of(name), 1)
                else:
                    if u[0] == "tok":
                        name, lh, ll, k0 = ("tok", u[1], i), h_hi, h_lo, 4 * u[2]
                        first, last = u[2] == 0, u[2] == 1
                    elif u[0] == "branch":
                        name, first, last = ("unit", t, i), True, True
                        lh, ll, k0 = {1: (y_hi, y_lo, 0), 2: (y_hi, y_lo, 4), 0: (r_hi, r_lo, 0)}[u[1]]
                        if p == 0:
                            if u[1] == 1:
                                copied(pe, ("pv", HEADS - 2))
                                copied(pe, ("pv", HEADS - 1))
                            elif u[1] == 2:
                                copied(pe, ("pool", 0))
                                copied(pe, ("pool", 1))
                            else:
                                pe.wait_ge(yr_ready, TT)
                    else:
                        name, lh, ll, k0 = ("out", u[2], i), y_hi, y_lo, 4 * u[1]
                        first, last = u[1] == 0, u[1] == 1
                        if p == 0:
                            copied(pe, ("m", 2 * u[1]))
                            copied(pe, ("m", 2 * u[1] + 1))
                    o = room(pe, name) if first and p < 2 else ps(name)
                    for kk in range(2):
                        k = 2 * (p // 2) + kk
                        ins = mm3(o[:], lh[:, k0 + k, P * i:P * i + P], ll[:, k0 + k, P * i:P * i + P],
                                  wh[:, kk], wl[:, kk], first and k == 0, last and k == 3)
                if p % 2:
                    ins.then_inc(used, 1)

            pe.wait_ge(cst_in, 32)
            pe.wait_ge(xn_ready, 2)
            for i in range(4):
                o = room(pe, ("x", i))
                for kk in range(2):
                    for tt in range(TT):
                        k = 2 * i + kk
                        ins = pe.transpose(o[:, T * kk + P * tt:T * kk + P * tt + P], xn[:, tt, P * k:P * k + P], ident)
                ins.then_inc(full_of(("x", i)), 1)

            def products(c, g, kind):
                if kind == 0 and g == 0:
                    pe.wait_ge(ops_ready, 1)
                for e in range(2):
                    name = ("prod", c, g, kind, e)
                    o = room(pe, name)
                    rows = slice(HD * e, HD * e + HD)
                    for i in range(2):
                        j = 2 * g + i
                        if kind < 2:
                            ins = pe.matmul(o[:, 256 * i:256 * i + 256], bk[c][rows, kind, j], ar[c][rows, j],
                                            start=True, stop=True)
                        else:
                            ins = pe.matmul(o[:, P * i:P * i + P], ar[c][rows, j, 0], bk[c][rows, 0, j],
                                            start=True, stop=True)
                    ins.then_inc(full_of(name), 1)

            def extra(t, p):
                if (t, p) == (1, 3):
                    pe.wait_ge(small_in, 80)
                    pe.wait_ge(ones_ready, 1)
                    pe.wait_ge(lora_ready, 1)
                    for c in range(TT):
                        o = room(pe, ("z", c))
                        pe.matmul(o[:], th[0:65, P * c:P * c + P], lora[0:65, 0], start=True, stop=True)\
                          .then_inc(full_of(("z", c)), 1)
                    for i in range(2):
                        o = room(pe, ("a", i))
                        for jj in range(2):
                            j = 2 * i + jj
                            ins = pe.matmul(o[:, T * jj:T * jj + T], lora[64:128, 1, P * j:P * j + P], lmix[64:128, 0],
                                            start=True, stop=True)
                        ins.then_inc(full_of(("a", i)), 1)
                if (t, p) in ((2, 3), (3, 1)):
                    c = t - 2
                    copied(pe, ("z", c))
                    for i in range(2):
                        o = room(pe, ("cum", c, i))
                        for jj in range(2):
                            j = 2 * i + jj
                            ins = pe.matmul(o[:, 256 * jj:256 * jj + 129], sg[:, c, P * j:P * j + P],
                                            cst[:, C_CUM:C_CUM + 129], start=True, stop=True)
                        ins.then_inc(full_of(("cum", c, i)), 1)
                if (t, p) == (3, 3):
                    pe.wait_ge(ksq_ready, 1)
                    o = room(pe, ("kk",))
                    for c in range(TT):
                        for j in range(PAIRS):
                            ins = pe.matmul(o[:, 8 * c + 2 * j:8 * c + 2 * j + 2], ksq[:, j, P * c:P * c + P],
                                            cst[:, C_BLK:C_BLK + P:HD], start=True, stop=True)
                    ins.then_inc(full_of(("kk",)), 1)
                if (t, p) == (4, 1):
                    pe.wait_ge(kkb_ready, 1)
                    for i in range(2):
                        o = room(pe, ("kb", i))
                        for jj in range(2):
                            for c in range(TT):
                                j = 2 * i + jj
                                ins = pe.transpose(o[:, T * jj + P * c:T * jj + P * c + P],
                                                   kkb[:, c, P * j:P * j + P], ident)
                        ins.then_inc(full_of(("kb", i)), 1)
                if (t, p) == (4, 3):
                    pe.wait_ge(lora_ready, 2)
                    for i in range(2):
                        o = room(pe, ("g", i))
                        for jj in range(2):
                            j = 2 * i + jj
                            ins = pe.matmul(o[:, T * jj:T * jj + T], lora[:, 2, P * j:P * j + P], sgx,
                                            start=True, stop=True)
                        ins.then_inc(full_of(("g", i)), 1)
                if (t, p) == (7, 1):
                    copied(pe, ("unit", 5))
                    copied(pe, ("unit", 6))
                    for c in range(TT):
                        o = room(pe, ("vt", c))
                        for j in range(PAIRS):
                            ins = pe.transpose(o[:, P * j:P * j + P], vmix[:, j, P * c:P * c + P], ident)
                        ins.then_inc(full_of(("vt", c)), 1)
                if (t, p) == (7, 3):
                    pe.wait_ge(rk_ready, 1)
                    for i in range(2):
                        o = room(pe, ("bonus", i))
                        pe.matmul(o[:], blk, ksq[:, 2 * i:2 * i + 2].rearrange("p j t -> p (j t)"),
                                  start=True, stop=True).then_inc(full_of(("bonus", i)), 1)
                if S_QK < t <= S_QK + 4 and p == 3:
                    n = t - 1 - S_QK
                    copied(pe, ("unit", t - 1))
                    o = room(pe, ("ss", n))
                    for c in range(TT):
                        for jj in range(2):
                            ins = pe.matmul(o[:, 4 * c + 2 * jj:4 * c + 2 * jj + 2],
                                            sq_att[n % 2][:, T * jj + P * c:T * jj + P * c + P],
                                            cst[:, C_BLK:C_BLK + P:HD], start=True, stop=True)
                    ins.then_inc(full_of(("ss", n)), 1)
                if S_QK + 1 < t <= S_QK + 5 and p == 1:
                    n = t - 2 - S_QK
                    pe.wait_ge(qkb_ready, n + 1)
                    o = room(pe, ("qb", n))
                    for jj in range(2):
                        for c in range(TT):
                            ins = pe.transpose(o[:, T * jj + P * c:T * jj + P * c + P],
                                               sq_att[n % 2][:, 256 * c + P * jj:256 * c + P * jj + P], ident)
                    ins.then_inc(full_of(("qb", n)), 1)
                if product_place(t, p):
                    products(*product_place(t, p))
                if (t, p) == (9, 2):
                    for a, name in ((0, ("bt",)), (1, ("kt",))):
                        o = room(pe, name)
                        for j in range(PAIRS):
                            ins = pe.transpose(o[:, P * j:P * j + P], bk[0][:, a, j], ident)
                        ins.then_inc(full_of(name), 1)
                if level_places(t) and p == 0:
                    c, l = level_places(t)
                    if l == 0:
                        pe.wait_ge(nt_ready, 2 * c + 2)
                        pe.wait_ge(x1_ready, c + 1)
                    else:
                        copied(pe, ("X", c, l - 1))
                    o = room(pe, ("Y", c, l))
                    for h in range(HEADS):
                        if l < LEVELS:
                            ins = pe.matmul(o[:, HD * h:HD * h + HD], gm[:, h, 0], x_c[:, h], start=True, stop=True)
                        else:
                            ins = pe.matmul(o[HD:P, HD * h:HD * h + HD], corner[:, h], x_c[0:HD, h], start=True, stop=True)
                    ins.then_inc(full_of(("Y", c, l)), 1)
                if level_places(t) and p == 2:
                    c, l = level_places(t)
                    if l == 0:
                        pe.wait_ge(xt1_ready, 2 * c + 2)
                    else:
                        copied(pe, ("XT", c, l - 1))
                    copied(pe, ("Y", c, l))
                    if l < LEVELS:
                        o = room(pe, ("X", c, l))
                        for h in range(HEADS):
                            ins = pe.matmul(o[:, HD * h:HD * h + HD], xt_e[:, h], y_c[:, h], start=True, stop=True)
                        ins.then_inc(full_of(("X", c, l)), 1)
                    o = room(pe, ("XT", c, l))
                    for h in range(HEADS):
                        if l < LEVELS:
                            ins = pe.matmul(o[:, HD * h:HD * h + HD], y_e[:, h], xt_c[:, h], start=True, stop=True)
                        else:
                            ins = pe.matmul(o[0:HD, HD * h:HD * h + HD], y_c[HD:P, h], xt_c[HD:P, h], start=True, stop=True)
                    ins.then_inc(full_of(("XT", c, l)), 1)
                if t in S_APPLY:
                    c = S_APPLY.index(t)
                    if p == 0:
                        for g in range(2):
                            for e in range(2):
                                copied(pe, ("prod", c, g, 1, e))
                        copied(pe, ("vt", c))
                        if c == 1:
                            copied(pe, ("state",))
                        for e in range(2):
                            o = room(pe, ("rhs", c, e))
                            rows = slice(HD * e, HD * e + HD)
                            for j in range(PAIRS):
                                h = 2 * j + e
                                ins = pe.matmul(o[:, HD * j:HD * j + HD], gm[:, h, 2], vtok[:, c, HD * h:HD * h + HD],
                                                start=True, stop=c == 0)
                                if c == 1:
                                    ins = pe.matmul(o[:, HD * j:HD * j + HD], ar[c][rows, j, 0], s_in[rows, j],
                                                    start=False, stop=True)
                            ins.then_inc(full_of(("rhs", c, e)), 1)
                    if p == 1:
                        for e in range(2):
                            copied(pe, ("rhs", c, e))
                        copied(pe, ("XT", c, LEVELS))
                        o = room(pe, ("sa", c))
                        for h in range(HEADS):
                            ins = pe.matmul(o[:, HD * h:HD * h + HD], xt_e[:, h], rhs_sb[:, h], start=True, stop=True)
                        ins.then_inc(full_of(("sa", c)), 1)
                    if p == 2:
                        copied(pe, ("sa", c))
                        for e in range(2):
                            o = room(pe, ("o", c, e))
                            rows = slice(HD * e, HD * e + HD)
                            for j in range(PAIRS):
                                h = 2 * j + e
                                oo = o[:, HD * j:HD * j + HD]
                                pe.matmul(oo, gm[:, h, 1], sa_sb[:, h], start=True, stop=False)
                                ins = pe.matmul(oo, gm[:, h, 3], vtok[:, c, HD * h:HD * h + HD],
                                                start=False, stop=c == 0)
                                if c == 1:
                                    ins = pe.matmul(oo, ar[c][rows, j, 1], s_in[rows, j], start=False, stop=True)
                            ins.then_inc(full_of(("o", c, e)), 1)
                    if p == 3 and c == 0:
                        copied(pe, ("bt",))
                        copied(pe, ("kt",))
                        o = room(pe, ("state",))
                        for h in range(HEADS):
                            j, e = h // 2, h % 2
                            oo = o[HD * e:HD * e + HD, HD * j:HD * j + HD]
                            pe.matmul(oo, btok[:, HD * h:HD * h + HD], sa_sb[:, h], start=True, stop=False)
                            ins = pe.matmul(oo, ktok[:, HD * h:HD * h + HD], vtok[:, 0, HD * h:HD * h + HD],
                                            start=False, stop=True)
                        ins.then_inc(full_of(("state",)), 1)
                if (t, p) in ((S_GN[0], 3), (S_GN[1], 0)):
                    c = S_GN.index(t)
                    pe.wait_ge(on_ready, c + 1)
                    o = room(pe, ("ot", c))
                    for j in range(PAIRS):
                        ins = pe.transpose(o[:, P * j:P * j + P], oc[:, P * j:P * j + P], ident)
                    ins.then_inc(full_of(("ot", c)), 1)
                if S_HEAD <= t <= S_HEAD + HEADS:
                    h = t - S_HEAD
                    if p == 1 and h < HEADS:
                        copied(pe, ("qb", 3))
                        j, rows = h // 2, slice(HD * (h % 2), HD * (h % 2) + HD)
                        o = room(pe, ("score", h))
                        pe.matmul(o[:, 0:P], qraw[rows, j, 0:P], kraw[rows, j, 0:P], start=True, stop=True)
                        pe.matmul(o[:, P:P + T], qraw[rows, j, P:T], kraw[rows, j], start=True, stop=True)\
                          .then_inc(full_of(("score", h)), 1)
                    if p == 0 and h >= 1:
                        pe.wait_ge(p_ready, h)
                        o = room(pe, ("pt", h - 1))
                        for i in range(3):
                            ins = pe.transpose(o[:, P * i:P * i + P], prob[:, P * i:P * i + P], ident)
                        ins.then_inc(full_of(("pt", h - 1)), 1)
                    if p == 3 and h >= 1:
                        n = h - 1
                        copied(pe, ("pt", n))
                        for tt in range(TT):
                            copied(pe, ("tok", N_RWKV + 2 * W, tt))
                        o = room(pe, ("pv", n))
                        rows = slice(HD * (n % 2), HD * (n % 2) + HD)
                        pe.matmul(o[rows, 0:T], vatt[:, 0, HD * n:HD * n + HD], prob_t[:, 0:T], start=True, stop=False)
                        pe.matmul(o[rows, P:T], vatt[:, 1, HD * n:HD * n + HD], prob_t[:, T:T + P],
                                  start=False, stop=True).then_inc(full_of(("pv", n)), 1)
                if t == S_PY and p in (0, 2):
                    i = p // 2
                    pe.wait_ge(pd_ready, 2 * i + 2)
                    o = room(pe, ("pool", i))
                    for gi in range(2):
                        g = 2 * i + gi
                        ins = pe.matmul(o[:, T * gi:T * gi + T], pool_sb[:, g], pu[:, g, PAD:PAD + T],
                                        start=True, stop=True)
                    ins.then_inc(full_of(("pool", i)), 1)
                if (t, p) in ((S_OUT - 1, 3), (S_OUT, 3)):
                    ch = t - S_OUT + 1
                    pe.wait_ge(m_pre, ch + 1)
                    for i in range(2):
                        o = room(pe, ("m", 2 * ch + i))
                        for kk in range(2):
                            for tt in range(TT):
                                k = 2 * i + kk
                                ins = pe.transpose(o[:, T * kk + P * tt:T * kk + P * tt + P],
                                                   gates[ch][:, tt, P * k:P * k + P], ident)
                        ins.then_inc(full_of(("m", 2 * ch + i)), 1)
                if t == S_FF - 1 and p in (1, 3):
                    for i in (p - 1, p):
                        for tt in range(TT):
                            copied(pe, ("out", i // 2, tt))
                        o = room(pe, ("h2", i))
                        for kk in range(2):
                            for tt in range(TT):
                                k = 2 * i + kk
                                ins = pe.transpose(o[:, T * kk + P * tt:T * kk + P * tt + P],
                                                   xs[:, tt, P * k:P * k + P], ident)
                        ins.then_inc(full_of(("h2", i)), 1)

            for t in range(SLOTS):
                for p in range(4):
                    part(t, p)
                    extra(t, p)

        @block.scalar
        def _(act):
            def high(v):
                act.wait_ge(loaded[v % STAGES], 16 * (v // STAGES + 1))
                if v >= RING:
                    act.wait_ge(used, v - RING + 1)
                nc.scalar.copy(w_hi[:, v % RING], stage[:, v % STAGES]).then_inc(hi_done, 1)

            for tt in range(TT):
                act.wait_ge(x_in, 16 * TT)
                nc.scalar.activation(xn[:, tt], xs[:, tt], ACT.Square, accum_out=ss1[:, tt:tt + 1]).then_inc(ss_ready, 1)
            act.wait_ge(rs_ready, 1)
            act.wait_ge(ss_ready, 2)
            for tt in range(TT):
                nc.scalar.mul(xn[:, tt], xs[:, tt], rs1[:, tt:tt + 1]).then_inc(xn_ready, 1)
            act.wait_ge(cst_in, 32)
            for i in range(4):
                o = take(act, ("x", i))
                for kk in range(2):
                    k = 2 * i + kk
                    ins = nc.scalar.mul(h_hi[:, k], o[:, T * kk:T * kk + T], col(V_G1 + k))
                ins.then_inc(h_hi_done, 1)
                if i < AHEAD:
                    high(i)

            def extra(t, p):
                if (t, p) == (1, 0):
                    copied(act, ("unit", 0))
                    nc.scalar.activation(th[0:64], lmix[0:64, 0], ACT.Tanh).then_inc(lora_ready, 1)
                    nc.scalar.activation(sgx, lmix[:, 1], ACT.Sigmoid).then_inc(lora_ready, 1)
                if (t, p) == (1, 3):
                    for c in range(TT):
                        o = take(act, ("z", c))
                        nc.scalar.activation(sg[:, c], o[:], ACT.Sigmoid).then_inc(drained_of(("z", c)), 1)
                    for i in range(2):
                        o = take(act, ("a", i))
                        for jj in range(2):
                            j = 2 * i + jj
                            ins = nc.scalar.activation(a_s[:, j], o[:, T * jj:T * jj + T], ACT.Sigmoid, bias=col(V_A0 + j))
                        ins.then_inc(drained_of(("a", i)), 1)
                if (t, p) in ((2, 3), (3, 1)):
                    c = t - 2
                    for i in range(2):
                        o = take(act, ("cum", c, i))
                        v = o[:].rearrange("p (j t) -> p j t", j=2)[:, :, 0:129]
                        nc.scalar.activation(e_up[:, c, 2 * i:2 * i + 2], v, ACT.Exp)
                        nc.scalar.activation(e_dn[:, c, 2 * i:2 * i + 2], v, ACT.Exp, scale=-1.0)\
                          .then_inc(drained_of(("cum", c, i)), 1)
                    if t == 3:
                        act.wait_ge(kkraw_ready, 1)
                        nc.scalar.activation(ksq, kkn, ACT.Square).then_inc(ksq_ready, 1)
                if (t, p) == (4, 0):
                    act.wait_ge(kk_inv, 1)
                    nc.scalar.copy(kkb.rearrange("p c (h v) -> p c h v", v=HD), by_channel(kk_tok)).then_inc(kkb_ready, 1)
                if S_QK + 1 < t <= S_QK + 5 and p == 0:
                    n = t - 2 - S_QK
                    act.wait_ge(qk_inv, n + 1)
                    nc.scalar.copy(sq_att[n % 2].rearrange("p (c h v) -> p c h v", c=TT, v=HD), by_channel(qk_tok[n % 2]))\
                      .then_inc(qkb_ready, 1)
                if (t, p) == (4, 3):
                    for i in range(2):
                        o = take(act, ("g", i))
                        nc.scalar.copy(gg[:, 2 * i:2 * i + 2], o[:].rearrange("p (j t) -> p j t", j=2))\
                          .then_inc(drained_of(("g", i)), 1)
                if (t, p) == (7, 1):
                    for c in range(TT):
                        o = take(act, ("vt", c))
                        nc.scalar.copy(vtok[:, c], o[:]).then_inc(drained_of(("vt", c)), 1)
                if (t, p) == (9, 2):
                    for dst, name in ((btok, ("bt",)), (ktok, ("kt",))):
                        o = take(act, name)
                        nc.scalar.copy(dst, o[:]).then_inc(drained_of(name), 1)
                if level_places(t) and p == 2:
                    c, l = level_places(t)
                    rows = lambda v: v.rearrange("p (h s) -> p h s", h=HEADS)
                    if l < LEVELS:
                        o = take(act, ("X", c, l))
                        nc.scalar.copy(x_c, rows(o[:])).then_inc(drained_of(("X", c, l)), 1)
                        o = take(act, ("XT", c, l))
                        nc.scalar.copy(xt_e[0:HD, :, 0:HD], rows(o[0:HD]))
                        nc.scalar.copy(xt_e[HD:P, :, HD:P], rows(o[HD:P]))
                        nc.scalar.copy(xt_c, rows(o[:])).then_inc(drained_of(("XT", c, l)), 1)
                    else:
                        o = take(act, ("XT", c, l))
                        nc.scalar.copy(xt_e[0:HD, :, HD:P], rows(o[0:HD])).then_inc(drained_of(("XT", c, l)), 1)
                if product_place(t, p) and product_place(t, p)[2] == 2:
                    c, g, _ = product_place(t, p)
                    act.wait_ge(xte_ready, 2 * c + g + 1)
                    hs = slice(4 * g, 4 * g + 4)
                    nc.scalar.copy(xt_c[0:HD, hs], xt_e[0:HD, hs, 0:HD])
                    nc.scalar.copy(xt_c[HD:P, hs], xt_e[HD:P, hs, HD:P]).then_inc(xt1_ready, 1)
                if t in S_APPLY:
                    c = S_APPLY.index(t)
                    if p == 1:
                        o = take(act, ("sa", c))
                        nc.scalar.copy(sa_sb, o[:].rearrange("p (h v) -> p h v", h=HEADS)).then_inc(drained_of(("sa", c)), 1)
                    if p == 2:
                        if c:
                            copied(act, ("ot", 0))
                        for e in range(2):
                            o = take(act, ("o", c, e))
                            nc.scalar.copy(o_sb.rearrange("p (j e) v -> p e j v", e=2)[:, e],
                                           o[:, 0:256].rearrange("p (j v) -> p j v", j=PAIRS))\
                              .then_inc(drained_of(("o", c, e)), 1)
                if t - 1 in S_APPLY:
                    c = S_APPLY.index(t - 1)
                    if p == 0:
                        act.wait_ge(oc_ready, c + 1)
                        nc.scalar.activation(osq, oc, ACT.Square).then_inc(osq_ready, 1)
                if (t, p) in ((S_GN[0], 3), (S_GN[1], 0)):
                    c = S_GN.index(t)
                    act.wait_ge(yr_pre, c + 1)
                    nc.scalar.copy(r_hi[:, :, P * c:P * c + P], ytmp).then_inc(yr_hi_done, 1)
                if S_HEAD <= t <= S_HEAD + HEADS:
                    h = t - S_HEAD
                    if p == 1 and h < HEADS:
                        act.wait_ge(neg_ready, 2 * h + 2)
                        for tt in range(TT):
                            w = prob[:, 0:P] if tt == 0 else prob[:, P:P + T]
                            nc.scalar.activation(w, w, ACT.Exp, bias=nmax[:, tt:tt + 1],
                                                 accum_out=psm[:, tt:tt + 1]).then_inc(exps_ready, 1)
                    if p == 0 and h >= 1:
                        o = take(act, ("pt", h - 1))
                        nc.scalar.copy(prob_t, o[:, 0:384]).then_inc(drained_of(("pt", h - 1)), 1)
                    if p == 3 and h >= 1:
                        n = h - 1
                        o = take(act, ("pv", n))
                        rows = slice(HD * (n % 2), HD * (n % 2) + HD)
                        nc.scalar.copy(y_hi[rows, n // 2], o[rows, 0:T]).then_inc(ya_hi, 1)
                if t == S_PY and p in (0, 2):
                    i = p // 2
                    o = take(act, ("pool", i))
                    for gi in range(2):
                        g = 2 * i + gi
                        ins = nc.scalar.mul(y_hi[:, 4 + g], o[:, T * gi:T * gi + T], col(V_PS + g))
                    ins.then_inc(yp_hi, 1)
                if (t, p) in ((S_OUT - 1, 3), (S_OUT, 3)):
                    ch = t - S_OUT + 1
                    for i in range(2):
                        o = take(act, ("m", 2 * ch + i))
                        k = 4 * ch + 2 * i
                        nc.scalar.mul(y_hi[:, k:k + 2], o[:].rearrange("p (k t) -> p k t", k=2), 0.5).then_inc(m_hi, 1)
                if t == S_FF - 1 and p in (1, 3):
                    for i in (p - 1, p):
                        o = take(act, ("h2", i))
                        for kk in range(2):
                            k = 2 * i + kk
                            ins = nc.scalar.mul(h_hi[:, k], o[:, T * kk:T * kk + T], col(V_G2 + k))
                        ins.then_inc(h2_hi, 1)
                if (t, p) == (S_FF - 1, 3):
                    for ch in range(2):
                        for tt in range(TT):
                            copied(act, ("out", ch, tt))
                    for tt in range(TT):
                        nc.scalar.activation(big[:, 2 + tt], xs[:, tt], ACT.Square, accum_out=ss2[:, tt:tt + 1])\
                          .then_inc(ss2_ready, 1)

            def finish(t):
                u = UNITS[t]
                if t < S_QK:
                    act.wait_ge(consts_ready, 1)
                    o = take(act, ("unit", t))
                    for j in range(2):
                        nc.scalar.mul(mix_dst(t, j), o[:, T * j:T * j + T], omu[:, mix_tile(t, j):mix_tile(t, j) + 1])\
                          .then_inc(keep_part, 1)
                elif t < S_VA:
                    n = t - S_QK
                    o = take(act, ("unit", t))
                    nc.scalar.copy((qraw if n < 2 else kraw)[:, 2 * (n % 2):2 * (n % 2) + 2],
                                   o[:].rearrange("p (j t) -> p j t", j=2))
                    if n >= 2:
                        take(act, ("qb", n - 2))
                    nc.scalar.activation(sq_att[n % 2], o[:], ACT.Square).then_inc(drained_of(("unit", t)), 1)
                elif u[0] == "tok" and u[2] == 1:
                    p = (t - S_GATE) // 2
                    for tt in range(TT):
                        name = ("tok", u[1], tt)
                        o = take(act, name)
                        if t < S_GATE:
                            nc.scalar.copy(vatt[:, tt], o[:]).then_inc(drained_of(name), 1)
                        else:
                            nc.scalar.activation(gates[p][:, tt], o[:], ACT.Tanh, scale=0.5).then_inc(drained_of(name), 1)
                elif t in (S_POOL, S_POOL + 1):
                    i = t - S_POOL
                    act.wait_ge(pad_ready, 1)
                    o = take(act, ("unit", t))
                    nc.scalar.copy(pu[:, 2 * i:2 * i + 2, PAD:PAD + T], o[:].rearrange("p (g t) -> p g t", g=2))\
                      .then_inc(drained_of(("unit", t)), 1)
                elif u[0] == "ff1":
                    i = u[1]
                    if i >= 2:
                        act.wait_ge(f_ready, i - 1)
                    o = take(act, ("ff", i))
                    nc.scalar.activation(ffs[i % 2], o[:], ACT.Relu).then_inc(drained_of(("ff", i)), 1)
                    copied(act, ("ff", i))
                    if i >= 2:
                        act.wait_ge(used, 2 * (UNITS.index(("ff2", i - 2)) + 1))
                    nc.scalar.activation(r_hi[:, 2 * (i % 2):2 * (i % 2) + 2], ffs[i % 2].rearrange("p (k t) -> p k t", k=2),
                                         ACT.Square).then_inc(f_hi, 1)

            for t in range(SLOTS):
                if 2 * t + AHEAD < PIECES:
                    high(2 * t + AHEAD)
                extra(t, 0)
                extra(t, 1)
                if 2 * t + 1 + AHEAD < PIECES:
                    high(2 * t + 1 + AHEAD)
                extra(t, 2)
                finish(t)
                extra(t, 3)

        @block.vector
        def _(dve):
            step = [0]

            def link(ins):
                step[0] += 1
                ins.then_inc(own, 1)
                dve.wait_ge(own, step[0])

            def low(v):
                dve.wait_ge(hi_done, v + 1)
                dve.tensor_tensor(w_lo[:, v % RING], stage[:, v % STAGES], w_hi[:, v % RING].bitcast(F32), ALU.subtract)\
                   .then_inc(lo_done, 1)

            def rest(dst, src, high_part):
                return dve.tensor_tensor(dst, src, high_part.bitcast(F32), ALU.subtract)

            dve.wait_ge(cst_in, 32)
            dve.tensor_scalar(omu, vec[:, V_MU:V_MU + 14], -1.0, 1.0, ALU.mult, ALU.add)
            dve.tensor_scalar(oka, vec[:, V_KA:V_KA + 4], -1.0, 1.0, ALU.mult, ALU.add)
            link(dve.tensor_scalar(gq8, vec[:, V_QN:V_QN + 1], HD ** -0.5, None, ALU.mult))
            dve.sem_inc(consts_ready, 1)
            dve.wait_ge(ss_ready, 2)
            dve.tensor_scalar(rs1, ss1, 1.0 / D, RMS_EPS, ALU.mult, ALU.add).then_inc(ms_ready, 1)
            for i in range(4):
                dve.wait_ge(h_hi_done, i + 1)
                o = take(dve, ("x", i))
                for kk in range(2):
                    k = 2 * i + kk
                    ins = dve.scalar_tensor_tensor(out=h_lo[:, k], in0=o[:, T * kk:T * kk + T], scalar=col(V_G1 + k),
                                                   in1=h_hi[:, k].bitcast(F32), op0=ALU.mult, op1=ALU.subtract)
                ins.then_inc(drained_of(("x", i)), 1)
                if i < AHEAD:
                    low(i)

            def extra(t, p):
                if (t, p) == (3, 0):
                    copied(dve, ("unit", 1))
                    copied(dve, ("unit", 2))
                    for j in range(PAIRS):
                        ins = dve.tensor_scalar(kkn[:, j], kmix[:, j], col(V_KK + j), None, ALU.mult)
                    ins.then_inc(kkraw_ready, 1)
                if (t, p) == (3, 3):
                    o = take(dve, ("kk",))
                    dve.tensor_scalar(kk_tok, o[:, 0:16].rearrange("p (c h) -> p c h", c=TT), 1e-24, None, ALU.max)\
                       .then_inc(drained_of(("kk",)), 1)
                if (t, p) == (4, 2):
                    for i in range(2):
                        o = take(dve, ("kb", i))
                        dve.tensor_tensor(kkn[:, 2 * i:2 * i + 2], kkn[:, 2 * i:2 * i + 2],
                                          o[:].rearrange("p (j t) -> p j t", j=2), ALU.mult).then_inc(drained_of(("kb", i)), 1)
                    for i in range(2):
                        copied(dve, ("kb", i))
                    copied(dve, ("a", 0))
                    copied(dve, ("a", 1))
                    for j in range(PAIRS):
                        ins = dve.tensor_scalar(k2[:, j], a_s[:, j], col(V_KA + j), oka[:, j:j + 1], ALU.mult, ALU.add)
                    link(ins)
                    dve.tensor_tensor(k2, k2, kmix, ALU.mult)
                    link(dve.tensor_tensor(a_s, a_s, kkn, ALU.mult))
                if (t, p) in ((5, 0), (5, 1)):
                    c = p
                    for i in range(2):
                        copied(dve, ("cum", c, i))
                    ts = slice(P * c, P * c + P)
                    dve.tensor_tensor(bk[c][:, 0], a_s[:, :, ts], e_dn[:, c, :, 1:129], ALU.mult)
                    dve.tensor_tensor(bk[c][:, 1], k2[:, :, ts], e_dn[:, c, :, 1:129], ALU.mult)
                    dve.scalar_tensor_tensor(out=ar[c][:, :, 0], in0=kkn[:, :, ts], scalar=-1.0, in1=e_up[:, c, :, 0:128],
                                             op0=ALU.mult, op1=ALU.mult)
                if (t, p) == (5, 2):
                    copied(dve, ("unit", 3))
                    copied(dve, ("unit", 4))
                    for c in range(TT):
                        dve.tensor_tensor(ar[c][:, :, 1], rmix[:, :, P * c:P * c + P], e_up[:, c, :, 1:129], ALU.mult)
                    ins = dve.tensor_tensor(e_end, e_up[:, 0, :, 128:129].squeeze(2), e_dn[:, 1, :, 0:1].squeeze(2), ALU.mult)
                    ins.then_inc(ops_ready, 1)
                    for j in range(PAIRS):
                        ins = dve.scalar_tensor_tensor(out=ksq[:, j], in0=rmix[:, j], scalar=col(V_RK + j), in1=k2[:, j],
                                                       op0=ALU.mult, op1=ALU.mult)
                    ins.then_inc(rk_ready, 1)
                if (t, p) == (7, 3):
                    copied(dve, ("unit", 5))
                    copied(dve, ("unit", 6))
                    for i in range(2):
                        o = take(dve, ("bonus", i))
                        dve.tensor_tensor(vmix[:, 2 * i:2 * i + 2], o[:].rearrange("p (j t) -> p j t", j=2),
                                          vmix[:, 2 * i:2 * i + 2], ALU.mult).then_inc(drained_of(("bonus", i)), 1)
                if S_QK < t <= S_QK + 4 and p == 3:
                    n = t - 1 - S_QK
                    o = take(dve, ("ss", n))
                    dve.tensor_scalar(qk_tok[n % 2], o[:, 0:8].rearrange("p (c h) -> p c h", c=TT), 1.0 / HD, RMS_EPS,
                                      ALU.mult, ALU.add).then_inc(drained_of(("ss", n)), 1)
                if S_QK + 1 < t <= S_QK + 5 and p == 2:
                    n = t - 2 - S_QK
                    o = take(dve, ("qb", n))
                    dst = (qraw if n < 2 else kraw)[:, 2 * (n % 2):2 * (n % 2) + 2]
                    dve.scalar_tensor_tensor(out=dst, in0=dst, scalar=gq8 if n < 2 else col(V_KN),
                                             in1=o[:].rearrange("p (j t) -> p j t", j=2),
                                             op0=ALU.mult, op1=ALU.mult).then_inc(drained_of(("qb", n)), 1)
                if product_place(t, p):
                    c, g, kind = product_place(t, p)
                    for e in range(2):
                        name = ("prod", c, g, kind, e)
                        o = take(dve, name)
                        if kind < 2:
                            if kind == 0:
                                dve.tensor_copy(corner.rearrange("p (i e) s -> p e i s", e=2)[:, e, 2 * g:2 * g + 2],
                                                o[0:HD].rearrange("p (i n) -> p i n", i=2)[:, :, HD:P])
                            dst = gm.rearrange("p (i e) a s -> p e i a s", e=2)[:, e, 2 * g:2 * g + 2, 2 * kind:2 * kind + 2]
                            m = (C_SDI, C_SI)[kind]
                            dve.tensor_tensor(dst.rearrange("p i a s -> p i (a s)"),
                                              o[:].rearrange("p (i n) -> p i n", i=2), wide(cst[:, m:m + 256], 2),
                                              ALU.mult).then_inc(drained_of(name), 1)
                        else:
                            for b in range(2):
                                rows = slice(HD * b, HD * b + HD)
                                ins = dve.tensor_tensor(x_c.rearrange("p (i e) s -> p e i s", e=2)[rows, e, 2 * g:2 * g + 2],
                                                        o[rows, 0:256].rearrange("p (i s) -> p i s", i=2)[:, :, rows],
                                                        wide(cst[rows, C_M1:C_M1 + HD], 2), ALU.mult)
                            ins.then_inc(drained_of(name), 1)
                    if kind == 2:
                        hs = slice(4 * g, 4 * g + 4)
                        dve.wait_ge(nt_ready, 2 * c + g + 1)
                        dve.tensor_tensor(xt_e[:, hs], gm[:, hs, 0], wide(cst[:, C_M1T:C_M1T + P], 4), ALU.mult)\
                           .then_inc(xte_ready, 1)
                if level_places(t) and p == 0:
                    c, l = level_places(t)
                    rows = lambda v: v.rearrange("p (h s) -> p h s", h=HEADS)
                    o = take(dve, ("Y", c, l))
                    if l < LEVELS:
                        dve.wait_ge(y_zero, 1)
                        m = cst[:, C_LEV + HD * l:C_LEV + HD * l + HD]
                        dve.tensor_tensor(y_c, rows(o[:]), wide(m, HEADS), ALU.mult)
                        dve.tensor_tensor(y_e[0:HD, :, 0:HD], rows(o[0:HD]), wide(m[0:HD], HEADS), ALU.mult)
                        dve.tensor_tensor(y_e[HD:P, :, HD:P], rows(o[HD:P]), wide(m[HD:P], HEADS), ALU.mult)\
                           .then_inc(drained_of(("Y", c, l)), 1)
                    else:
                        dve.tensor_copy(y_c[HD:P], rows(o[HD:P])).then_inc(drained_of(("Y", c, l)), 1)
                if t in S_APPLY:
                    c = S_APPLY.index(t)
                    if p == 0:
                        for e in range(2):
                            o = take(dve, ("rhs", c, e))
                            dve.tensor_copy(rhs_sb.rearrange("p (j e) v -> p e j v", e=2)[:, e],
                                            o[:, 0:256].rearrange("p (j v) -> p j v", j=PAIRS))\
                               .then_inc(drained_of(("rhs", c, e)), 1)
                    if p == 3 and c == 0:
                        o = take(dve, ("state",))
                        for j in range(PAIRS):
                            ins = dve.tensor_scalar(s_in[:, j], o[:, HD * j:HD * j + HD], e_end[:, j:j + 1], None, ALU.mult)
                        ins.then_inc(drained_of(("state",)), 1)
                if t - 1 in S_APPLY:
                    c = S_APPLY.index(t - 1)
                    heads = lambda v: v.rearrange("p (h v) -> p h v", h=HEADS)
                    per_head = lambda v: v.unsqueeze(2).to_broadcast([P, HEADS, HD])
                    if p == 0:
                        copied(dve, ("o", c, 0))
                        copied(dve, ("o", c, 1))
                        link(dve.tensor_reduce(gsum, o_sb, AX_X, ALU.add))
                        link(dve.tensor_scalar(gsum, gsum, -1.0 / HD, None, ALU.mult))
                        dve.tensor_tensor(heads(oc), o_sb, per_head(gsum), ALU.add).then_inc(oc_ready, 1)
                    if p == 1:
                        dve.wait_ge(osq_ready, c + 1)
                        link(dve.tensor_reduce(gvar, heads(osq), AX_X, ALU.add))
                        dve.tensor_scalar(gvar, gvar, 1.0 / HD, GN_EPS, ALU.mult, ALU.add).then_inc(gvar_ready, 1)
                    if p == 2:
                        dve.wait_ge(groot_ready, c + 1)
                        dve.tensor_tensor(heads(oc), heads(oc), per_head(gvar), ALU.mult).then_inc(on_ready, 1)
                if (t, p) in ((S_GN[0], 3), (S_GN[1], 0)):
                    c = S_GN.index(t)
                    ts = slice(P * c, P * c + P)
                    o = take(dve, ("ot", c))
                    for j in range(PAIRS):
                        ins = dve.tensor_scalar(ytmp[:, j], o[:, P * j:P * j + P], col(V_LG + j), col(V_LB + j),
                                                ALU.mult, ALU.add)
                    ins.then_inc(drained_of(("ot", c)), 1)
                    copied(dve, ("ot", c))
                    link(dve.tensor_tensor(ytmp, ytmp, vmix[:, :, ts], ALU.add))
                    copied(dve, ("g", 0))
                    copied(dve, ("g", 1))
                    dve.tensor_tensor(ytmp, ytmp, gg[:, :, ts], ALU.mult).then_inc(yr_pre, 1)
                    dve.wait_ge(yr_hi_done, c + 1)
                    rest(r_lo[:, :, ts], ytmp, r_hi[:, :, ts]).then_inc(yr_ready, 1)
                if S_HEAD <= t <= S_HEAD + HEADS:
                    h = t - S_HEAD
                    if p == 1 and h < HEADS:
                        o = take(dve, ("score", h))
                        dve.scalar_tensor_tensor(out=prob, in0=cst[:, C_BIAS:C_BIAS + 384], scalar=SLOPES[h],
                                                 in1=o[:, 0:384], op0=ALU.mult, op1=ALU.add)\
                           .then_inc(drained_of(("score", h)), 1)
                        copied(dve, ("score", h))
                        dve.tensor_reduce(nmax[:, 0:1], prob[:, 0:P], AX_X, ALU.max, negate=True).then_inc(neg_ready, 1)
                        dve.tensor_reduce(nmax[:, 1:2], prob[:, P:P + T], AX_X, ALU.max, negate=True).then_inc(neg_ready, 1)
                    if p == 2 and h < HEADS:
                        dve.wait_ge(exps_ready, 2 * h + 2)
                        link(dve.reciprocal(psm, psm))
                        dve.tensor_scalar(prob[:, 0:P], prob[:, 0:P], psm[:, 0:1], None, ALU.mult)
                        dve.tensor_scalar(prob[:, P:P + T], prob[:, P:P + T], psm[:, 1:2], None, ALU.mult)\
                           .then_inc(p_ready, 1)
                    if p == 3 and h >= 1:
                        n = h - 1
                        dve.wait_ge(ya_hi, h)
                        o = take(dve, ("pv", n))
                        rows = slice(HD * (n % 2), HD * (n % 2) + HD)
                        rest(y_lo[rows, n // 2], o[rows, 0:T], y_hi[rows, n // 2]).then_inc(drained_of(("pv", n)), 1)
                if t == S_PY and p in (0, 2):
                    i = p // 2
                    dve.wait_ge(yp_hi, i + 1)
                    o = take(dve, ("pool", i))
                    for gi in range(2):
                        g = 2 * i + gi
                        ins = dve.scalar_tensor_tensor(out=y_lo[:, 4 + g], in0=o[:, T * gi:T * gi + T], scalar=col(V_PS + g),
                                                       in1=y_hi[:, 4 + g].bitcast(F32), op0=ALU.mult, op1=ALU.subtract)
                    ins.then_inc(drained_of(("pool", i)), 1)
                if (t, p) in ((S_OUT - 1, 3), (S_OUT, 3)):
                    ch = t - S_OUT + 1
                    for i in range(2):
                        dve.wait_ge(m_hi, 2 * ch + i + 1)
                        o = take(dve, ("m", 2 * ch + i))
                        k = 4 * ch + 2 * i
                        dve.scalar_tensor_tensor(out=y_lo[:, k:k + 2], in0=o[:].rearrange("p (k t) -> p k t", k=2), scalar=0.5,
                                                 in1=y_hi[:, k:k + 2].bitcast(F32), op0=ALU.mult, op1=ALU.subtract)\
                            .then_inc(drained_of(("m", 2 * ch + i)), 1)
                if t == S_FF - 1 and p in (1, 3):
                    for i in (p - 1, p):
                        dve.wait_ge(h2_hi, i + 1)
                        o = take(dve, ("h2", i))
                        for kk in range(2):
                            k = 2 * i + kk
                            ins = dve.scalar_tensor_tensor(out=h_lo[:, k], in0=o[:, T * kk:T * kk + T], scalar=col(V_G2 + k),
                                                           in1=h_hi[:, k].bitcast(F32), op0=ALU.mult, op1=ALU.subtract)
                        ins.then_inc(drained_of(("h2", i)), 1)
                if (t, p) == (S_FF, 3):
                    dve.wait_ge(ss2_ready, 2)
                    link(dve.tensor_scalar(r2, ss2, 1.0 / D, RMS_EPS, ALU.mult, ALU.add))
                    link(dve.reciprocal(r2, r2))

            def finish(t):
                u = UNITS[t]
                if t < S_QK:
                    o = take(dve, ("unit", t))
                    dve.wait_ge(keep_part, 2 * t + 2)
                    for j in range(2):
                        dst, m = mix_dst(t, j), mix_tile(t, j)
                        ins = dve.scalar_tensor_tensor(out=dst[:, 1:T], in0=o[:, T * j:T * j + T - 1], scalar=col(V_MU + m),
                                                       in1=dst[:, 1:T], op0=ALU.mult, op1=ALU.add)
                    ins.then_inc(drained_of(("unit", t)), 1)
                elif u[0] == "branch":
                    n, ch = u[1], u[2]
                    g = 2 * n + ch
                    for tt in range(TT):
                        o = take(dve, ("unit", t, tt))
                        copied(dve, ("tok", N_RWKV + N_ATTN + N_POOL + 512 * g, tt))
                        dve.scalar_tensor_tensor(out=gates[g][:, tt], in0=gates[g][:, tt], scalar=1.0, in1=o[:],
                                                 op0=ALU.add, op1=ALU.mult)\
                           .then_inc(drained_of(("unit", t, tt)), 1)
                    if n == 0:
                        for tt in range(TT):
                            copied(dve, ("unit", t, tt))
                        dve.wait_ge(sum_ready, ch + 1)
                        dve.tensor_tensor(gates[ch], gates[ch], gates[2 + ch], ALU.add).then_inc(m_pre, 1)
                elif u[0] == "out" and u[1] == 1:
                    for tt in range(TT):
                        name = ("out", u[2], tt)
                        o = take(dve, name)
                        xc = xs[:, tt, 512 * u[2]:512 * u[2] + 512]
                        dve.tensor_tensor(xc, xc, o[:], ALU.add).then_inc(drained_of(name), 1)
                elif u[0] == "ff1":
                    i = u[1]
                    copied(dve, ("ff", i))
                    link(dve.tensor_tensor(fsq[i % 2], ffs[i % 2], ffs[i % 2], ALU.mult))
                    dve.wait_ge(f_hi, i + 1)
                    b = 2 * (i % 2)
                    rest(r_lo[:, b:b + 2], fsq[i % 2].rearrange("p (k t) -> p k t", k=2), r_hi[:, b:b + 2])\
                        .then_inc(f_ready, 1)

            for t in range(SLOTS):
                if 2 * t + AHEAD < PIECES:
                    low(2 * t + AHEAD)
                extra(t, 0)
                extra(t, 1)
                if 2 * t + 1 + AHEAD < PIECES:
                    low(2 * t + 1 + AHEAD)
                extra(t, 2)
                finish(t)
                extra(t, 3)
            for tt in range(TT):
                for c in range(2):
                    if (tt, c) == (1, 1):
                        dve.wait_ge(used, PIECES)
                        o = ps(("mlp", tt, c))
                    else:
                        o = take(dve, ("mlp", tt, c))
                    xc = xs[:, tt, 512 * c:512 * c + 512]
                    dve.scalar_tensor_tensor(out=xc, in0=o[:], scalar=r2[:, tt:tt + 1], in1=xc, op0=ALU.mult, op1=ALU.add)\
                       .then_inc(fin_ready, 1)

        @block.gpsimd
        def _(pool):
            pool.memset(th[64:65], 1.0).then_inc(ones_ready, 1)
            pool.wait_ge(ones_ready, 1)
            pool.memset(minus_half, -0.5).then_inc(ones_ready, 1)
            pool.wait_ge(ones_ready, 2)

            def inverse_root(ap, done):
                shape = list(ap.shape)
                half = minus_half if len(shape) == 2 else minus_half.unsqueeze(2)
                pool.tensor_tensor(ap, ap, half.to_broadcast(shape), ALU.pow).then_inc(done, 1)

            pool.wait_ge(ms_ready, 1)
            inverse_root(rs1, rs_ready)
            copied(pool, ("kk",))
            inverse_root(kk_tok, kk_inv)

            def add_identity(c, g):
                hs = slice(4 * g, 4 * g + 4)
                for e in range(2):
                    copied(pool, ("prod", c, g, 0, e))
                pool.tensor_tensor(gm[:, hs, 0], gm[:, hs, 0], wide(ident, 4), ALU.subtract).then_inc(nt_ready, 1)
                if g == 1:
                    for i in range(2):
                        for e in range(2):
                            copied(pool, ("prod", c, i, 2, e))
                    pool.tensor_tensor(x_c, x_c, wide(cst[:, C_IDC:C_IDC + HD], HEADS), ALU.add).then_inc(x1_ready, 1)

            def inverse_norm(n):
                copied(pool, ("ss", n))
                inverse_root(qk_tok[n % 2], qk_inv)

            pool.wait_ge(ops_ready, 1)
            pool.memset(y_e, 0.0).then_inc(y_zero, 1)
            add_identity(0, 0)
            inverse_norm(0)
            add_identity(0, 1)
            for n in (1, 2, 3):
                inverse_norm(n)
            copied(pool, ("kt",))
            pool.memset(pu[:, :, 0:PAD], 0.0).then_inc(pad_ready, 1)
            pool.memset(pt1[:, 0:PAD], 0.0).then_inc(pad_ready, 1)
            pool.memset(pt2[:, 0:PAD], 0.0).then_inc(pad_ready, 1)
            pool.wait_ge(pad_ready, 3)
            steps = 0
            for g, w in enumerate(WINDOWS):
                copied(pool, ("unit", S_POOL + g // 2))
                src, s = pu[:, g], 1
                while s < w:
                    dst = (pt1, pt2)[s.bit_length() % 2]
                    pool.tensor_tensor(dst[:, PAD:], src[:, PAD:], src[:, PAD - s:PAD + T - s], ALU.add).then_inc(pool_step, 1)
                    steps += 1
                    pool.wait_ge(pool_step, steps)
                    src, s = dst, 2 * s
                pool.tensor_tensor(pd[:, 0:PAD], src[:, PAD:2 * PAD], cst[:, C_INV + PAD * g:C_INV + PAD * g + PAD], ALU.mult)\
                    .then_inc(pool_step, 1)
                pool.tensor_scalar(pd[:, PAD:T], src[:, 2 * PAD:], 1.0 / w, None, ALU.mult).then_inc(pool_step, 1)
                steps += 2
                pool.wait_ge(pool_step, steps)
                pool.tensor_tensor(pu[:, g, PAD:], pd, pu[:, g, PAD:], ALU.subtract).then_inc(pd_ready, 1)
                pool.wait_ge(pd_ready, g + 1)

            def group_norm_root(c):
                pool.wait_ge(gvar_ready, c + 1)
                inverse_root(gvar, groot_ready)

            group_norm_root(0)
            add_identity(1, 0)
            add_identity(1, 1)
            group_norm_root(1)
            for ch in range(2):
                for n in (1, 2):
                    for tt in range(TT):
                        copied(pool, ("unit", S_BR + 2 * (n - 1) + ch, tt))
                pool.tensor_tensor(gates[2 + ch], gates[2 + ch], gates[4 + ch], ALU.add).then_inc(sum_ready, 1)


def shape_constants():
    c = np.zeros((P, C_ALL), np.float32)
    t, s = np.arange(P)[:, None], np.arange(P)[None, :]
    c[:, C_ID:C_ID + P] = t == s
    c[:, C_BLK:C_BLK + P] = t // HD == s // HD
    j = np.arange(129)[None, :]
    c[:, C_CUM:C_CUM + 129] = -np.exp(-0.5) * ((t < j).astype(np.float64) - (t < 64))
    c[:, C_BIAS:C_BIAS + P] = np.where(s <= t, s - t, -1e30)
    s2 = np.arange(T)[None, :]
    c[:, C_BIAS + P:C_BIAS + P + T] = np.where(s2 <= t + P, s2 - t - P, -1e30)
    c[:, C_SDI:C_SDI + P] = (t < s) & (t // HD == s // HD)
    c[:, C_SDI + P:C_SDI + 2 * P] = t <= s
    c[:, C_SI:C_SI + P] = t < s
    c[:, C_SI + P:C_SI + 2 * P] = t <= s
    r = np.arange(HD)[None, :]
    q = t % HD
    for l in range(LEVELS):
        b = 2 << l
        c[:, C_LEV + HD * l:C_LEV + HD * l + HD] = ((q // b % 2 == 1) & (r // b == q // b - 1)).astype(np.float32) - (q == r)
    c[:, C_M1:C_M1 + HD] = (q % 2 == 1) & (r == q - 1)
    c[:, C_IDC:C_IDC + HD] = q == r
    c[:, C_M1T:C_M1T + P] = ((s % 2 == 1) & (t == s - 1)).astype(np.float32) - (t == s)
    for g, w in enumerate(WINDOWS):
        c[:, C_INV + PAD * g:C_INV + PAD * g + PAD] = 1.0 / np.minimum(np.arange(PAD) + 1, w)
    return c


def channel_columns(shift_mu, a0, k_k, k_a, r_k, lnx_g, lnx_b, pool_scale, norm1_g, norm2_g, qn_g, kn_g):
    rows = [a.reshape(-1, P) for a in (shift_mu, a0, k_k, k_a, r_k, lnx_g, lnx_b, pool_scale, norm1_g, norm2_g)]
    rows += [np.concatenate([a, a], axis=1) for a in (qn_g, kn_g)]
    return np.ascontiguousarray(np.concatenate(rows, axis=0).T)


_WEIGHTS = ["x", "w_in", "w_up", "w0", "a_up", "g_up", "pool_w", "w_branch", "w_out", "w_ff1", "w_ff2"]


def kernel(**inputs):
    import concourse.bacc as _bacc
    from concourse.bass_utils import run_bass_kernel_spmd as _run

    a = {k: np.ascontiguousarray(v) for k, v in inputs.items()}
    arrays = {f"in_{k}": a[k] for k in _WEIGHTS}
    arrays["in_vecs"] = channel_columns(*(a[k] for k in (
        "shift_mu", "a0", "k_k", "k_a", "r_k", "lnx_g", "lnx_b", "pool_scale", "norm1_g", "norm2_g", "qn_g", "kn_g")))
    arrays["in_consts"] = shape_constants()
    nc = _bacc.Bacc("TRN2", target_bir_lowering=False, num_devices=1)
    args = [nc.dram_tensor(n, v.shape, mybir.dt.from_np(v.dtype), kind="ExternalInput").ap() for n, v in arrays.items()]
    args.append(nc.dram_tensor("out_0", (1, T, D), F32, kind="ExternalOutput").ap())
    build_layer(nc, *args)
    r = _run(nc, [arrays], core_ids=[0])
    return r.results[0]["out_0"]
```

```python
from contextlib import ExitStack

import numpy as np

import concourse.bass as bass
from concourse import mybir

F32 = mybir.dt.float32
F32R = mybir.dt.float32r
ALU = mybir.AluOpType
ACT = mybir.ActivationFunctionType
AX_X = mybir.AxisListType.X

P = 128
T, D = 256, 1024
TT = T // P
KD = D // P
HEADS, HD = 8, 64
W = HEADS * HD
PAIRS = HEADS // 2
N_RWKV, N_ATTN, N_POOL = 3 * W + 256, 3 * W, W
D_FF = 4 * D
RMS_EPS, GN_EPS = 1e-6, 64e-5
WINDOWS = (2, 4, 8, 16)
PAD = 16
LEVELS = 5
SLOPES = [2.0 ** (-8.0 * (h + 1) / HEADS) for h in range(HEADS)]

C_ID, C_BLK, C_CUM, C_BIAS = 0, 128, 256, 386
C_SDI = C_BIAS + 384
C_SI = C_SDI + 256
C_LEV = C_SI + 256
C_M1 = C_LEV + LEVELS * HD
C_IDC = C_M1 + HD
C_M1T = C_IDC + HD
C_INV = C_M1T + 128
C_ALL = C_INV + 4 * 16
V_MU, V_A0, V_KK, V_KA, V_RK, V_LG, V_LB, V_PS, V_G1, V_G2, V_QN, V_KN = 0, 14, 18, 22, 26, 30, 34, 38, 42, 50, 58, 59
V_ALL = 60

UNITS = [("feat", c) for c in (3 * W, W, W + 256, 0, 256, 2 * W, 2 * W + 256)]
UNITS += [("feat", N_RWKV + c) for c in (0, 256, W, W + 256)]
UNITS += [("tok", N_RWKV + 2 * W, kh) for kh in range(2)]
UNITS += [("feat", N_RWKV + N_ATTN + c) for c in (0, 256)]
UNITS += [("feat", N_RWKV + N_ATTN + N_POOL + 256 * q) for q in range(12)]
UNITS += [("branch", n, ch) for n in (1, 2, 0) for ch in range(2)]
UNITS += [("out", kh, ch) for kh in range(2) for ch in range(2)]
UNITS += [("ff1", 0)]
for i in range(1, D_FF // 256):
    UNITS += [("ff1", i), ("ff2", i - 1)]
UNITS += [("ff2", D_FF // 256 - 1)]
SLOTS = len(UNITS)
PIECES = 2 * SLOTS
STAGES = 3
RING = 6
FIRST_AHEAD = 3
AHEAD = 5
S_QK, S_VA, S_POOL, S_GATE, S_BR, S_OUT = 7, 11, 13, 15, 27, 33
S_FF = 37
S_PROD, S_LEV, S_APPLY, S_GN = (8, 17), (10, 19), (16, 25), (22, 28)
S_HEAD = 13
S_PY = 24
V_POOL_W = 2 * (S_HEAD + HEADS) + 8


def split_places(n):
    def lead(n):
        return n + min(AHEAD, FIRST_AHEAD + n // 4)
    return range(lead(n - 1) + 1 if n else FIRST_AHEAD, min(lead(n) + 1, PIECES))


def level_places(t):
    for c in range(TT):
        if S_LEV[c] <= t <= S_LEV[c] + LEVELS:
            return c, t - S_LEV[c]
    return None


def product_place(t, p):
    for c in range(TT):
        n = 4 * (t - S_PROD[c]) + p
        if 0 <= n < 6:
            return c, n // 3, n % 3
    return None


def plan_turns():
    turn, count, signalled, ring = {}, [0] * 8, [0] * 8, [0]

    def use(name, bank=None, dense=False):
        if bank is None:
            bank = 4 + ring[0] % 4
            ring[0] += 1
        turn[name] = (bank, count[bank], signalled[bank])
        count[bank] += 1
        signalled[bank] += not dense

    for i in range(4):
        use(("x", i))
    for t, u in enumerate(UNITS):
        for p in range(4):
            if p == 0:
                if u[0] == "feat":
                    use(("unit", t), t % 2, dense=True)
                elif u[0] == "tok" and u[2] == 0:
                    use(("tok", u[1], 0), 1)
                    use(("tok", u[1], 1), 0, dense=True)
                elif u[0] == "branch":
                    b = 2 * ((t - S_BR + 1) % 2)
                    use(("unit", t, 0), b, dense=True)
                    use(("unit", t, 1), b + 1, dense=True)
                elif u[0] == "out" and u[1] == 0:
                    for tt in range(TT):
                        use(("out", u[2], tt), 2 * (1 - u[2]) + tt, dense=tt == 1)
                elif u[0] == "ff1":
                    use(("ff", u[1]), dense=True)
                elif u == ("ff2", 0):
                    for b in range(4):
                        use(("mlp", b // 2, b % 2), b)
            for n in pe_uses(t, p):
                use(*n)
    return turn


def pe_uses(t, p):
    if (t, p) == (2, 1):
        return [(("z", 0),), (("z", 1),), (("a", 0),), (("a", 1),)]
    if (t, p) == (3, 1):
        return [(("cum", 0, 0),), (("cum", 0, 1),)]
    if (t, p) == (3, 3):
        return [(("cum", 1, 0),), (("cum", 1, 1),)]
    if (t, p) == (4, 0):
        return [(("kk",),)]
    if (t, p) == (5, 0):
        return [(("kb", 0),), (("kb", 1),)]
    if (t, p) == (4, 3):
        return [(("g", 0),), (("g", 1),)]
    if (t, p) == (7, 3):
        return [(("vt", 0),), (("vt", 1),)]
    out = []
    if (t, p) == (8, 1):
        out += [(("bonus", 0),), (("bonus", 1),)]
    if S_QK < t <= S_QK + 4 and p == 3:
        out.append((("ss", t - 1 - S_QK), 2))
    if S_QK + 1 < t <= S_QK + 5 and p == 1:
        out.append((("qb", t - 2 - S_QK), 3))
    if product_place(t, p):
        out += [(("prod", *product_place(t, p), e),) for e in range(2)]
    if (t, p) == (9, 2):
        out += [(("bt",),), (("kt",),)]
    if level_places(t):
        c, l = level_places(t)
        if p == 0:
            out += [(("Y", c, l),)]
        if p == 2 and l < LEVELS:
            out += [(("X", c, l),)]
        if p == 0 and l > 0:
            out += [(("XT", c, l - 1),)]
        if p == 2 and l == LEVELS:
            out += [(("XT", c, l),)]
    if t in S_APPLY:
        c = S_APPLY.index(t)
        if p == 0:
            out += [(("rhs", c, e),) for e in range(2)]
        if p == 1:
            out += [(("sa", c),)]
        if p == 2:
            out += [(("o", c, e),) for e in range(2)]
        if p == 3 and c == 0:
            out += [(("state",),)]
    if t in S_GN and p == 3:
        out += [(("ot", S_GN.index(t)),)]
    if S_HEAD <= t <= S_HEAD + HEADS:
        h = t - S_HEAD
        if p == 1 and h >= 1:
            out += [(("pt", h - 1), 3)]
        if p == 1 and h < HEADS:
            out += [(("score", h), 2)]
        if p == 3 and h >= 1:
            out += [(("pv", h - 1), 3)]
    if t == S_PY and p in (0, 2):
        out += [(("pool", p // 2), 2 + p // 2)]
    if t == S_FF - 1 and p in (1, 3):
        out += [(("h2", p - 1 + i),) for i in range(2)]
    return out


def dense_ends():
    ends = {}
    for t, u in enumerate(UNITS):
        if u[0] == "feat":
            ends[("unit", t)] = 2 * t + 2
        for tt in range(TT):
            if u[0] == "branch":
                ends[("unit", t, tt)] = 2 * t + 1 + tt
        if u[0] == "tok" and u[2] == 1:
            ends[("tok", u[1], 1)] = 2 * t + 2
        if u[0] == "out" and u[1] == 1:
            ends[("out", u[2], 1)] = 2 * t + 2
        if u[0] == "ff1":
            ends[("ff", u[1])] = 2 * t + 2
    return ends


DENSE_END = dense_ends()


def build_layer(nc: bass.Bass, x, w_in, w_up, w0, a_up, g_up, pool_w, w_branch, w_out, w_ff1, w_ff2, vecs, consts, out):
    turn = plan_turns()
    ctx = ExitStack()
    with ctx:
        def sb(name, shape, dt=F32):
            return ctx.enter_context(nc.sbuf_tensor(name, shape, dt))

        def sem(name):
            return ctx.enter_context(nc.semaphore(name))

        stage = sb("stage", [P, STAGES, 1024])
        w_hi = sb("w_hi", [P, RING, 1024], F32R)
        w_lo = sb("w_lo", [P, RING, 1024], F32R)
        h_hi = sb("h_hi", [P, KD, T], F32R)
        h_lo = sb("h_lo", [P, KD, T], F32R)
        y_hi = sb("y_hi", [P, KD, T], F32R)
        y_lo = sb("y_lo", [P, KD, T], F32R)
        r_hi = sb("r_hi", [P, 4, T], F32R)
        r_lo = sb("r_lo", [P, 4, T], F32R)
        xs = sb("xs", [P, TT, D])
        cst = sb("cst", [P, C_ALL])
        vec = sb("vec", [P, V_ALL])
        big = sb("big", [P, 6, 1024])
        mat = sb("mat", [P, 6176])
        lora = sb("lora", [P, 3, 512])
        vmix = sb("vmix", [P, PAIRS, T])
        lmix = sb("lmix", [P, 2, T])
        tsg = sb("tsg", [P, 2, T])
        gg = sb("gg", [P, PAIRS, T])
        ops = sb("ops", [P, 4096])
        vtok = sb("vtok", [P, TT, W])
        s_in = sb("s_in", [P, PAIRS, HD])
        att = sb("att", [P, 1024])
        small = sb("small", [P, 96])

        ident = cst[:, C_ID:C_ID + P]
        blk = cst[:, C_BLK:C_BLK + P]
        gates = [big[:, p].rearrange("p (t n) -> p t n", t=TT) for p in range(6)]
        q4 = lambda v: v.rearrange("p (j t) -> p j t", j=PAIRS)
        rmix, kmix = q4(big[:, 0]), q4(big[:, 1])
        btok, ktok = big[:, 2, 0:512], big[:, 2, 512:1024]
        qraw, kraw = q4(big[:, 3]), q4(big[:, 4])
        vatt = big[:, 5].rearrange("p (t n) -> p t n", t=TT)
        pool_sb = big[:, 5, 0:512].rearrange("p (g d) -> p g d", g=4)
        sg = big[:, 2].rearrange("p (t n) -> p t n", t=TT)
        xn = big[:, 4:6]
        flat = mat[:]
        a_s, kkn, k2, ksq = (q4(flat[:, 1024 * i:1024 * i + 1024]) for i in range(4))
        e_up, e_dn = (flat[:, 4096 + 1040 * i:4096 + 1040 * i + 1032].rearrange("p (c j t) -> p c j t", c=TT, j=PAIRS)
                      for i in range(2))
        gm = flat[:, 0:4096].rearrange("p (h a s) -> p h a s", h=HEADS, a=4)
        xt_e = flat[:, 4096:5120].rearrange("p (h s) -> p h s", h=HEADS)
        x_c, y_c = (flat[:, o:o + 512].rearrange("p (h s) -> p h s", h=HEADS) for o in (5120, 5632))
        opv = ops[:].rearrange("p (c z) -> p c z", c=TT)
        bk = [opv[:, c, 0:1024].rearrange("p (a j t) -> p a j t", a=2, j=PAIRS) for c in range(TT)]
        ar = [opv[:, c, 1024:2048].rearrange("p (j a t) -> p j a t", j=PAIRS, a=2) for c in range(TT)]
        pu = ops[:, 0:4 * (PAD + T)].rearrange("p (g t) -> p g t", g=4)
        pt1, pt2 = (ops[:, 1088 + 272 * i:1088 + 272 * i + 272] for i in range(2))
        pd = ops[:, 1632:1632 + 256]
        corner = lora[0:HD, 0].rearrange("p (h s) -> p h s", h=HEADS)
        th, sgx = tsg[:, 0], tsg[:, 1]
        osq = tsg[:].rearrange("p a t -> p (a t)")
        rhs_sb, sa_sb = (lora[:, i].rearrange("p (h v) -> p h v", h=HEADS) for i in range(2))
        oc = lora[:, 2]
        o_sb = oc.rearrange("p (h v) -> p h v", h=HEADS)
        ytmp = lmix[:].rearrange("p a t -> p (a t)").rearrange("p (j t) -> p j t", j=PAIRS)
        sq_att = [att[:, 512 * i:512 * i + 512] for i in range(2)]
        prob, prob_t = att[:, 0:384], att[:, 512:896]
        ffs, fsq = ([flat[:, 512 * i + o:512 * i + o + 512] for i in range(2)] for o in (0, 1024))
        omu, oka, gq8 = small[:, 0:14], small[:, 14:18], small[:, 18:19]
        ss1, rs1, ss2, r2, nmax, psm = (small[:, 20 + 2 * i:22 + 2 * i] for i in range(6))
        gsum, gvar = small[:, 32:40], small[:, 40:48]
        e_end, minus_half = small[:, 48:52], small[:, 52:53]
        kk_tok = small[:, 56:72].rearrange("p (c h) -> p c h", c=TT)
        qk_tok = [small[:, 72 + 8 * i:80 + 8 * i].rearrange("p (c h) -> p c h", c=TT) for i in range(2)]
        kkb = flat[:, 3072:4096].rearrange("p (c n) -> p c n", c=TT)

        def col(i):
            return vec[:, i:i + 1]

        def by_channel(ap):
            return ap.unsqueeze(3).to_broadcast([P, ap.shape[1], ap.shape[2], HD])

        def wide(ap, n):
            return ap.unsqueeze(1).to_broadcast([ap.shape[0], n, ap.shape[1]])

        banks = [ctx.enter_context(nc.psum_tensor(f"bank{i}", [P, 512], F32)) for i in range(8)]
        full = [sem(f"full{i}") for i in range(8)]
        drained = [sem(f"drained{i}") for i in range(8)]

        def ps(name):
            return banks[turn[name][0]]

        def full_of(name):
            return full[turn[name][0]]

        def drained_of(name):
            return drained[turn[name][0]]

        def room(eng, name):
            b, before, _ = turn[name]
            if before:
                eng.wait_ge(drained[b], before)
            return banks[b]

        def take(eng, name):
            b, _, before = turn[name]
            if name in DENSE_END:
                eng.wait_ge(used, DENSE_END[name])
            else:
                eng.wait_ge(full[b], before + 1)
            return banks[b]

        def copied(eng, name):
            b, before, _ = turn[name]
            eng.wait_ge(drained[b], before + 1)

        x_in = [sem(f"x_in{tt}") for tt in range(TT)]
        id_in, vec_in, cst_in, small_in, pool_in = (sem(n) for n in ("id_in", "vec_in", "cst_in", "small_in", "pool_in"))
        loaded = [sem(f"loaded{i}") for i in range(STAGES)]
        hi_done, lo_done = sem("hi_done"), sem("lo_done")
        used = sem("used")
        consts_ready = sem("consts_ready")
        ones_ready = sem("ones_ready")
        ss_ready, ms_ready, rs_ready = (
            sem(n) for n in ("ss_ready", "ms_ready", "rs_ready"))
        xn_ready = [sem(f"xn_ready{tt}") for tt in range(TT)]
        h_hi_done = sem("h_hi_done")
        keep_part = sem("keep_part")
        lora_ready = sem("lora_ready")
        kkraw_ready, ksq_ready, kk_inv, qk_inv, kkb_ready, qkb_ready = (
            sem(n) for n in ("kkraw_ready", "ksq_ready", "kk_inv", "qk_inv", "kkb_ready", "qkb_ready"))
        own = sem("own")
        rk_ready, ops_ready = sem("rk_ready"), sem("ops_ready")
        nt_ready, x1_ready, xte_ready = (
            sem(n) for n in ("nt_ready", "x1_ready", "xte_ready"))
        oc_ready, osq_ready, gvar_ready, groot_ready, on_ready, yr_pre, yr_hi_done, yr_ready = (
            sem(n) for n in ("oc_ready", "osq_ready", "gvar_ready", "groot_ready", "on_ready", "yr_pre", "yr_hi_done",
                             "yr_ready"))
        neg_ready, exps_ready, p_ready = sem("neg_ready"), sem("exps_ready"), sem("p_ready")
        ya_hi = sem("ya_hi")
        pad_ready, pool_step, pd_ready, yp_hi = (sem(n) for n in ("pad_ready", "pool_step", "pd_ready", "yp_hi"))
        sum_ready, m_pre, m_hi, m_ready = (sem(n) for n in ("sum_ready", "m_pre", "m_hi", "m_ready"))
        ss2_ready, h2_hi = sem("ss2_ready"), sem("h2_hi")
        f_hi, f_ready = sem("f_hi"), sem("f_ready")
        fin_ready, stored = sem("fin_ready"), sem("stored")

        block = ctx.enter_context(nc.Block())

        def piece_view(buf, v, slots=RING):
            kind = UNITS[v // 2][0]
            k = {"feat": KD, "ff1": KD, "ff2": 1, "branch": W // P}.get(kind, 2)
            return buf[:, v % slots].rearrange("p (k n) -> p k n", k=k)

        def piece_dram(v):
            u, half = UNITS[v // 2], v % 2
            if u[0] == "feat":
                return w_in[0, :, u[1] + P * half:u[1] + P * half + P].rearrange("(k p) n -> p k n", p=P)
            if u[0] == "ff1":
                c = 256 * u[1] + P * half
                return w_ff1[0, :, c:c + P].rearrange("(k p) n -> p k n", p=P)
            if u[0] == "ff2":
                r = 256 * u[1] + P * half
                return w_ff2[0, r:r + P, :].rearrange("(k p) n -> p k n", p=P)
            if u[0] == "branch":
                c = 512 * u[2] + 256 * half
                return w_branch[0, u[1], :, c:c + 256].rearrange("(k p) n -> p k n", p=P)
            if u[0] == "tok":
                r, m, c = 512 * u[2] + 256 * half, w_in[0], u[1]
            else:
                r, m, c = 512 * u[1] + 256 * half, w_out[0], 512 * u[2]
            return m[r:r + 256, c:c + 512].rearrange("(k p) n -> p k n", p=P)

        def mix_tile(t, j):
            return UNITS[t][1] // P + j

        def mix_dst(t, j):
            m = mix_tile(t, j)
            return (rmix, kmix, vmix, lmix)[m // 4][:, m % 4]

        @block.sync
        def _(sp):
            for tt in range(TT):
                sp.dma_start(xs[:, tt], x[0, P * tt:P * tt + P, :]).then_inc(x_in[tt], 16)
            sp.dma_start(cst[:, C_ID:C_ID + P], consts[:, C_ID:C_ID + P]).then_inc(id_in, 16)
            for v in range(PIECES):
                if v >= STAGES:
                    sp.wait_ge(lo_done, v - STAGES + 1)
                sp.dma_start(piece_view(stage, v, STAGES), piece_dram(v)).then_inc(loaded[v % STAGES], 16)
                if v == 0:
                    sp.dma_start(vec[:], vecs).then_inc(vec_in, 16)
                if v == 2:
                    sp.dma_start(cst[:, P:C_ALL], consts[:, P:C_ALL]).then_inc(cst_in, 16)
                if v == 1:
                    sp.dma_start(lora[0:64, 0], w_up[0]).then_inc(small_in, 16)
                    sp.dma_start(lora[64:65, 0], w0).then_inc(small_in, 16)
                    sp.dma_start(lora[64:128, 1], a_up[0]).then_inc(small_in, 16)
                    sp.dma_start(lora[:, 2], g_up[0]).then_inc(small_in, 16)
                if v == V_POOL_W:
                    for h in (HEADS - 2, HEADS - 1):
                        sp.wait_ge(full_of(("pv", h)), turn[("pv", h)][2] + 1)
                    sp.dma_start(pool_sb, pool_w[0].rearrange("g c d -> c g d")).then_inc(pool_in, 16)
            for n in range(4):
                sp.wait_ge(fin_ready, n + 1)
                tt, c = n // 2, n % 2
                sp.dma_start(out[0, P * tt:P * tt + P, 512 * c:512 * c + 512],
                             xs[:, tt, 512 * c:512 * c + 512]).then_inc(stored, 16)
            sp.wait_ge(stored, 64)

        @block.tensor
        def _(pe):
            def mm3(o, lh, ll, rh, rl, first, last):
                pe.matmul(o, lh, rh, start=first, stop=False)
                pe.matmul(o, lh, rl, start=False, stop=False)
                return pe.matmul(o, ll, rh, start=False, stop=last)

            def part(t, p):
                u, v = UNITS[t], 2 * t + p // 2
                if p % 2 == 0:
                    pe.wait_ge(lo_done, v + 1)
                wh, wl = piece_view(w_hi, v), piece_view(w_lo, v)
                i = p % 2
                if u[0] in ("feat", "ff1"):
                    name = ("unit", t) if u[0] == "feat" else ("ff", u[1])
                    if p == 0:
                        o = room(pe, name)
                    else:
                        o = ps(name)
                    j = p // 2
                    for k in range(4 * i, 4 * i + 4):
                        if p < 2 and k % 2 == 0 and (t == 0 or u == ("ff1", 0)):
                            copied(pe, ("h2" if t else "x", k // 2))
                        ins = mm3(o[:, T * j:T * j + T], wh[:, k], wl[:, k], h_hi[:, k], h_lo[:, k], k == 0, k == 7)
                elif u[0] == "ff2":
                    kt, buf = p // 2, 2 * (u[1] % 2)
                    if p == 0:
                        pe.wait_ge(f_ready, u[1] + 1)
                    for c in range(2):
                        name = ("mlp", i, c)
                        if u[1] == 0 and kt == 0:
                            room(pe, name)
                        ins = mm3(ps(name)[:], r_hi[:, buf + kt, P * i:P * i + P], r_lo[:, buf + kt, P * i:P * i + P],
                                  wh[:, 0, 512 * c:512 * c + 512], wl[:, 0, 512 * c:512 * c + 512],
                                  u[1] == 0 and kt == 0, u == UNITS[-1] and kt == 1)
                        if u == UNITS[-1] and kt == 1 and (i, c) != (1, 1):
                            ins.then_inc(full_of(name), 1)
                elif u[0] == "branch":
                    if p == 0:
                        if u[1] == 1:
                            copied(pe, ("pv", HEADS - 2))
                            copied(pe, ("pv", HEADS - 1))
                        elif u[1] == 2:
                            copied(pe, ("pool", 0))
                            copied(pe, ("pool", 1))
                        else:
                            pe.wait_ge(yr_ready, TT)
                    rh, rl, k0 = {1: (y_hi, y_lo, 0), 2: (y_hi, y_lo, 4), 0: (r_hi, r_lo, 0)}[u[1]]
                    name = ("unit", t, p // 2)
                    o = ps(name) if i else room(pe, name)
                    for k in range(W // P):
                        ins = mm3(o[:, T * i:T * i + T], wh[:, k, P * i:P * i + P], wl[:, k, P * i:P * i + P],
                                  rh[:, k0 + k], rl[:, k0 + k], k == 0, k == W // P - 1)
                else:
                    if u[0] == "tok":
                        name, lh, ll, k0 = ("tok", u[1], i), h_hi, h_lo, 4 * u[2]
                        first, last = u[2] == 0, u[2] == 1
                    else:
                        name, lh, ll, k0 = ("out", u[2], i), y_hi, y_lo, 4 * u[1]
                        first, last = u[1] == 0, u[1] == 1
                        if i == 0:
                            pe.wait_ge(m_ready, 2 * u[1] + p // 2 + 1)
                    o = room(pe, name) if first and p < 2 else ps(name)
                    for kk in range(2):
                        k = 2 * (p // 2) + kk
                        ins = mm3(o[:], lh[:, k0 + k, P * i:P * i + P], ll[:, k0 + k, P * i:P * i + P],
                                  wh[:, kk], wl[:, kk], first and k == 0, last and k == 3)
                    if last and p == 2:
                        ins.then_inc(full_of(name), 1)
                if p % 2:
                    ins.then_inc(used, 1)

            pe.wait_ge(id_in, 16)
            for tt in range(TT):
                for i in range(4):
                    pe.wait_ge(xn_ready[tt], i // 2 + 1)
                    o = room(pe, ("x", i))
                    for kk in range(2):
                        k = 2 * i + kk
                        ins = pe.transpose(o[:, T * kk + P * tt:T * kk + P * tt + P], xn[:, tt, P * k:P * k + P], ident)
                    if tt == TT - 1:
                        ins.then_inc(full_of(("x", i)), 1)

            def products(c, g, kind):
                if kind == 0 and g == 0:
                    pe.wait_ge(ops_ready, 1)
                for e in range(2):
                    name = ("prod", c, g, kind, e)
                    o = room(pe, name)
                    rows = slice(HD * e, HD * e + HD)
                    for i in range(2):
                        j = 2 * g + i
                        if kind < 2:
                            ins = pe.matmul(o[:, 256 * i:256 * i + 256], bk[c][rows, kind, j], ar[c][rows, j],
                                            start=True, stop=True)
                        else:
                            ins = pe.matmul(o[:, P * i:P * i + P], ar[c][rows, j, 0], bk[c][rows, 0, j],
                                            start=True, stop=True)
                    ins.then_inc(full_of(name), 1)

            def lower(o, transposed, rhs, start, stop):
                pe.matmul(o[0:HD], transposed[0:HD, 0:HD], rhs[0:HD], start=start, stop=stop)
                return pe.matmul(o[HD:P], transposed[:, HD:P], rhs, start=start, stop=stop)

            def extra(t, p):
                if (t, p) == (2, 1):
                    pe.wait_ge(small_in, 64)
                    pe.wait_ge(ones_ready, 1)
                    pe.wait_ge(lora_ready, 1)
                    for c in range(TT):
                        o = room(pe, ("z", c))
                        pe.matmul(o[:], th[0:65, P * c:P * c + P], lora[0:65, 0], start=True, stop=True)\
                          .then_inc(full_of(("z", c)), 1)
                    for i in range(2):
                        o = room(pe, ("a", i))
                        for jj in range(2):
                            j = 2 * i + jj
                            ins = pe.matmul(o[:, T * jj:T * jj + T], lora[64:128, 1, P * j:P * j + P], lmix[64:128, 0],
                                            start=True, stop=True)
                        ins.then_inc(full_of(("a", i)), 1)
                if (t, p) in ((3, 1), (3, 3)):
                    c = p // 2
                    pe.wait_ge(cst_in, 16)
                    copied(pe, ("z", c))
                    for i in range(2):
                        o = room(pe, ("cum", c, i))
                        for jj in range(2):
                            j = 2 * i + jj
                            ins = pe.matmul(o[:, 256 * jj:256 * jj + 129], sg[:, c, P * j:P * j + P],
                                            cst[:, C_CUM:C_CUM + 129], start=True, stop=True)
                        ins.then_inc(full_of(("cum", c, i)), 1)
                if (t, p) == (4, 0):
                    pe.wait_ge(ksq_ready, 1)
                    o = room(pe, ("kk",))
                    for c in range(TT):
                        for j in range(PAIRS):
                            ins = pe.matmul(o[:, 8 * c + 2 * j:8 * c + 2 * j + 2], ksq[:, j, P * c:P * c + P],
                                            cst[:, C_BLK:C_BLK + P:HD], start=True, stop=True)
                    ins.then_inc(full_of(("kk",)), 1)
                if (t, p) == (5, 0):
                    pe.wait_ge(kkb_ready, 1)
                    for i in range(2):
                        o = room(pe, ("kb", i))
                        for jj in range(2):
                            for c in range(TT):
                                j = 2 * i + jj
                                ins = pe.transpose(o[:, T * jj + P * c:T * jj + P * c + P],
                                                   kkb[:, c, P * j:P * j + P], ident)
                        ins.then_inc(full_of(("kb", i)), 1)
                if (t, p) == (4, 3):
                    pe.wait_ge(lora_ready, 2)
                    for i in range(2):
                        o = room(pe, ("g", i))
                        for jj in range(2):
                            j = 2 * i + jj
                            ins = pe.matmul(o[:, T * jj:T * jj + T], lora[:, 2, P * j:P * j + P], sgx,
                                            start=True, stop=True)
                        ins.then_inc(full_of(("g", i)), 1)
                if (t, p) == (7, 3):
                    copied(pe, ("unit", 5))
                    copied(pe, ("unit", 6))
                    for c in range(TT):
                        o = room(pe, ("vt", c))
                        for j in range(PAIRS):
                            ins = pe.transpose(o[:, P * j:P * j + P], vmix[:, j, P * c:P * c + P], ident)
                        ins.then_inc(full_of(("vt", c)), 1)
                if (t, p) == (8, 1):
                    pe.wait_ge(rk_ready, 1)
                    for i in range(2):
                        o = room(pe, ("bonus", i))
                        pe.matmul(o[:], blk, ksq[:, 2 * i:2 * i + 2].rearrange("p j t -> p (j t)"),
                                  start=True, stop=True).then_inc(full_of(("bonus", i)), 1)
                if S_QK < t <= S_QK + 4 and p == 3:
                    n = t - 1 - S_QK
                    copied(pe, ("unit", t - 1))
                    o = room(pe, ("ss", n))
                    for c in range(TT):
                        for jj in range(2):
                            ins = pe.matmul(o[:, 4 * c + 2 * jj:4 * c + 2 * jj + 2],
                                            sq_att[n % 2][:, T * jj + P * c:T * jj + P * c + P],
                                            cst[:, C_BLK:C_BLK + P:HD], start=True, stop=True)
                    ins.then_inc(full_of(("ss", n)), 1)
                if S_QK + 1 < t <= S_QK + 5 and p == 1:
                    n = t - 2 - S_QK
                    pe.wait_ge(qkb_ready, n + 1)
                    o = room(pe, ("qb", n))
                    for jj in range(2):
                        for c in range(TT):
                            ins = pe.transpose(o[:, T * jj + P * c:T * jj + P * c + P],
                                               sq_att[n % 2][:, 256 * c + P * jj:256 * c + P * jj + P], ident)
                    ins.then_inc(full_of(("qb", n)), 1)
                if product_place(t, p):
                    products(*product_place(t, p))
                if (t, p) == (9, 2):
                    for a, name in ((0, ("bt",)), (1, ("kt",))):
                        o = room(pe, name)
                        for j in range(PAIRS):
                            ins = pe.transpose(o[:, P * j:P * j + P], bk[0][:, a, j], ident)
                        ins.then_inc(full_of(name), 1)
                if level_places(t) and p == 0:
                    c, l = level_places(t)
                    if l == 0:
                        pe.wait_ge(nt_ready, 2 * c + 2)
                        pe.wait_ge(x1_ready, c + 1)
                    else:
                        copied(pe, ("X", c, l - 1))
                    o = room(pe, ("Y", c, l))
                    for h in range(HEADS):
                        if l < LEVELS:
                            for b in range(2):
                                rows = slice(HD * b, HD * b + HD)
                                ins = pe.matmul(o[rows, HD * h:HD * h + HD], gm[rows, h, 0, rows], x_c[rows, h],
                                                start=True, stop=True)
                        else:
                            ins = pe.matmul(o[HD:P, HD * h:HD * h + HD], corner[:, h], x_c[0:HD, h], start=True, stop=True)
                    ins.then_inc(full_of(("Y", c, l)), 1)
                if level_places(t) and p == 2:
                    c, l = level_places(t)
                    if l == 0:
                        pe.wait_ge(xte_ready, 2 * c + 2)
                    else:
                        copied(pe, ("XT", c, l - 1))
                    copied(pe, ("Y", c, l))
                    name = ("X" if l < LEVELS else "XT", c, l)
                    o = room(pe, name)
                    for h in range(HEADS):
                        if l < LEVELS:
                            for b in range(2):
                                rows = slice(HD * b, HD * b + HD)
                                ins = pe.matmul(o[rows, HD * h:HD * h + HD], xt_e[rows, h, rows], y_c[rows, h],
                                                start=True, stop=True)
                        else:
                            ins = pe.matmul(o[0:HD, HD * h:HD * h + HD], y_c[HD:P, h], xt_e[HD:P, h, HD:P],
                                            start=True, stop=True)
                    ins.then_inc(full_of(name), 1)
                if level_places(t) and p == 0 and level_places(t)[1] > 0:
                    c, l = level_places(t)
                    l -= 1
                    o = room(pe, ("XT", c, l))
                    for j in range(PAIRS):
                        ins = pe.transpose(o[:, P * j:P * j + P], x_c[:, 2 * j:2 * j + 2].rearrange("p h s -> p (h s)"), ident)
                    ins.then_inc(full_of(("XT", c, l)), 1)
                if t in S_APPLY:
                    c = S_APPLY.index(t)
                    if p == 0:
                        for g in range(2):
                            for e in range(2):
                                copied(pe, ("prod", c, g, 1, e))
                        copied(pe, ("vt", c))
                        if c == 1:
                            copied(pe, ("state",))
                        for e in range(2):
                            o = room(pe, ("rhs", c, e))
                            rows = slice(HD * e, HD * e + HD)
                            for j in range(PAIRS):
                                h = 2 * j + e
                                ins = lower(o[:, HD * j:HD * j + HD], gm[:, h, 2], vtok[:, c, HD * h:HD * h + HD], True, c == 0)
                                if c == 1:
                                    ins = pe.matmul(o[:, HD * j:HD * j + HD], ar[c][rows, j, 0], s_in[rows, j],
                                                    start=False, stop=True)
                            ins.then_inc(full_of(("rhs", c, e)), 1)
                    if p == 1:
                        for e in range(2):
                            copied(pe, ("rhs", c, e))
                        copied(pe, ("XT", c, LEVELS))
                        o = room(pe, ("sa", c))
                        for h in range(HEADS):
                            ins = lower(o[:, HD * h:HD * h + HD], xt_e[:, h], rhs_sb[:, h], True, True)
                        ins.then_inc(full_of(("sa", c)), 1)
                    if p == 2:
                        copied(pe, ("sa", c))
                        for e in range(2):
                            o = room(pe, ("o", c, e))
                            rows = slice(HD * e, HD * e + HD)
                            for j in range(PAIRS):
                                h = 2 * j + e
                                oo = o[:, HD * j:HD * j + HD]
                                lower(oo, gm[:, h, 1], sa_sb[:, h], True, False)
                                ins = lower(oo, gm[:, h, 3], vtok[:, c, HD * h:HD * h + HD], False, c == 0)
                                if c == 1:
                                    ins = pe.matmul(oo, ar[c][rows, j, 1], s_in[rows, j], start=False, stop=True)
                            ins.then_inc(full_of(("o", c, e)), 1)
                    if p == 3 and c == 0:
                        copied(pe, ("bt",))
                        copied(pe, ("kt",))
                        o = room(pe, ("state",))
                        for h in range(HEADS):
                            j, e = h // 2, h % 2
                            oo = o[HD * e:HD * e + HD, HD * j:HD * j + HD]
                            pe.matmul(oo, btok[:, HD * h:HD * h + HD], sa_sb[:, h], start=True, stop=False)
                            ins = pe.matmul(oo, ktok[:, HD * h:HD * h + HD], vtok[:, 0, HD * h:HD * h + HD],
                                            start=False, stop=True)
                        ins.then_inc(full_of(("state",)), 1)
                if t in S_GN and p == 3:
                    c = S_GN.index(t)
                    pe.wait_ge(on_ready, c + 1)
                    o = room(pe, ("ot", c))
                    for j in range(PAIRS):
                        ins = pe.transpose(o[:, P * j:P * j + P], oc[:, P * j:P * j + P], ident)
                    ins.then_inc(full_of(("ot", c)), 1)
                if S_HEAD <= t <= S_HEAD + HEADS:
                    h = t - S_HEAD
                    if p == 1 and h >= 1:
                        pe.wait_ge(p_ready, h)
                        o = room(pe, ("pt", h - 1))
                        for i in range(3):
                            ins = pe.transpose(o[:, P * i:P * i + P], prob[:, P * i:P * i + P], ident)
                        ins.then_inc(full_of(("pt", h - 1)), 1)
                    if p == 1 and h < HEADS:
                        copied(pe, ("qb", 3))
                        j, rows = h // 2, slice(HD * (h % 2), HD * (h % 2) + HD)
                        o = room(pe, ("score", h))
                        pe.matmul(o[:, 0:P], qraw[rows, j, 0:P], kraw[rows, j, 0:P], start=True, stop=True)
                        pe.matmul(o[:, P:P + T], qraw[rows, j, P:T], kraw[rows, j], start=True, stop=True)\
                          .then_inc(full_of(("score", h)), 1)
                    if p == 3 and h >= 1:
                        n = h - 1
                        copied(pe, ("pt", n))
                        for tt in range(TT):
                            copied(pe, ("tok", N_RWKV + 2 * W, tt))
                        o = room(pe, ("pv", n))
                        rows = slice(HD * (n % 2), HD * (n % 2) + HD)
                        pe.matmul(o[rows, 0:T], vatt[:, 0, HD * n:HD * n + HD], prob_t[:, 0:T], start=True, stop=False)
                        pe.matmul(o[rows, P:T], vatt[:, 1, HD * n:HD * n + HD], prob_t[:, T:T + P],
                                  start=False, stop=True).then_inc(full_of(("pv", n)), 1)
                if t == S_PY and p in (0, 2):
                    i = p // 2
                    pe.wait_ge(pool_in, 16)
                    pe.wait_ge(pd_ready, 2 * i + 2)
                    o = room(pe, ("pool", i))
                    for gi in range(2):
                        g = 2 * i + gi
                        ins = pe.matmul(o[:, T * gi:T * gi + T], pool_sb[:, g], pu[:, g, PAD:PAD + T],
                                        start=True, stop=True)
                    ins.then_inc(full_of(("pool", i)), 1)
                if t == S_FF - 1 and p in (1, 3):
                    for tt in range(TT):
                        copied(pe, ("out", p // 2, tt))
                        for i in (p - 1, p):
                            o = ps(("h2", i)) if tt else room(pe, ("h2", i))
                            for kk in range(2):
                                k = 2 * i + kk
                                ins = pe.transpose(o[:, T * kk + P * tt:T * kk + P * tt + P],
                                                   xs[:, tt, P * k:P * k + P], ident)
                            if tt == TT - 1:
                                ins.then_inc(full_of(("h2", i)), 1)

            for t in range(SLOTS):
                for p in range(4):
                    part(t, p)
                    extra(t, p)

        @block.scalar
        def _(act):
            def high(v):
                act.wait_ge(loaded[v % STAGES], 16 * (v // STAGES + 1))
                if v >= RING:
                    act.wait_ge(used, v - RING + 1)
                nc.scalar.copy(w_hi[:, v % RING], stage[:, v % STAGES]).then_inc(hi_done, 1)

            for tt in range(TT):
                act.wait_ge(x_in[tt], 16)
                nc.scalar.activation(xn[:, tt], xs[:, tt], ACT.Square, accum_out=ss1[:, tt:tt + 1]).then_inc(ss_ready, 1)
            high(0)
            act.wait_ge(vec_in, 16)
            for i in range(4):
                o = take(act, ("x", i))
                for kk in range(2):
                    k = 2 * i + kk
                    ins = nc.scalar.mul(h_hi[:, k], o[:, T * kk:T * kk + T], col(V_G1 + k))
                ins.then_inc(h_hi_done, 1)
            for v in range(1, FIRST_AHEAD):
                high(v)

            def extra(t, p):
                if (t, p) == (1, 0):
                    copied(act, ("unit", 0))
                    nc.scalar.activation(th[0:64], lmix[0:64, 0], ACT.Tanh).then_inc(lora_ready, 1)
                    nc.scalar.activation(sgx, lmix[:, 1], ACT.Sigmoid).then_inc(lora_ready, 1)
                if (t, p) == (2, 1):
                    for c in range(TT):
                        o = take(act, ("z", c))
                        nc.scalar.activation(sg[:, c], o[:], ACT.Sigmoid).then_inc(drained_of(("z", c)), 1)
                    for i in range(2):
                        o = take(act, ("a", i))
                        for jj in range(2):
                            j = 2 * i + jj
                            ins = nc.scalar.activation(a_s[:, j], o[:, T * jj:T * jj + T], ACT.Sigmoid, bias=col(V_A0 + j))
                        ins.then_inc(drained_of(("a", i)), 1)
                if (t, p) in ((3, 1), (3, 3)):
                    c = p // 2
                    for i in range(2):
                        o = take(act, ("cum", c, i))
                        v = o[:].rearrange("p (j t) -> p j t", j=2)[:, :, 0:129]
                        nc.scalar.activation(e_up[:, c, 2 * i:2 * i + 2], v, ACT.Exp)
                        nc.scalar.activation(e_dn[:, c, 2 * i:2 * i + 2], v, ACT.Exp, scale=-1.0)\
                          .then_inc(drained_of(("cum", c, i)), 1)
                if (t, p) == (3, 2):
                    act.wait_ge(kkraw_ready, 1)
                    nc.scalar.activation(ksq, kkn, ACT.Square).then_inc(ksq_ready, 1)
                if (t, p) == (4, 3):
                    act.wait_ge(kk_inv, 1)
                    nc.scalar.copy(kkb.rearrange("p c (h v) -> p c h v", v=HD), by_channel(kk_tok)).then_inc(kkb_ready, 1)
                if S_QK + 1 < t <= S_QK + 5 and p == 0:
                    n = t - 2 - S_QK
                    act.wait_ge(qk_inv, n + 1)
                    nc.scalar.copy(sq_att[n % 2].rearrange("p (c h v) -> p c h v", c=TT, v=HD), by_channel(qk_tok[n % 2]))\
                      .then_inc(qkb_ready, 1)
                if (t, p) == (4, 3):
                    for i in range(2):
                        o = take(act, ("g", i))
                        nc.scalar.copy(gg[:, 2 * i:2 * i + 2], o[:].rearrange("p (j t) -> p j t", j=2))\
                          .then_inc(drained_of(("g", i)), 1)
                if (t, p) == (7, 3):
                    for c in range(TT):
                        o = take(act, ("vt", c))
                        nc.scalar.copy(vtok[:, c], o[:]).then_inc(drained_of(("vt", c)), 1)
                if (t, p) == (9, 2):
                    for dst, name in ((btok, ("bt",)), (ktok, ("kt",))):
                        o = take(act, name)
                        nc.scalar.copy(dst, o[:]).then_inc(drained_of(name), 1)
                if level_places(t) and p == 0 and level_places(t)[1] > 0:
                    c, l = level_places(t)
                    l -= 1
                    o = take(act, ("XT", c, l))
                    by_head = xt_e.rearrange("p (j e) s -> p e j s", e=2)
                    for b in range(2):
                        blk_rows = slice(HD * b, HD * b + HD)
                        for e in range(2):
                            ins = nc.scalar.copy(by_head[blk_rows, e, :, blk_rows],
                                                 o[HD * e:HD * e + HD].rearrange("p (j s) -> p j s", j=PAIRS)[:, :, blk_rows])
                    ins.then_inc(drained_of(("XT", c, l)), 1)
                if level_places(t) and p == 2:
                    c, l = level_places(t)
                    rows = lambda v: v.rearrange("p (h s) -> p h s", h=HEADS)
                    if l < LEVELS:
                        o = take(act, ("X", c, l))
                        nc.scalar.copy(x_c, rows(o[:])).then_inc(drained_of(("X", c, l)), 1)
                    else:
                        o = take(act, ("XT", c, l))
                        nc.scalar.copy(xt_e[0:HD, :, HD:P], rows(o[0:HD])).then_inc(drained_of(("XT", c, l)), 1)
                if t in S_APPLY:
                    c = S_APPLY.index(t)
                    if p == 1:
                        o = take(act, ("sa", c))
                        nc.scalar.copy(sa_sb, o[:].rearrange("p (h v) -> p h v", h=HEADS)).then_inc(drained_of(("sa", c)), 1)
                    if p == 2:
                        if c:
                            copied(act, ("ot", 0))
                        for e in range(2):
                            o = take(act, ("o", c, e))
                            nc.scalar.copy(o_sb.rearrange("p (j e) v -> p e j v", e=2)[:, e],
                                           o[:, 0:256].rearrange("p (j v) -> p j v", j=PAIRS))\
                              .then_inc(drained_of(("o", c, e)), 1)
                if t - 1 in S_APPLY:
                    c = S_APPLY.index(t - 1)
                    if p == 0:
                        act.wait_ge(oc_ready, c + 1)
                        nc.scalar.activation(osq, oc, ACT.Square).then_inc(osq_ready, 1)
                if t - 1 in S_GN and p == 1:
                    c = S_GN.index(t - 1)
                    act.wait_ge(yr_pre, c + 1)
                    nc.scalar.copy(r_hi[:, :, P * c:P * c + P], ytmp).then_inc(yr_hi_done, 1)
                if S_HEAD <= t <= S_HEAD + HEADS:
                    h = t - S_HEAD
                    if p == 1 and h >= 1:
                        o = take(act, ("pt", h - 1))
                        nc.scalar.copy(prob_t, o[:, 0:384]).then_inc(drained_of(("pt", h - 1)), 1)
                    if p == 1 and h < HEADS:
                        act.wait_ge(neg_ready, 2 * h + 2)
                        for tt in range(TT):
                            w = prob[:, 0:P] if tt == 0 else prob[:, P:P + T]
                            nc.scalar.activation(w, w, ACT.Exp, bias=nmax[:, tt:tt + 1],
                                                 accum_out=psm[:, tt:tt + 1]).then_inc(exps_ready, 1)
                    if p == 3 and h >= 1:
                        n = h - 1
                        o = take(act, ("pv", n))
                        rows = slice(HD * (n % 2), HD * (n % 2) + HD)
                        nc.scalar.copy(y_hi[rows, n // 2], o[rows, 0:T]).then_inc(ya_hi, 1)
                if t == S_PY and p in (0, 2):
                    i = p // 2
                    o = take(act, ("pool", i))
                    for gi in range(2):
                        g = 2 * i + gi
                        ins = nc.scalar.mul(y_hi[:, 4 + g], o[:, T * gi:T * gi + T], col(V_PS + g))
                    ins.then_inc(yp_hi, 1)
                if t == S_FF - 1 and p in (1, 3):
                    for i in (p - 1, p):
                        o = take(act, ("h2", i))
                        for kk in range(2):
                            k = 2 * i + kk
                            ins = nc.scalar.mul(h_hi[:, k], o[:, T * kk:T * kk + T], col(V_G2 + k))
                        ins.then_inc(h2_hi, 1)
                if (t, p) == (S_FF - 1, 3):
                    for ch in range(2):
                        for tt in range(TT):
                            copied(act, ("out", ch, tt))
                    for tt in range(TT):
                        nc.scalar.activation(big[:, 2 + tt], xs[:, tt], ACT.Square, accum_out=ss2[:, tt:tt + 1])\
                          .then_inc(ss2_ready, 1)

            def finish(t):
                u = UNITS[t]
                if t < S_QK:
                    act.wait_ge(consts_ready, 1)
                    o = take(act, ("unit", t))
                    for j in range(2):
                        nc.scalar.mul(mix_dst(t, j), o[:, T * j:T * j + T], omu[:, mix_tile(t, j):mix_tile(t, j) + 1])\
                          .then_inc(keep_part, 1)
                elif t < S_VA:
                    n = t - S_QK
                    o = take(act, ("unit", t))
                    nc.scalar.copy((qraw if n < 2 else kraw)[:, 2 * (n % 2):2 * (n % 2) + 2],
                                   o[:].rearrange("p (j t) -> p j t", j=2))
                    if n >= 2:
                        take(act, ("qb", n - 2))
                    nc.scalar.activation(sq_att[n % 2], o[:], ACT.Square).then_inc(drained_of(("unit", t)), 1)
                elif u[0] == "tok" and u[2] == 1:
                    for tt in range(TT):
                        name = ("tok", u[1], tt)
                        o = take(act, name)
                        nc.scalar.copy(vatt[:, tt], o[:]).then_inc(drained_of(name), 1)
                elif S_GATE <= t < S_BR:
                    o = take(act, ("unit", t))
                    nc.scalar.activation(gates[(t - S_GATE) // 2][:, t % 2 ^ S_GATE % 2], o[:], ACT.Tanh, scale=0.5)\
                      .then_inc(drained_of(("unit", t)), 1)
                elif u[0] == "branch" and u[1] == 0:
                    for i in range(2):
                        m = 2 * u[2] + i
                        act.wait_ge(m_pre, m + 1)
                        nc.scalar.mul(y_hi[:, 2 * m:2 * m + 2], gates[u[2]][:, i].rearrange("p (k t) -> p k t", k=2), 0.5)\
                          .then_inc(m_hi, 1)
                elif t in (S_POOL, S_POOL + 1):
                    i = t - S_POOL
                    act.wait_ge(pad_ready, 1)
                    o = take(act, ("unit", t))
                    nc.scalar.copy(pu[:, 2 * i:2 * i + 2, PAD:PAD + T], o[:].rearrange("p (g t) -> p g t", g=2))\
                      .then_inc(drained_of(("unit", t)), 1)
                elif u[0] == "ff1":
                    i = u[1]
                    if i >= 2:
                        act.wait_ge(f_ready, i - 1)
                    o = take(act, ("ff", i))
                    nc.scalar.activation(ffs[i % 2], o[:], ACT.Relu).then_inc(drained_of(("ff", i)), 1)
                    copied(act, ("ff", i))
                    if i >= 2:
                        act.wait_ge(used, 2 * (UNITS.index(("ff2", i - 2)) + 1))
                    nc.scalar.activation(r_hi[:, 2 * (i % 2):2 * (i % 2) + 2], ffs[i % 2].rearrange("p (k t) -> p k t", k=2),
                                         ACT.Square).then_inc(f_hi, 1)

            for t in range(SLOTS):
                for v in split_places(2 * t):
                    high(v)
                extra(t, 0)
                late = t == S_FF - 1
                for v in split_places(2 * t + 1) if not late else ():
                    high(v)
                extra(t, 1)
                extra(t, 2)
                finish(t)
                extra(t, 3)
                for v in split_places(2 * t + 1) if late else ():
                    high(v)

        @block.vector
        def _(dve):
            step = [0]

            def link(ins):
                step[0] += 1
                ins.then_inc(own, 1)
                dve.wait_ge(own, step[0])

            def low(v):
                dve.wait_ge(hi_done, v + 1)
                dve.tensor_tensor(w_lo[:, v % RING], stage[:, v % STAGES], w_hi[:, v % RING].bitcast(F32), ALU.subtract)\
                   .then_inc(lo_done, 1)

            def rest(dst, src, high_part):
                return dve.tensor_tensor(dst, src, high_part.bitcast(F32), ALU.subtract)

            for tt in range(TT):
                dve.wait_ge(ss_ready, tt + 1)
                dve.tensor_scalar(rs1[:, tt:tt + 1], ss1[:, tt:tt + 1], 1.0 / D, RMS_EPS, ALU.mult, ALU.add)\
                   .then_inc(ms_ready, 1)
                dve.wait_ge(rs_ready, tt + 1)
                for n in range(2):
                    dve.tensor_scalar(xn[:, tt, 512 * n:512 * n + 512], xs[:, tt, 512 * n:512 * n + 512], rs1[:, tt:tt + 1],
                                      None, ALU.mult).then_inc(xn_ready[tt], 1)
            low(0)
            dve.wait_ge(vec_in, 16)
            dve.tensor_scalar(omu, vec[:, V_MU:V_MU + 14], -1.0, 1.0, ALU.mult, ALU.add)
            dve.tensor_scalar(oka, vec[:, V_KA:V_KA + 4], -1.0, 1.0, ALU.mult, ALU.add)
            dve.tensor_scalar(gq8, vec[:, V_QN:V_QN + 1], HD ** -0.5, None, ALU.mult).then_inc(consts_ready, 1)
            for i in range(4):
                dve.wait_ge(h_hi_done, i + 1)
                o = take(dve, ("x", i))
                for kk in range(2):
                    k = 2 * i + kk
                    ins = dve.scalar_tensor_tensor(out=h_lo[:, k], in0=o[:, T * kk:T * kk + T], scalar=col(V_G1 + k),
                                                   in1=h_hi[:, k].bitcast(F32), op0=ALU.mult, op1=ALU.subtract)
                ins.then_inc(drained_of(("x", i)), 1)
            for v in range(1, FIRST_AHEAD):
                low(v)

            def extra(t, p):
                if (t, p) == (3, 0):
                    copied(dve, ("unit", 1))
                    copied(dve, ("unit", 2))
                    for j in range(PAIRS):
                        ins = dve.tensor_scalar(kkn[:, j], kmix[:, j], col(V_KK + j), None, ALU.mult)
                    ins.then_inc(kkraw_ready, 1)
                if (t, p) == (4, 0):
                    o = take(dve, ("kk",))
                    dve.tensor_scalar(kk_tok, o[:, 0:16].rearrange("p (c h) -> p c h", c=TT), 1e-24, None, ALU.max)\
                       .then_inc(drained_of(("kk",)), 1)
                if (t, p) == (4, 2):
                    copied(dve, ("a", 0))
                    copied(dve, ("a", 1))
                    for j in range(PAIRS):
                        ins = dve.tensor_scalar(k2[:, j], a_s[:, j], col(V_KA + j), oka[:, j:j + 1], ALU.mult, ALU.add)
                    link(ins)
                    dve.tensor_tensor(k2, k2, kmix, ALU.mult)
                if (t, p) == (5, 0):
                    for i in range(2):
                        o = take(dve, ("kb", i))
                        dve.tensor_tensor(kkn[:, 2 * i:2 * i + 2], kkn[:, 2 * i:2 * i + 2],
                                          o[:].rearrange("p (j t) -> p j t", j=2), ALU.mult).then_inc(drained_of(("kb", i)), 1)
                if (t, p) == (5, 3):
                    for i in range(2):
                        copied(dve, ("kb", i))
                    link(dve.tensor_tensor(a_s, a_s, kkn, ALU.mult))
                if t == 6 and p in (0, 2):
                    c = p // 2
                    for i in range(2):
                        copied(dve, ("cum", c, i))
                    ts = slice(P * c, P * c + P)
                    dve.tensor_tensor(bk[c][:, 0], a_s[:, :, ts], e_dn[:, c, :, 1:129], ALU.mult)
                    dve.tensor_tensor(bk[c][:, 1], k2[:, :, ts], e_dn[:, c, :, 1:129], ALU.mult)
                    dve.scalar_tensor_tensor(out=ar[c][:, :, 0], in0=kkn[:, :, ts], scalar=-1.0, in1=e_up[:, c, :, 0:128],
                                             op0=ALU.mult, op1=ALU.mult)
                if (t, p) == (5, 2):
                    copied(dve, ("unit", 3))
                    copied(dve, ("unit", 4))
                    for c in range(TT):
                        for i in range(2):
                            copied(dve, ("cum", c, i))
                        dve.tensor_tensor(ar[c][:, :, 1], rmix[:, :, P * c:P * c + P], e_up[:, c, :, 1:129], ALU.mult)
                if (t, p) == (7, 0):
                    dve.tensor_tensor(e_end, e_up[:, 0, :, 128:129].squeeze(2), e_dn[:, 1, :, 0:1].squeeze(2), ALU.mult)\
                       .then_inc(ops_ready, 1)
                    for j in range(PAIRS):
                        ins = dve.scalar_tensor_tensor(out=ksq[:, j], in0=rmix[:, j], scalar=col(V_RK + j), in1=k2[:, j],
                                                       op0=ALU.mult, op1=ALU.mult)
                    ins.then_inc(rk_ready, 1)
                if (t, p) == (8, 1):
                    copied(dve, ("unit", 5))
                    copied(dve, ("unit", 6))
                    for i in range(2):
                        o = take(dve, ("bonus", i))
                        dve.tensor_tensor(vmix[:, 2 * i:2 * i + 2], o[:].rearrange("p (j t) -> p j t", j=2),
                                          vmix[:, 2 * i:2 * i + 2], ALU.mult).then_inc(drained_of(("bonus", i)), 1)
                if S_QK < t <= S_QK + 4 and p == 3:
                    n = t - 1 - S_QK
                    o = take(dve, ("ss", n))
                    dve.tensor_scalar(qk_tok[n % 2], o[:, 0:8].rearrange("p (c h) -> p c h", c=TT), 1.0 / HD, RMS_EPS,
                                      ALU.mult, ALU.add).then_inc(drained_of(("ss", n)), 1)
                if S_QK + 1 < t <= S_QK + 5 and p == 2:
                    n = t - 2 - S_QK
                    o = take(dve, ("qb", n))
                    dst = (qraw if n < 2 else kraw)[:, 2 * (n % 2):2 * (n % 2) + 2]
                    dve.scalar_tensor_tensor(out=dst, in0=dst, scalar=gq8 if n < 2 else col(V_KN),
                                             in1=o[:].rearrange("p (j t) -> p j t", j=2),
                                             op0=ALU.mult, op1=ALU.mult).then_inc(drained_of(("qb", n)), 1)
                if product_place(t, p):
                    c, g, kind = product_place(t, p)
                    for e in range(2):
                        name = ("prod", c, g, kind, e)
                        o = take(dve, name)
                        if kind < 2:
                            if kind == 0:
                                dve.tensor_copy(corner.rearrange("p (i e) s -> p e i s", e=2)[:, e, 2 * g:2 * g + 2],
                                                o[0:HD].rearrange("p (i n) -> p i n", i=2)[:, :, HD:P])
                            dst = gm.rearrange("p (i e) a s -> p e i a s", e=2)[:, e, 2 * g:2 * g + 2, 2 * kind:2 * kind + 2]
                            m = (C_SDI, C_SI)[kind]
                            dve.tensor_tensor(dst.rearrange("p i a s -> p i (a s)"),
                                              o[:].rearrange("p (i n) -> p i n", i=2), wide(cst[:, m:m + 256], 2),
                                              ALU.mult).then_inc(drained_of(name), 1)
                        else:
                            for b in range(2):
                                rows = slice(HD * b, HD * b + HD)
                                ins = dve.tensor_tensor(x_c.rearrange("p (i e) s -> p e i s", e=2)[rows, e, 2 * g:2 * g + 2],
                                                        o[rows, 0:256].rearrange("p (i s) -> p i s", i=2)[:, :, rows],
                                                        wide(cst[rows, C_M1:C_M1 + HD], 2), ALU.mult)
                            ins.then_inc(drained_of(name), 1)
                before = product_place(*((t, p - 1) if p else (t - 1, 3)))
                if before and before[2] == 2:
                    c, g, _ = before
                    hs = slice(4 * g, 4 * g + 4)
                    dve.wait_ge(nt_ready, 2 * c + g + 1)
                    dve.tensor_tensor(xt_e[:, hs], gm[:, hs, 0], wide(cst[:, C_M1T:C_M1T + P], 4), ALU.mult)\
                       .then_inc(xte_ready, 1)
                if level_places(t) and p == 0:
                    c, l = level_places(t)
                    rows = lambda v: v.rearrange("p (h s) -> p h s", h=HEADS)
                    o = take(dve, ("Y", c, l))
                    if l < LEVELS:
                        dve.tensor_tensor(y_c, rows(o[:]), wide(cst[:, C_LEV + HD * l:C_LEV + HD * l + HD], HEADS), ALU.mult)\
                           .then_inc(drained_of(("Y", c, l)), 1)
                    else:
                        dve.tensor_copy(y_c[HD:P], rows(o[HD:P])).then_inc(drained_of(("Y", c, l)), 1)
                if t in S_APPLY:
                    c = S_APPLY.index(t)
                    if p == 0:
                        for e in range(2):
                            o = take(dve, ("rhs", c, e))
                            dve.tensor_copy(rhs_sb.rearrange("p (j e) v -> p e j v", e=2)[:, e],
                                            o[:, 0:256].rearrange("p (j v) -> p j v", j=PAIRS))\
                               .then_inc(drained_of(("rhs", c, e)), 1)
                    if p == 3 and c == 0:
                        o = take(dve, ("state",))
                        for j in range(PAIRS):
                            ins = dve.tensor_scalar(s_in[:, j], o[:, HD * j:HD * j + HD], e_end[:, j:j + 1], None, ALU.mult)
                        ins.then_inc(drained_of(("state",)), 1)
                if t - 1 in S_APPLY:
                    c = S_APPLY.index(t - 1)
                    heads = lambda v: v.rearrange("p (h v) -> p h v", h=HEADS)
                    per_head = lambda v: v.unsqueeze(2).to_broadcast([P, HEADS, HD])
                    if p == 0:
                        copied(dve, ("o", c, 0))
                        copied(dve, ("o", c, 1))
                        link(dve.tensor_reduce(gsum, o_sb, AX_X, ALU.add))
                        link(dve.tensor_scalar(gsum, gsum, -1.0 / HD, None, ALU.mult))
                        dve.tensor_tensor(heads(oc), o_sb, per_head(gsum), ALU.add).then_inc(oc_ready, 1)
                    if p == 1:
                        dve.wait_ge(osq_ready, c + 1)
                        link(dve.tensor_reduce(gvar, heads(osq), AX_X, ALU.add))
                        dve.tensor_scalar(gvar, gvar, 1.0 / HD, GN_EPS, ALU.mult, ALU.add).then_inc(gvar_ready, 1)
                    if p == 2:
                        dve.wait_ge(groot_ready, c + 1)
                        dve.tensor_tensor(heads(oc), heads(oc), per_head(gvar), ALU.mult).then_inc(on_ready, 1)
                if t in S_GN and p == 3:
                    c = S_GN.index(t)
                    ts = slice(P * c, P * c + P)
                    o = take(dve, ("ot", c))
                    for j in range(PAIRS):
                        ins = dve.tensor_scalar(ytmp[:, j], o[:, P * j:P * j + P], col(V_LG + j), col(V_LB + j),
                                                ALU.mult, ALU.add)
                    ins.then_inc(drained_of(("ot", c)), 1)
                    copied(dve, ("ot", c))
                    link(dve.tensor_tensor(ytmp, ytmp, vmix[:, :, ts], ALU.add))
                    copied(dve, ("g", 0))
                    copied(dve, ("g", 1))
                    dve.tensor_tensor(ytmp, ytmp, gg[:, :, ts], ALU.mult).then_inc(yr_pre, 1)
                if t - 1 in S_GN and p == 1:
                    c = S_GN.index(t - 1)
                    ts = slice(P * c, P * c + P)
                    dve.wait_ge(yr_hi_done, c + 1)
                    rest(r_lo[:, :, ts], ytmp, r_hi[:, :, ts]).then_inc(yr_ready, 1)
                if S_HEAD <= t <= S_HEAD + HEADS:
                    h = t - S_HEAD
                    if p == 1 and h < HEADS:
                        o = take(dve, ("score", h))
                        dve.scalar_tensor_tensor(out=prob, in0=cst[:, C_BIAS:C_BIAS + 384], scalar=SLOPES[h],
                                                 in1=o[:, 0:384], op0=ALU.mult, op1=ALU.add)\
                           .then_inc(drained_of(("score", h)), 1)
                        copied(dve, ("score", h))
                        dve.tensor_reduce(nmax[:, 0:1], prob[:, 0:P], AX_X, ALU.max, negate=True).then_inc(neg_ready, 1)
                        dve.tensor_reduce(nmax[:, 1:2], prob[:, P:P + T], AX_X, ALU.max, negate=True).then_inc(neg_ready, 1)
                    if p == 2 and h < HEADS:
                        dve.wait_ge(exps_ready, 2 * h + 2)
                        link(dve.reciprocal(psm, psm))
                        dve.tensor_scalar(prob[:, 0:P], prob[:, 0:P], psm[:, 0:1], None, ALU.mult)
                        dve.tensor_scalar(prob[:, P:P + T], prob[:, P:P + T], psm[:, 1:2], None, ALU.mult)\
                           .then_inc(p_ready, 1)
                    if p == 3 and h >= 1:
                        n = h - 1
                        dve.wait_ge(ya_hi, h)
                        o = take(dve, ("pv", n))
                        rows = slice(HD * (n % 2), HD * (n % 2) + HD)
                        rest(y_lo[rows, n // 2], o[rows, 0:T], y_hi[rows, n // 2]).then_inc(drained_of(("pv", n)), 1)
                if t == S_PY and p in (0, 2):
                    i = p // 2
                    dve.wait_ge(yp_hi, i + 1)
                    o = take(dve, ("pool", i))
                    for gi in range(2):
                        g = 2 * i + gi
                        ins = dve.scalar_tensor_tensor(out=y_lo[:, 4 + g], in0=o[:, T * gi:T * gi + T], scalar=col(V_PS + g),
                                                       in1=y_hi[:, 4 + g].bitcast(F32), op0=ALU.mult, op1=ALU.subtract)
                    ins.then_inc(drained_of(("pool", i)), 1)
                if t == S_FF - 1 and p in (1, 3):
                    for i in (p - 1, p):
                        dve.wait_ge(h2_hi, i + 1)
                        o = take(dve, ("h2", i))
                        for kk in range(2):
                            k = 2 * i + kk
                            ins = dve.scalar_tensor_tensor(out=h_lo[:, k], in0=o[:, T * kk:T * kk + T], scalar=col(V_G2 + k),
                                                           in1=h_hi[:, k].bitcast(F32), op0=ALU.mult, op1=ALU.subtract)
                        ins.then_inc(drained_of(("h2", i)), 1)
                if (t, p) == (S_FF, 3):
                    dve.wait_ge(ss2_ready, 2)
                    link(dve.tensor_scalar(r2, ss2, 1.0 / D, RMS_EPS, ALU.mult, ALU.add))
                    link(dve.reciprocal(r2, r2))

            def finish(t):
                u = UNITS[t]
                if t < S_QK:
                    o = take(dve, ("unit", t))
                    dve.wait_ge(keep_part, 2 * t + 2)
                    for j in range(2):
                        dst, m = mix_dst(t, j), mix_tile(t, j)
                        ins = dve.scalar_tensor_tensor(out=dst[:, 1:T], in0=o[:, T * j:T * j + T - 1], scalar=col(V_MU + m),
                                                       in1=dst[:, 1:T], op0=ALU.mult, op1=ALU.add)
                    ins.then_inc(drained_of(("unit", t)), 1)
                elif u[0] == "branch":
                    n, ch = u[1], u[2]
                    g = 2 * n + ch
                    for i in range(2):
                        copied(dve, ("unit", S_GATE + 2 * g + i))
                        o = take(dve, ("unit", t, i))
                        dve.scalar_tensor_tensor(out=gates[g][:, i], in0=gates[g][:, i], scalar=1.0, in1=o[:],
                                                 op0=ALU.add, op1=ALU.mult)\
                           .then_inc(drained_of(("unit", t, i)), 1)
                    if n == 0:
                        dve.wait_ge(sum_ready, ch + 1)
                        for i in range(2):
                            copied(dve, ("unit", t, i))
                            dve.tensor_tensor(gates[ch][:, i], gates[ch][:, i], gates[2 + ch][:, i], ALU.add).then_inc(m_pre, 1)
                        for i in range(2):
                            m = 2 * ch + i
                            dve.wait_ge(m_hi, m + 1)
                            dve.scalar_tensor_tensor(out=y_lo[:, 2 * m:2 * m + 2], scalar=0.5, op0=ALU.mult, op1=ALU.subtract,
                                                     in0=gates[ch][:, i].rearrange("p (k t) -> p k t", k=2),
                                                     in1=y_hi[:, 2 * m:2 * m + 2].bitcast(F32)).then_inc(m_ready, 1)
                elif u[0] == "out" and u[1] == 1:
                    for tt in range(TT):
                        name = ("out", u[2], tt)
                        o = take(dve, name)
                        xc = xs[:, tt, 512 * u[2]:512 * u[2] + 512]
                        dve.tensor_tensor(xc, xc, o[:], ALU.add).then_inc(drained_of(name), 1)
                elif u[0] == "ff1":
                    i = u[1]
                    copied(dve, ("ff", i))
                    link(dve.tensor_tensor(fsq[i % 2], ffs[i % 2], ffs[i % 2], ALU.mult))
                    dve.wait_ge(f_hi, i + 1)
                    b = 2 * (i % 2)
                    rest(r_lo[:, b:b + 2], fsq[i % 2].rearrange("p (k t) -> p k t", k=2), r_hi[:, b:b + 2])\
                        .then_inc(f_ready, 1)

            for t in range(SLOTS):
                for v in split_places(2 * t):
                    low(v)
                extra(t, 0)
                late = t == S_FF - 1
                for v in split_places(2 * t + 1) if not late else ():
                    low(v)
                extra(t, 1)
                extra(t, 2)
                finish(t)
                extra(t, 3)
                for v in split_places(2 * t + 1) if late else ():
                    low(v)
            for tt in range(TT):
                for c in range(2):
                    if (tt, c) == (1, 1):
                        dve.wait_ge(used, PIECES)
                        o = ps(("mlp", tt, c))
                    else:
                        o = take(dve, ("mlp", tt, c))
                    xc = xs[:, tt, 512 * c:512 * c + 512]
                    dve.scalar_tensor_tensor(out=xc, in0=o[:], scalar=r2[:, tt:tt + 1], in1=xc, op0=ALU.mult, op1=ALU.add)\
                       .then_inc(fin_ready, 1)

        @block.gpsimd
        def _(pool):
            pool.memset(th[64:65], 1.0).then_inc(ones_ready, 1)
            pool.wait_ge(ones_ready, 1)
            pool.memset(minus_half, -0.5).then_inc(ones_ready, 1)
            pool.wait_ge(ones_ready, 2)

            def inverse_root(ap, done):
                shape = list(ap.shape)
                half = minus_half if len(shape) == 2 else minus_half.unsqueeze(2)
                pool.tensor_tensor(ap, ap, half.to_broadcast(shape), ALU.pow).then_inc(done, 1)

            for tt in range(TT):
                pool.wait_ge(ms_ready, tt + 1)
                inverse_root(rs1[:, tt:tt + 1], rs_ready)
            copied(pool, ("kk",))
            inverse_root(kk_tok, kk_inv)

            def add_identity(c, g):
                hs = slice(4 * g, 4 * g + 4)
                for e in range(2):
                    copied(pool, ("prod", c, g, 0, e))
                pool.tensor_tensor(gm[:, hs, 0], gm[:, hs, 0], wide(ident, 4), ALU.subtract).then_inc(nt_ready, 1)
                if g == 1:
                    for i in range(2):
                        for e in range(2):
                            copied(pool, ("prod", c, i, 2, e))
                    pool.tensor_tensor(x_c, x_c, wide(cst[:, C_IDC:C_IDC + HD], HEADS), ALU.add).then_inc(x1_ready, 1)

            def inverse_norm(n):
                copied(pool, ("ss", n))
                inverse_root(qk_tok[n % 2], qk_inv)

            add_identity(0, 0)
            inverse_norm(0)
            add_identity(0, 1)
            for n in (1, 2, 3):
                inverse_norm(n)
            copied(pool, ("kt",))
            pool.memset(pu[:, :, 0:PAD], 0.0).then_inc(pad_ready, 1)
            pool.memset(pt1[:, 0:PAD], 0.0).then_inc(pad_ready, 1)
            pool.memset(pt2[:, 0:PAD], 0.0).then_inc(pad_ready, 1)
            pool.wait_ge(pad_ready, 3)
            steps = 0
            for g, w in enumerate(WINDOWS):
                copied(pool, ("unit", S_POOL + g // 2))
                src, s = pu[:, g], 1
                while s < w:
                    dst = (pt1, pt2)[s.bit_length() % 2]
                    pool.tensor_tensor(dst[:, PAD:], src[:, PAD:], src[:, PAD - s:PAD + T - s], ALU.add).then_inc(pool_step, 1)
                    steps += 1
                    pool.wait_ge(pool_step, steps)
                    src, s = dst, 2 * s
                pool.tensor_tensor(pd[:, 0:PAD], src[:, PAD:2 * PAD], cst[:, C_INV + PAD * g:C_INV + PAD * g + PAD], ALU.mult)\
                    .then_inc(pool_step, 1)
                pool.tensor_scalar(pd[:, PAD:T], src[:, 2 * PAD:], 1.0 / w, None, ALU.mult).then_inc(pool_step, 1)
                steps += 2
                pool.wait_ge(pool_step, steps)
                pool.tensor_tensor(pu[:, g, PAD:], pd, pu[:, g, PAD:], ALU.subtract).then_inc(pd_ready, 1)
                pool.wait_ge(pd_ready, g + 1)

            def group_norm_root(c):
                pool.wait_ge(gvar_ready, c + 1)
                inverse_root(gvar, groot_ready)

            group_norm_root(0)
            add_identity(1, 0)
            add_identity(1, 1)
            group_norm_root(1)
            for ch in range(2):
                for n in (1, 2):
                    for tt in range(TT):
                        copied(pool, ("unit", S_BR + 2 * (n - 1) + ch, tt))
                pool.tensor_tensor(gates[2 + ch], gates[2 + ch], gates[4 + ch], ALU.add).then_inc(sum_ready, 1)


def shape_constants():
    c = np.zeros((P, C_ALL), np.float32)
    t, s = np.arange(P)[:, None], np.arange(P)[None, :]
    c[:, C_ID:C_ID + P] = t == s
    c[:, C_BLK:C_BLK + P] = t // HD == s // HD
    j = np.arange(129)[None, :]
    c[:, C_CUM:C_CUM + 129] = -np.exp(-0.5) * ((t < j).astype(np.float64) - (t < 64))
    c[:, C_BIAS:C_BIAS + P] = np.where(s <= t, s - t, -1e30)
    s2 = np.arange(T)[None, :]
    c[:, C_BIAS + P:C_BIAS + P + T] = np.where(s2 <= t + P, s2 - t - P, -1e30)
    c[:, C_SDI:C_SDI + P] = (t < s) & (t // HD == s // HD)
    c[:, C_SDI + P:C_SDI + 2 * P] = t <= s
    c[:, C_SI:C_SI + P] = t < s
    c[:, C_SI + P:C_SI + 2 * P] = t <= s
    r = np.arange(HD)[None, :]
    q = t % HD
    for l in range(LEVELS):
        b = 2 << l
        c[:, C_LEV + HD * l:C_LEV + HD * l + HD] = ((q // b % 2 == 1) & (r // b == q // b - 1)).astype(np.float32) - (q == r)
    c[:, C_M1:C_M1 + HD] = (q % 2 == 1) & (r == q - 1)
    c[:, C_IDC:C_IDC + HD] = q == r
    c[:, C_M1T:C_M1T + P] = ((s % 2 == 1) & (t == s - 1)).astype(np.float32) - (t == s)
    for g, w in enumerate(WINDOWS):
        c[:, C_INV + PAD * g:C_INV + PAD * g + PAD] = 1.0 / np.minimum(np.arange(PAD) + 1, w)
    return c


def channel_columns(shift_mu, a0, k_k, k_a, r_k, lnx_g, lnx_b, pool_scale, norm1_g, norm2_g, qn_g, kn_g):
    rows = [a.reshape(-1, P) for a in (shift_mu, a0, k_k, k_a, r_k, lnx_g, lnx_b, pool_scale, norm1_g, norm2_g)]
    rows += [np.concatenate([a, a], axis=1) for a in (qn_g, kn_g)]
    return np.ascontiguousarray(np.concatenate(rows, axis=0).T)


_WEIGHTS = ["x", "w_in", "w_up", "w0", "a_up", "g_up", "pool_w", "w_branch", "w_out", "w_ff1", "w_ff2"]


def kernel(**inputs):
    import concourse.bacc as _bacc
    from concourse.bass_utils import run_bass_kernel_spmd as _run

    a = {k: np.ascontiguousarray(v) for k, v in inputs.items()}
    arrays = {f"in_{k}": a[k] for k in _WEIGHTS}
    arrays["in_vecs"] = channel_columns(*(a[k] for k in (
        "shift_mu", "a0", "k_k", "k_a", "r_k", "lnx_g", "lnx_b", "pool_scale", "norm1_g", "norm2_g", "qn_g", "kn_g")))
    arrays["in_consts"] = shape_constants()
    nc = _bacc.Bacc("TRN2", target_bir_lowering=False, num_devices=1)
    args = [nc.dram_tensor(n, v.shape, mybir.dt.from_np(v.dtype), kind="ExternalInput").ap() for n, v in arrays.items()]
    args.append(nc.dram_tensor("out_0", (1, T, D), F32, kind="ExternalOutput").ap())
    build_layer(nc, *args)
    r = _run(nc, [arrays], core_ids=[0])
    return r.results[0]["out_0"]
```
